# Optimizing a Trainium2 kernel written in Bass

```python
import jax, jax.numpy as jnp
from jax import lax
import numpy as np
import math

D_MODEL = 1024
BATCH = 1
SEQ = 256
DEPTH = 1

GRID_W = 64
Q_BLOCK = 128
ROPE_THETA = 10000.0
EPS = 1e-6
H_A = 8
QK_NOPE = 64
QK_ROPE = 32
V_DIM_A = 64
Q_LORA = 256
KV_LORA = 128
H_B = 8
KV_B = 2
HD_B = 64
D_FF = 4 * D_MODEL
PLE_DIM = 256
IN_SPLITS = [Q_LORA, KV_LORA + QK_ROPE, H_B * HD_B, KV_B * HD_B, KV_B * HD_B, D_MODEL, D_MODEL]
D_IN = sum(IN_SPLITS)


def rmsnorm(x, g):
    xf = x.astype(jnp.float32)
    y = xf * lax.rsqrt(jnp.mean(xf * xf, axis=-1, keepdims=True) + EPS)
    return (y * g.astype(jnp.float32)).astype(x.dtype)

def rope_angles(pos, dim):
    inv = ROPE_THETA ** (-jnp.arange(0, dim, 2, dtype=jnp.float32) / dim)
    return pos.astype(jnp.float32)[:, None] * inv[None, :]

def apply_rope(x, ang):
    cos = jnp.cos(ang)[None, :, None, :].astype(x.dtype)
    sin = jnp.sin(ang)[None, :, None, :].astype(x.dtype)
    x1, x2 = jnp.split(x, 2, axis=-1)
    return jnp.concatenate([x1 * cos - x2 * sin, x1 * sin + x2 * cos], axis=-1)

def blocked_attention(q, k, v):
    B, S, Hk, G, dk = q.shape
    nb = S // Q_BLOCK
    qb = q.reshape(B, nb, Q_BLOCK, Hk, G, dk).transpose(1, 0, 2, 3, 4, 5)

    def one_block(qblk):
        s = jnp.einsum("bqhgd,bkhd->bhgqk", qblk, k).astype(jnp.float32)
        pr = jax.nn.softmax(s, axis=-1).astype(v.dtype)
        return jnp.einsum("bhgqk,bkhd->bqhgd", pr, v)

    o = lax.map(one_block, qb)
    return o.transpose(1, 0, 2, 3, 4, 5).reshape(B, S, Hk * G, v.shape[-1])

def first_inputs(seed: int = 0) -> dict:
    key = jax.random.key(seed)
    ks = jax.random.split(key, 24)
    f32 = jnp.float32

    def w(k, shape, fan_in):
        return jax.random.normal(k, shape, f32) * (fan_in ** -0.5)

    def gain(k, shape):
        return 1.0 + 0.05 * jax.random.normal(k, shape, f32)

    L = DEPTH
    return {
        "x": jax.random.normal(ks[0], (BATCH, SEQ, D_MODEL), f32),
        "p": jax.random.normal(ks[1], (DEPTH, BATCH, SEQ, PLE_DIM), f32),
        "g_mix": gain(ks[2], (L, D_MODEL)),
        "w_in": w(ks[3], (L, D_MODEL, D_IN), D_MODEL),
        "g_qa": gain(ks[4], (L, Q_LORA)),
        "w_qb": w(ks[5], (L, Q_LORA, H_A * (QK_NOPE + QK_ROPE)), Q_LORA),
        "g_kva": gain(ks[6], (L, KV_LORA)),
        "w_kvb": w(ks[7], (L, KV_LORA, H_A * (QK_NOPE + V_DIM_A)), KV_LORA),
        "g_qn": gain(ks[8], (L, HD_B)),
        "g_kn": gain(ks[9], (L, HD_B)),
        "w_oa": w(ks[10], (L, H_A * V_DIM_A, D_MODEL), H_A * V_DIM_A),
        "w_ob": w(ks[11], (L, H_B * HD_B, D_MODEL), H_B * HD_B),
        "w_o": w(ks[12], (L, D_MODEL, D_MODEL), D_MODEL),
        "g_mlp": gain(ks[13], (L, D_MODEL)),
        "w_up": w(ks[14], (L, D_MODEL, D_FF), D_MODEL),
        "w_down": w(ks[15], (L, D_FF, D_MODEL), D_FF),
        "g_ple": gain(ks[16], (L, D_MODEL)),
        "w_ple_gate": w(ks[17], (L, D_MODEL, D_MODEL), D_MODEL),
        "w_ple": w(ks[18], (L, PLE_DIM, D_MODEL), PLE_DIM),
        "g_final": gain(ks[19], (D_MODEL,)),
    }

def first_block(x, p, g_mix, w_in, g_qa, w_qb, g_kva, w_kvb, g_qn, g_kn, w_oa, w_ob, w_o,
              g_mlp, w_up, w_down, g_ple, w_ple_gate, w_ple, g_final):
    B, S, D = x.shape
    ROWS = S // GRID_W
    t = jnp.arange(S)
    row = jnp.broadcast_to(jnp.arange(ROWS)[:, None], (ROWS, GRID_W)).reshape(-1)
    col = jnp.broadcast_to(jnp.arange(GRID_W)[None, :], (ROWS, GRID_W)).reshape(-1)
    ang_1d = rope_angles(t, QK_ROPE)
    ang_row = rope_angles(row, HD_B // 2)
    ang_col = rope_angles(col, HD_B // 2)
    split_idx = list(np.cumsum(IN_SPLITS)[:-1])
    scale_a = (QK_NOPE + QK_ROPE) ** -0.5
    scale_b = HD_B ** -0.5

    for i in range(DEPTH):
        h = rmsnorm(x, g_mix[i])
        z = jnp.einsum("bsd,de->bse", h, w_in[i])
        q_lat, kv_lat, qb, kb, vb, gate_a, gate_b = jnp.split(z, split_idx, axis=-1)

        cq = rmsnorm(q_lat, g_qa[i])
        qa = jnp.einsum("bsr,re->bse", cq, w_qb[i]).reshape(B, S, H_A, QK_NOPE + QK_ROPE)
        qa_nope, qa_rope = jnp.split(qa, [QK_NOPE], axis=-1)
        qa_rope = apply_rope(qa_rope, ang_1d)
        c_kv, k_pe = jnp.split(kv_lat, [KV_LORA], axis=-1)
        c_kv = rmsnorm(c_kv, g_kva[i])
        k_pe = apply_rope(k_pe[:, :, None, :], ang_1d)
        kva = jnp.einsum("bsr,re->bse", c_kv, w_kvb[i]).reshape(B, S, H_A, QK_NOPE + V_DIM_A)
        ka_nope, va = jnp.split(kva, [QK_NOPE], axis=-1)
        qa_full = (jnp.concatenate([qa_nope, qa_rope], axis=-1) * scale_a)[:, :, :, None, :]
        ka_full = jnp.concatenate([ka_nope, jnp.broadcast_to(k_pe, (B, S, H_A, QK_ROPE))], axis=-1)
        oa = blocked_attention(qa_full, ka_full, va).reshape(B, S, H_A * V_DIM_A)
        ya = jnp.einsum("bse,ed->bsd", oa, w_oa[i])

        qb = rmsnorm(qb.reshape(B, S, H_B, HD_B), g_qn[i])
        kb = rmsnorm(kb.reshape(B, S, KV_B, HD_B), g_kn[i])
        vb = vb.reshape(B, S, KV_B, HD_B)
        qr, qc = jnp.split(qb, 2, axis=-1)
        qb = jnp.concatenate([apply_rope(qr, ang_row), apply_rope(qc, ang_col)], axis=-1)
        kr, kc = jnp.split(kb, 2, axis=-1)
        kb = jnp.concatenate([apply_rope(kr, ang_row), apply_rope(kc, ang_col)], axis=-1)
        qb = (qb * scale_b).reshape(B, S, KV_B, H_B // KV_B, HD_B)
        ob = blocked_attention(qb, kb, vb).reshape(B, S, H_B * HD_B)
        yb = jnp.einsum("bse,ed->bsd", ob, w_ob[i])

        merged = jax.nn.sigmoid(gate_a) * ya + jax.nn.sigmoid(gate_b) * yb
        x = x + jnp.einsum("bsd,de->bse", merged, w_o[i])

        h2 = rmsnorm(x, g_mlp[i])
        u = jax.nn.relu(jnp.einsum("bsd,df->bsf", h2, w_up[i]))
        x = x + jnp.einsum("bsf,fd->bsd", u * u, w_down[i])

        h3 = rmsnorm(x, g_ple[i])
        gate = jax.nn.sigmoid(jnp.einsum("bsd,de->bse", h3, w_ple_gate[i]))
        x = x + gate * jnp.einsum("bsk,kd->bsd", p[i], w_ple[i])

    return rmsnorm(x, g_final)


DEPTH_2 = 2

BLOCK_Q = 128
D_FF_2 = 2816
GLA_HEADS = 4
GLA_DK = 64
GLA_DV = 128
GLA_GATE_RANK = 16
GLA_GATE_NORMALIZER = 16.0
GLA_CHUNK = 64
FOX_HEADS = 8
FOX_DH = 64
DSA_HEADS = 16
DSA_DH = 64
DSA_LATENT = 256
IDX_HEADS = 8
IDX_DIM = 64
TOPK_MAX = 256
T5_BUCKETS = 32
T5_MAX_DIST = 128

N_EVEN = (DEPTH_2 + 1) // 2
N_ODD = DEPTH_2 // 2

EVEN_SIZES = (GLA_HEADS * GLA_DK, GLA_HEADS * GLA_DK, GLA_HEADS * GLA_DV, GLA_HEADS * GLA_DV, GLA_GATE_RANK,
              FOX_HEADS * FOX_DH, FOX_HEADS * FOX_DH, FOX_HEADS * FOX_DH, FOX_HEADS)
ODD_SIZES = (DSA_HEADS * DSA_DH, DSA_LATENT, IDX_HEADS * IDX_DIM, IDX_DIM, IDX_HEADS)
D_IN_EVEN = sum(EVEN_SIZES)
D_IN_ODD = sum(ODD_SIZES)
EVEN_SPLITS = tuple(int(v) for v in np.cumsum(EVEN_SIZES)[:-1])
ODD_SPLITS = tuple(int(v) for v in np.cumsum(ODD_SIZES)[:-1])
D_MIX_EVEN = GLA_HEADS * GLA_DV + FOX_HEADS * FOX_DH
D_MIX_ODD = DSA_HEADS * DSA_DH


def rmsnorm_2(x, g):
    xf = x.astype(jnp.float32)
    y = xf * lax.rsqrt(jnp.mean(xf * xf, axis=-1, keepdims=True) + EPS)
    return (y * g.astype(jnp.float32)).astype(x.dtype)

def swiglu(h, w_in, w_out):
    a, b = jnp.split(h @ w_in, 2, axis=-1)
    return (jax.nn.silu(a) * b) @ w_out

def to_blocks(t, nb):
    return t.reshape((t.shape[0], nb, BLOCK_Q) + t.shape[2:]).swapaxes(0, 1)

def gla_chunked(q, k, v, gk):
    B, S, H, dk = q.shape
    dv = v.shape[-1]
    C = GLA_CHUNK
    N = S // C

    def chunks(t):
        return t.astype(jnp.float32).reshape(B, N, C, H, t.shape[-1]).transpose(1, 0, 3, 2, 4)

    qc = chunks(q) * (dk ** -0.5)
    kc, vc, gc = chunks(k), chunks(v), chunks(gk)
    G = jnp.cumsum(gc, axis=-2)
    G_last = G[..., -1, :]
    q_dec = qc * jnp.exp(G)
    k_dec = kc * jnp.exp(-G)
    k_to_end = kc * jnp.exp(G_last[..., None, :] - G)
    causal = jnp.tril(jnp.ones((C, C), dtype=bool))
    A = jnp.where(causal, jnp.einsum('nbhid,nbhjd->nbhij', q_dec, k_dec), 0.0)
    o_intra = jnp.einsum('nbhij,nbhjv->nbhiv', A, vc)

    def step(state, inp):
        qd, ke, vv, gl = inp
        o = jnp.einsum('bhid,bhdv->bhiv', qd, state)
        state = jnp.exp(gl)[..., None] * state + jnp.einsum('bhjd,bhjv->bhdv', ke, vv)
        return state, o

    state0 = jnp.zeros((B, H, dk, dv), jnp.float32)
    _, o_inter = lax.scan(step, state0, (q_dec, k_to_end, vc, G_last))
    o = o_intra + o_inter
    return o.transpose(1, 0, 3, 2, 4).reshape(B, S, H, dv)

def fox_attention(q, k, v, log_f):
    B, S, H, dh = q.shape
    nb = S // BLOCK_Q
    F = jnp.cumsum(log_f, axis=1)
    F_keys = F.transpose(0, 2, 1)
    key_pos = jnp.arange(S)

    def one_block(args):
        i, qb, Fb = args
        q_pos = i * BLOCK_Q + jnp.arange(BLOCK_Q)
        s = jnp.einsum('bqhd,bkhd->bhqk', qb, k).astype(jnp.float32) * (dh ** -0.5)
        s = s + (Fb.transpose(0, 2, 1)[..., :, None] - F_keys[..., None, :])
        s = jnp.where(key_pos[None, :] <= q_pos[:, None], s, -jnp.inf)
        p = jax.nn.softmax(s, axis=-1)
        return jnp.einsum('bhqk,bkhd->bqhd', p.astype(v.dtype), v)

    o = lax.map(one_block, (jnp.arange(nb), to_blocks(q, nb), to_blocks(F, nb)))
    return o.swapaxes(0, 1).reshape(B, S, H, dh)

def t5_bucket(dist):
    max_exact = T5_BUCKETS // 2
    d = jnp.maximum(dist, 1).astype(jnp.float32)
    large = max_exact + (jnp.log(d / max_exact) / math.log(T5_MAX_DIST / max_exact)
                         * (T5_BUCKETS - max_exact)).astype(jnp.int32)
    large = jnp.minimum(large, T5_BUCKETS - 1)
    return jnp.where(dist < max_exact, dist, large)

def dsa_attention(q_lat, c, q_idx, k_idx, w_idx, t5_table):
    B, S, H, DL = q_lat.shape
    k_top = min(TOPK_MAX, S // 4)
    nb = S // BLOCK_Q
    key_pos = jnp.arange(S)
    w_scaled = w_idx.astype(jnp.float32) * (IDX_HEADS ** -0.5)
    gather = jax.vmap(lambda cb, ib: cb[ib])

    def one_block(args):
        i, qb, qib, wb = args
        q_pos = i * BLOCK_Q + jnp.arange(BLOCK_Q)
        logit_idx = jnp.einsum('bqhd,bkd->bqhk', qib, k_idx).astype(jnp.float32) * (IDX_DIM ** -0.5)
        score = jnp.einsum('bqh,bqhk->bqk', wb, jax.nn.relu(logit_idx))
        score = jnp.where((key_pos[None, :] <= q_pos[:, None])[None], score, -jnp.inf)
        _, idx = lax.top_k(score, k_top)
        c_sel = gather(c, idx)
        dist = q_pos[None, :, None] - idx
        bias = t5_table[t5_bucket(jnp.maximum(dist, 0))]
        s = jnp.einsum('bqhl,bqkl->bqhk', qb, c_sel).astype(jnp.float32) * (DSA_DH ** -0.5)
        s = s + bias.transpose(0, 1, 3, 2).astype(jnp.float32)
        s = jnp.where((dist >= 0)[:, :, None, :], s, -jnp.inf)
        p = jax.nn.softmax(s, axis=-1)
        return jnp.einsum('bqhk,bqkl->bqhl', p.astype(c.dtype), c_sel)

    o = lax.map(one_block, (jnp.arange(nb), to_blocks(q_lat, nb), to_blocks(q_idx, nb), to_blocks(w_scaled, nb)))
    return o.swapaxes(0, 1).reshape(B, S, H, DL)

def even_mixer(h, w_in, gla_w_gate, gla_b_gate, gla_norm_g, fox_b_f, w_out):
    B, S, _ = h.shape
    q_g, k_g, v_g, g_out, gk_low, q_f, k_f, v_f, f_logit = jnp.split(h @ w_in, EVEN_SPLITS, axis=-1)
    gk = jax.nn.log_sigmoid((gk_low @ gla_w_gate + gla_b_gate).astype(jnp.float32)) / GLA_GATE_NORMALIZER
    o_gla = gla_chunked(q_g.reshape(B, S, GLA_HEADS, GLA_DK), k_g.reshape(B, S, GLA_HEADS, GLA_DK),
                        v_g.reshape(B, S, GLA_HEADS, GLA_DV), gk.reshape(B, S, GLA_HEADS, GLA_DK)).astype(h.dtype)
    o_gla = rmsnorm_2(o_gla, gla_norm_g) * jax.nn.silu(g_out.reshape(B, S, GLA_HEADS, GLA_DV))
    log_f = jax.nn.log_sigmoid((f_logit + fox_b_f).astype(jnp.float32))
    o_fox = fox_attention(q_f.reshape(B, S, FOX_HEADS, FOX_DH), k_f.reshape(B, S, FOX_HEADS, FOX_DH),
                          v_f.reshape(B, S, FOX_HEADS, FOX_DH), log_f)
    o = jnp.concatenate([o_gla.reshape(B, S, -1), o_fox.reshape(B, S, -1)], axis=-1)
    return o @ w_out

def odd_mixer(h, w_in, kv_norm_g, w_uk, w_uv, w_out, t5_table):
    B, S, _ = h.shape
    q, ckv, q_idx, k_idx, w_idx = jnp.split(h @ w_in, ODD_SPLITS, axis=-1)
    c = rmsnorm_2(ckv, kv_norm_g)
    q_lat = jnp.einsum('bshd,hdl->bshl', q.reshape(B, S, DSA_HEADS, DSA_DH), w_uk)
    o_lat = dsa_attention(q_lat, c, q_idx.reshape(B, S, IDX_HEADS, IDX_DIM), k_idx, w_idx, t5_table)
    o = jnp.einsum('bshl,hld->bshd', o_lat, w_uv).reshape(B, S, D_MIX_ODD)
    return o @ w_out

def second_inputs(seed: int = 0) -> dict:
    key = jax.random.key(seed)
    ks = jax.random.split(key, 17)
    f32 = jnp.float32

    def nrm(k, shape, fan_in):
        return jax.random.normal(k, shape, f32) * (fan_in ** -0.5)

    def gain(k, shape):
        return 1.0 + 0.02 * jax.random.normal(k, shape, f32)

    return {
        "x": jax.random.normal(ks[0], (BATCH, SEQ, D_MODEL), f32),
        "norm_g": gain(ks[1], (DEPTH_2, 3, D_MODEL)),
        "ffn_w_in": nrm(ks[2], (DEPTH_2, 2, D_MODEL, 2 * D_FF_2), D_MODEL),
        "ffn_w_out": nrm(ks[3], (DEPTH_2, 2, D_FF_2, D_MODEL), D_FF_2),
        "even_w_in": nrm(ks[4], (N_EVEN, D_MODEL, D_IN_EVEN), D_MODEL),
        "gla_w_gate": nrm(ks[5], (N_EVEN, GLA_GATE_RANK, GLA_HEADS * GLA_DK), GLA_GATE_RANK),
        "gla_b_gate": 0.02 * jax.random.normal(ks[6], (N_EVEN, GLA_HEADS * GLA_DK), f32),
        "gla_norm_g": gain(ks[7], (N_EVEN, GLA_DV)),
        "fox_b_f": 2.0 + 0.5 * jax.random.normal(ks[8], (N_EVEN, FOX_HEADS), f32),
        "even_w_out": nrm(ks[9], (N_EVEN, D_MIX_EVEN, D_MODEL), D_MIX_EVEN),
        "odd_w_in": nrm(ks[10], (N_ODD, D_MODEL, D_IN_ODD), D_MODEL),
        "mla_kv_norm_g": gain(ks[11], (N_ODD, DSA_LATENT)),
        "mla_w_uk": nrm(ks[12], (N_ODD, DSA_HEADS, DSA_DH, DSA_LATENT), DSA_LATENT),
        "mla_w_uv": nrm(ks[13], (N_ODD, DSA_HEADS, DSA_LATENT, DSA_DH), DSA_LATENT),
        "odd_w_out": nrm(ks[14], (N_ODD, D_MIX_ODD, D_MODEL), D_MIX_ODD),
        "t5_table": 0.5 * jax.random.normal(ks[15], (T5_BUCKETS, DSA_HEADS), f32),
        "final_norm_g": gain(ks[16], (D_MODEL,)),
    }

def second_block(x, norm_g, ffn_w_in, ffn_w_out, even_w_in, gla_w_gate, gla_b_gate, gla_norm_g, fox_b_f,
              even_w_out, odd_w_in, mla_kv_norm_g, mla_w_uk, mla_w_uv, odd_w_out, t5_table, final_norm_g):
    for layer in range(DEPTH_2):
        g = norm_g[layer]
        x = x + 0.5 * swiglu(rmsnorm_2(x, g[0]), ffn_w_in[layer, 0], ffn_w_out[layer, 0])
        h = rmsnorm_2(x, g[1])
        j = layer // 2
        if layer % 2 == 0:
            x = x + even_mixer(h, even_w_in[j], gla_w_gate[j], gla_b_gate[j], gla_norm_g[j], fox_b_f[j], even_w_out[j])
        else:
            x = x + odd_mixer(h, odd_w_in[j], mla_kv_norm_g[j], mla_w_uk[j], mla_w_uv[j], odd_w_out[j], t5_table)
        x = x + 0.5 * swiglu(rmsnorm_2(x, g[2]), ffn_w_in[layer, 1], ffn_w_out[layer, 1])
    return rmsnorm_2(x, final_norm_g)


def setup_inputs(seed=0):
    out = dict(first_inputs(seed))
    for name, value in second_inputs(seed + 1).items():
        if name != "x":
            out[name + "_2"] = value
    return out


def reference(
    x, p, g_mix, w_in, g_qa, w_qb, g_kva, w_kvb, g_qn, g_kn, w_oa, w_ob, w_o, g_mlp, w_up,
    w_down, g_ple, w_ple_gate, w_ple, g_final, norm_g_2, ffn_w_in_2, ffn_w_out_2, even_w_in_2,
    gla_w_gate_2, gla_b_gate_2, gla_norm_g_2, fox_b_f_2, even_w_out_2, odd_w_in_2,
    mla_kv_norm_g_2, mla_w_uk_2, mla_w_uv_2, odd_w_out_2, t5_table_2, final_norm_g_2,
):
    x = first_block(
        x, p, g_mix, w_in, g_qa, w_qb, g_kva, w_kvb, g_qn, g_kn, w_oa, w_ob, w_o, g_mlp, w_up,
        w_down, g_ple, w_ple_gate, w_ple, g_final,
    )
    return second_block(
        x, norm_g_2, ffn_w_in_2, ffn_w_out_2, even_w_in_2, gla_w_gate_2, gla_b_gate_2,
        gla_norm_g_2, fox_b_f_2, even_w_out_2, odd_w_in_2, mla_kv_norm_g_2, mla_w_uk_2,
        mla_w_uv_2, odd_w_out_2, t5_table_2, final_norm_g_2,
    )


_drawn_inputs = setup_inputs


def setup_inputs(seed=0):
    import zlib

    import numpy as np

    out = dict(_drawn_inputs(seed))
    spreads = {}
    factors = {'g_mix': 3.051,
     'g_qa': 4.685,
     'g_kva': 3.415,
     'g_qn': 5.531,
     'g_kn': 4.638,
     'g_ple': 3.424,
     'gla_b_gate_2': 4.844,
     'gla_norm_g_2': 3.801,
     'mla_kv_norm_g_2': 7.814,
     'final_norm_g_2': 2.722}
    for name, (base, spread) in spreads.items():
        noise = np.random.default_rng([zlib.crc32(name.encode()), seed]).standard_normal(out[name].shape)
        drawn = base * np.exp(spread * noise) if base else spread * noise
        out[name] = __import__('jax').numpy.asarray(drawn.astype(out[name].dtype))
    for name, factor in factors.items():
        out[name] = (out[name] * factor).astype(out[name].dtype)
    return out
```

```python
from contextlib import ExitStack

import concourse.bass as bass
from concourse import mybir
import numpy as np

F = mybir.dt.float32
R = mybir.dt.float32r
ACT = mybir.ActivationFunctionType
ALU = mybir.AluOpType
AX = mybir.AxisListType

S = 256
D = 1024
CW = 2048
NRAW = 3
NHL = 4
EPS = 1e-6
NEG = -1e30
GONE = -3e38
H2 = 2816



def plan():
    out = []

    def cols(tag, w, k, c0, n, kts=None):
        out.append((tag, [(w, 128 * t, c0, n) for t in (kts or range(k))]))

    def wide(tag, w, c0):
        for part in range(2):
            cols(f"{tag}.{part}", w, 8, c0, 512, range(4 * part, 4 * part + 4))

    wide("z0", "w_in", 0)
    wide("z1", "w_in", 512)
    cols("z2", "w_in", 8, 1024, 160)
    cols("wqb", "w_qb", 2, 0, 768)
    cols("wkvb", "w_kvb", 1, 0, 1024)
    for g in range(8):
        cols(f"gate{g}", "w_in", 8, 1184 + 256 * g, 256)
    for c in range(2):
        cols(f"oa{c}", "w_oa", 4, 512 * c, 512)
        cols(f"ob{c}", "w_ob", 4, 512 * c, 512)
    wide("o0", "w_o", 0)
    wide("o1", "w_o", 512)
    for g in range(17):
        if g < 16:
            cols(f"up{g}", "w_up", 8, 256 * g, 256)
        if g >= 1:
            cols(f"dn{g - 1}", "w_down", 0, 0, 1024, (2 * g - 2, 2 * g - 1))
    cols("ple", "w_ple", 2, 0, 1024)
    wide("pg0", "w_ple_gate", 0)
    wide("pg1", "w_ple_gate", 512)

    def ffn(layer, half):
        a, b = f"ffn_in{layer}{half}", f"ffn_out{layer}{half}"
        for g in range(12):
            if g < 11:
                cols(f"fa{layer}{half}.{g}", a, 8, 256 * g, 256)
                cols(f"fb{layer}{half}.{g}", a, 8, H2 + 256 * g, 256)
            if g >= 1:
                cols(f"fd{layer}{half}.{g - 1}", b, 0, 0, 1024, (2 * g - 2, 2 * g - 1))

    ffn(0, 0)
    out.append(("small", [("even_in", 128 * t, c, n) for t in range(8) for c, n in ((1536, 16), (3088, 8))]))
    wide("vg", "even_in", 512)
    for g in range(2):
        cols(f"go{g}", "even_in", 8, 1024 + 256 * g, 256)
    cols("qg", "even_in", 8, 0, 256)
    cols("kg", "even_in", 8, 256, 256)
    for n, c0 in (("qf", 1552), ("kf", 2064)):
        for g in range(2):
            cols(f"{n}{g}", "even_in", 8, c0 + 256 * g, 256)
    wide("vf", "even_in", 2576)
    wide("eo0", "even_out", 0)
    wide("eo1", "even_out", 512)
    ffn(0, 1)
    ffn(1, 0)
    cols("ckv", "odd_in", 8, 1024, 256)
    cols("kwi", "odd_in", 8, 1792, 72)
    for g in range(2):
        cols(f"qi{g}", "odd_in", 8, 1280 + 256 * g, 256)
    for g in range(4):
        cols(f"q{g}", "odd_in", 8, 256 * g, 256)
    cols("uk", "w_ukT", 2, 0, 1024)
    cols("uv", "w_uv", 2, 0, 1024)
    wide("oo0", "odd_out", 0)
    wide("oo1", "odd_out", 512)
    ffn(1, 1)
    return out



CONST = dict(ident=(0, 128), tri=(128, 128), ones=(256, 128), tri64=(384, 128), m64=(512, 128), cm=(640, 256),
             cosA=(896, 64), sinA=(960, 64), cosB=(1024, 128), sinB=(1152, 128), hot=(1280, 512), sel=(1792, 1024),
             mhalf=(2816, 16))
NCONST = 2832
GAIN = dict(g_mix=(0, 8), g_qa=(8, 2), g_kva=(10, 1), g_mlp=(11, 8), g_ple=(19, 8), n00=(27, 8), n01=(35, 8),
            n02=(43, 8), n10=(51, 8), n11=(59, 8), n12=(67, 8), g_gla=(75, 1), g_ckv=(76, 2))
NGAIN = 78


def constants():
    c = np.zeros((128, NCONST), np.float32)

    def put(name, a):
        o, n = CONST[name]
        a = np.asarray(a, np.float32)
        c[:a.shape[0], o:o + n] = a.reshape(a.shape[0], n)

    p = np.arange(128)
    le = p[:, None] <= p[None, :]
    same = (p[:, None] // 64) == (p[None, :] // 64)
    put("ident", np.eye(128))
    put("tri", le)
    put("ones", np.ones((128, 128)))
    put("tri64", (le & same) / 16.0)
    put("m64", le & same)
    put("cm", np.concatenate([np.zeros((128, 128)), np.where(p[None, :] <= p[:, None], 0.0, NEG)], 1))
    inv = np.float32(10000.0) ** (-np.arange(0, 32, 2, dtype=np.float32) / np.float32(32))

    def angles(pos):
        a = (pos.astype(np.float32)[:, None] * inv[None, :]).astype(np.float32).astype(np.float64)
        co, si = np.cos(a), np.sin(a)
        return np.concatenate([co, co], 1), np.concatenate([-si, si], 1)

    t = np.arange(S)
    ca, sa = angles(t)
    cr, sr = angles(t // 64)
    cc, sc = angles(t % 64)

    def tok(a):
        return a.reshape(2, 128, -1).transpose(1, 0, 2)

    put("cosA", tok(ca))
    put("sinA", tok(sa))
    put("cosB", tok(np.concatenate([cr, cc], 1)))
    put("sinB", tok(np.concatenate([sr, sc], 1)))
    dist = np.maximum(np.arange(512) - 255, 0)
    d = np.maximum(dist, 1).astype(np.float32)
    large = 16 + (np.log(d / np.float32(16)).astype(np.float32) / np.float32(np.log(8.0)) * np.float32(16)).astype(np.int32)
    bucket = np.where(dist < 16, dist, np.minimum(large, 31))
    put("hot", np.arange(32)[:, None] == bucket[None, :])
    sel = np.zeros((8, 8, 128))
    sel[np.arange(8), np.arange(8)] = 1.0
    put("sel", sel)
    put("mhalf", np.full((128, 16), -0.5))
    return c


class Lane:

    def __init__(self, sem):
        self.sem, self.n, self.q, self.seen = sem, 0, [], {}

    def add(self, fn, after, mark=True):
        waits = []
        todo = list(after)
        while todo:
            w = todo.pop(0)
            if isinstance(w, list):
                todo += w
            elif w is not None and self.seen.get(w[0].name, 0) < w[1]:
                self.seen[w[0].name] = w[1]
                waits.append(w)
        self.q.append((waits, fn, self.sem if mark else None, 1))
        if mark:
            self.n += 1
            return (self.sem, self.n)
        return None

    def dma(self, out, in_, sem, value, after):
        self.add(lambda e: e.dma_start(out, in_), after, mark=False)
        waits, fn, _, _ = self.q.pop()
        self.q.append((waits, fn, sem, 16))
        return (sem, value)

    def play(self, eng):
        for waits, fn, sem, by in self.q:
            for s, v in waits:
                eng.wait_ge(s, v)
            ins = fn(eng)
            if sem is not None:
                ins.then_inc(sem, by)


def program(nc, W, XIN, PT_IN, CST, GNS, GQK, GFIN, GFIN2, GLAG, FOXB, T5, OUT):
    P = plan()
    with ExitStack() as ctx:
        def sb(name, shape, dt=F):
            return ctx.enter_context(nc.sbuf_tensor(name, shape, dt))

        def sem(name):
            return ctx.enter_context(nc.semaphore(name))

        ps = [ctx.enter_context(nc.psum_tensor(f"ps{i}", [128, 512], F)) for i in range(8)]
        raw = sb("raw", [128, NRAW, CW])
        whi = sb("whi", [128, NHL, CW], R)
        wlo = sb("wlo", [128, NHL, CW], R)
        X = sb("X", [128, 2, D])
        xn = sb("xn", [128, 2, D])
        xnf = xn[:, :, :].rearrange("p t d -> p (t d)")
        hh = sb("hh", [128, 8, S], R)
        hl = sb("hl", [128, 8, S], R)
        cst = sb("cst", [128, NCONST])
        gns = sb("gns", [128, NGAIN])
        pbuf = sb("pbuf", [128, 3, 512])
        ptb = sb("ptb", [128, 2, 512])
        ra = sb("ra", [128, 4096], R)
        fa = sb("fa", [128, 11456])
        st = sb("st", [128, 256])
        gw = sb("gw", [17, 256])
        fb8 = sb("fb8", [128, 8])
        t5s = sb("t5s", [32, 16])
        scratch = nc.dram_tensor("t5_rows", [16, 512], F, kind="Internal")

        PE, AC, VE, PO, SP = [Lane(sem(n)) for n in ("s_pe", "s_act", "s_dve", "s_pool", "s_sp")]
        s_raw = [sem(f"s_raw{i}") for i in range(NRAW)]
        s_in = sem("s_in")
        s_x = sem("s_x")
        s_misc = sem("s_misc")
        s_t5w = sem("s_t5w")
        s_bias = [sem(f"s_bias{i}") for i in range(3)]
        s_gf = sem("s_gf")
        s_out = sem("s_out")

        def C(name, rows=128):
            o, n = CONST[name]
            return cst[0:rows, o:o + n]

        def G(name):
            o, n = GAIN[name]
            return gns[:, o:o + n]

        def far(o, n):
            return fa[:, o:o + n]

        def rar(o, n):
            return ra[:, o:o + n]

        def vcopy(o, i, *w):
            return VE.add(lambda e: e.tensor_copy(o, i), w)

        def vtt(o, a, b, op, *w):
            return VE.add(lambda e: e.tensor_tensor(o, a, b, op), w)

        def vts(o, a, s1, s2, op0, op1, *w):
            if s2 is None:
                return VE.add(lambda e: e.tensor_scalar(o, a, s1, None, op0), w)
            return VE.add(lambda e: e.tensor_scalar(o, a, s1, s2, op0, op1), w)

        def vstt(o, a, s, b, op0, op1, *w):
            return VE.add(lambda e: e.scalar_tensor_tensor(out=o, in0=a, scalar=s, in1=b, op0=op0, op1=op1), w)

        def vred(o, a, op, *w, negate=False):
            return VE.add(lambda e: e.tensor_reduce(o, a, AX.X, op, negate=negate), w)

        def vrecip(o, a, *w):
            return VE.add(lambda e: e.reciprocal(o, a), w)

        def vset(o, v, *w):
            return VE.add(lambda e: e.memset(o, v), w)

        def act(o, i, f, *w, scale=1.0, bias=None, accum=None):
            if bias is None and accum is None:
                return AC.add(lambda e: e.activation(o, i, f, scale=scale), w)
            if accum is None:
                return AC.add(lambda e: e.activation(o, i, f, bias=bias, scale=scale), w)
            if bias is None:
                return AC.add(lambda e: e.activation(o, i, f, scale=scale, accum_out=accum), w)
            return AC.add(lambda e: e.activation(o, i, f, bias=bias, scale=scale, accum_out=accum), w)

        def ppow(o, a, n, *w):
            ex = C("mhalf")[:, 0:1].to_broadcast([128, n])
            return PO.add(lambda e: e.tensor_tensor(o, a, ex, ALU.pow), w)

        def mm(o, l, r, first, last, *w, mark=False):
            return PE.add(lambda e: e.matmul(o, l, r, start=first, stop=last, skip_group_check=True), w, mark)

        def tp(o, i, *w, mark=False):
            n = i.shape[0]
            ident = C("ident")[0:n, 0:n]
            return PE.add(lambda e: e.transpose(o, i, ident), w, mark)

        free = {b: [] for b in range(8)}

        def all_now():
            return [(l.sem, l.n) for l in (PE, AC, VE, PO) if l.n]

        loaded, ready, used = {}, {}, {}
        width = [sum(n for *_, n in pieces) for _, pieces in P]

        def load(i):
            if i < len(P):
                k = i % NRAW
                loaded[i] = SP.dma(raw[:, k, 0:width[i]], W[i, :, 0:width[i]], s_raw[k], 16 * (i // NRAW + 1),
                                   [ready.get(i - NRAW)])

        def split(i):
            if i < len(P):
                r, h, l = (a[:, i % n, 0:width[i]] for a, n in ((raw, NRAW), (whi, NHL), (wlo, NHL)))
                t = act(h, r, ACT.Copy, loaded[i], used.get(i - NHL))
                ready[i] = vtt(l, r, h.bitcast(F), ALU.subtract, t)
                load(i + NRAW)

        at = [0]

        def take(tag):
            i = at[0]
            assert P[i][0] == tag, (P[i][0], tag)
            at[0] += 1
            return i

        def done(i, tok):
            used[i] = tok
            split(i + NHL)

        def mm3(o, lh, ll, rh, rl, first, last, *w, mark=False):
            mm(o, lh, rh, first, False, *w)
            mm(o, lh, rl, False, False)
            return mm(o, ll, rh, False, last, mark=mark)

        def gemm_b(tag, xh, xl, nk, wd, outs, *w):
            i = take(tag)
            s = i % NHL
            w = (ready[i],) + w
            for f, o in enumerate(outs):
                for k in range(nk):
                    c = k * wd + f * 128
                    t = mm3(o, whi[:, s, c:c + 128], wlo[:, s, c:c + 128], xh[:, k, :], xl[:, k, :],
                            k == 0, k == nk - 1, *w, mark=(f == len(outs) - 1 and k == nk - 1))
                    w = ()
            done(i, t)
            return t

        def gemm_a(tag, xh, xl, ks, wd, outs, first, last, *w):
            i = take(tag)
            s = i % NHL
            w = (ready[i],) + w
            for n, k in enumerate(ks):
                for t in range(2):
                    tk = slice(128 * t, 128 * t + 128)
                    for c, o in enumerate(outs[t]):
                        a = n * wd + c * 512
                        b = min(a + 512, (n + 1) * wd)
                        tok = mm3(o, xh[:, k, tk], xl[:, k, tk], whi[:, s, a:b], wlo[:, s, a:b],
                                  first and n == 0, last and n == len(ks) - 1, *w,
                                  mark=(n == len(ks) - 1 and t == 1 and c == len(outs[t]) - 1))
                        w = ()
            done(i, tok)
            return tok

        def wide_a(tag, xh, xl, banks, *w):
            outs = [[ps[b][:, :]] for b in banks]
            gemm_a(tag + ".0", xh, xl, range(4), 512, outs, True, False, *w, [free[b] for b in banks])
            return gemm_a(tag + ".1", xh, xl, range(4, 8), 512, outs, False, True)

        def norm_stat(src, d, junk, o, *w):
            ss = [act(junk(t), src(t), ACT.Square, *w, accum=st[:, t:t + 1]) for t in range(2)]
            m = vts(st[:, 2:4], st[:, 0:2], 1.0 / d, EPS, ALU.mult, ALU.add, *ss)
            return ppow(o, st[:, 2:4], 2, m)

        def norm_t(src, d, gain, oh, ol, *w, banks=(0, 1, 2, 3)):
            nk = d // 128
            r = norm_stat(src, d, lambda t: xn[:, t, 0:d], st[:, 4:6], *w)
            y = [vts(xn[:, t, 0:d], src(t), st[:, 4 + t:5 + t], None, ALU.mult, None, r) for t in range(2)]
            toks = []
            for k0 in range(0, nk, 2):
                b = banks[(k0 // 2) % len(banks)]
                kk = range(k0, min(k0 + 2, nk))
                for k in kk:
                    for t in range(2):
                        c = (k - k0) * 256 + t * 128
                        tr = tp(ps[b][:, c:c + 128], xn[:, t, k * 128:(k + 1) * 128], y, free[b],
                                mark=(k == kk[-1] and t == 1))
                hs = [act(oh[:, k, :], ps[b][:, (k - k0) * 256:(k - k0 + 1) * 256], ACT.Copy, tr, *w,
                          scale=gain[:, k:k + 1]) for k in kk]
                for k in kk:
                    lo = vstt(ol[:, k, :], ps[b][:, (k - k0) * 256:(k - k0 + 1) * 256], gain[:, k:k + 1],
                              oh[:, k, :].bitcast(F), ALU.mult, ALU.subtract, hs, *w)
                free[b] = [lo]
                toks.append(lo)
            return toks

        def residual(banks, scale, tok):
            out = []
            for t in range(2):
                for c in range(2):
                    b = banks[t][c]
                    xs = X[:, t, c * 512:(c + 1) * 512]
                    r = vstt(xs, ps[b][:, :], scale, xs, ALU.mult, ALU.add, tok)
                    free[b] = [r]
                    out.append(r)
            return out

        def attention(heads, causal, oh, ol, *w):
            n = len(heads)
            stt = xnf[:, 0:1024].rearrange("p (s c) -> p s c", s=2)
            off = (0, 128) if causal else (0, 256)
            kl = (128, 256) if causal else (256, 256)
            tot = off[1] + kl[1]
            s1, s2, p3, pt, pv, ex, pair = {}, {}, {}, {}, {}, {}, {}
            outs = []

            def scores(h):
                hd = heads[h]
                b = h % 3
                for t in range(2):
                    o = ps[b][:, off[t]:off[t] + kl[t]]
                    more = hd.get("more")
                    s1[h] = mm(o, hd["q"](t), hd["k"](kl[t]), True, more is None, *w, free[b],
                               mark=(t == 1 and more is None))
                    if more is not None:
                        s1[h] = mm(o, more(t)[0], more(t)[1], False, True, mark=(t == 1))

            def soft(h):
                hd = heads[h]
                b = h % 3
                sl = h % 3
                if hd.get("ev") is not None:
                    src = stt[:, h % 2, 0:tot]
                    e = hd["ev"](ps[b], src, s1[h], ex.get(h - 2))
                    free[b] = [e]
                else:
                    src = ps[b][:, 0:tot]
                    e = s1[h]
                c = 16 + 6 * (h % 8)
                nm, sm, rs = st[:, c:c + 2], st[:, c + 2:c + 4], st[:, c + 4:c + 6]
                if causal:
                    m = [vred(nm[:, t:t + 1], src[:, off[t]:off[t] + kl[t]], ALU.max, e, ex.get(h - 8), negate=True)
                         for t in range(2)]
                else:
                    m = vred(nm, src.rearrange("p (t k) -> p t k", t=2), ALU.max, e, ex.get(h - 8), negate=True)
                for t in range(2):
                    ex[h] = act(pbuf[:, sl, off[t]:off[t] + kl[t]], src[:, off[t]:off[t] + kl[t]], ACT.Exp, m,
                                p3.get(h - 3), s2.get(h - 8), bias=nm[:, t:t + 1], accum=sm[:, t:t + 1])
                if hd.get("ev") is None:
                    free[b] = [ex[h]]
                r = vrecip(rs, sm, ex[h])
                for t in range(2):
                    s2[h] = vts(pbuf[:, sl, off[t]:off[t] + kl[t]], pbuf[:, sl, off[t]:off[t] + kl[t]], rs[:, t:t + 1],
                                None, ALU.mult, None, r)

            def turn(h):
                b = 3 + h % 2
                sl = h % 3
                for t in range(2):
                    for k in range(kl[t] // 128):
                        c = 256 * k + 128 * (t - k if causal else t)
                        p3[h] = tp(ps[b][:, c:c + 128], pbuf[:, sl, off[t] + 128 * k:off[t] + 128 * k + 128], s2[h],
                                   free[b], mark=(t == 1 and k == kl[t] // 128 - 1))
                pt[h] = act(ptb[:, h % 2, 0:tot], ps[b][:, 0:tot], ACT.Copy, p3[h], pv.get(h - 2))
                free[b] = [pt[h]]

            def weigh(h):
                hd = heads[h]
                pr, par = divmod(h, 2)
                b = 5 + pr % 2
                o = ps[b][64 * par:64 * par + 64, 0:256]
                mm(o, hd["v"](0), ptb[:, h % 2, 0:256], True, False, pt[h], free[b])
                if causal:
                    pv[h] = mm(o[:, 128:256], hd["v"](1), ptb[:, h % 2, 256:384], False, True, mark=True)
                else:
                    pv[h] = mm(o, hd["v"](1), ptb[:, h % 2, 256:512], False, True, mark=True)
                if par:
                    t = act(oh(pr), ps[b][:, 0:256], ACT.Copy, pv[h])
                    t = vtt(ol(pr), ps[b][:, 0:256], oh(pr).bitcast(F), ALU.subtract, t)
                    free[b] = [t]
                    outs.append(t)

            for i in range(n + 3):
                if i < n:
                    scores(i)
                    soft(i)
                if 2 <= i < n + 2:
                    turn(i - 2)
                if i >= 3:
                    weigh(i - 3)
            return outs

        SPX = AC.dma(X[:, :, :], XIN.rearrange("(t p) d -> p t d", p=128), s_x, 16, [])
        k = 0
        for o, a in ((cst[:, :], CST), (gns[:, :], GNS), (fa[:, 10816:11456], GQK.partition_broadcast(128)),
                     (gw[:, :], GLAG), (fb8[:, :], FOXB.partition_broadcast(128)), (t5s[:, :], T5)):
            k += 16
            PO.dma(o, a, s_in, k, [])
        IN = (s_in, k)
        for i in range(NRAW):
            load(i)
        for i in range(NHL):
            split(i)

        n1 = norm_t(lambda t: X[:, t, :], D, G("g_mix"), hh, hl, SPX, IN)
        z = far(0, 2368).rearrange("p (t c) -> p t c", t=2)
        qa = far(2368, 1536).rearrange("p (t c) -> p t c", t=2)
        qaT = far(3904, 2048).rearrange("p (h c) -> p h c", h=8)
        kaT = far(5952, 2048).rearrange("p (h c) -> p h c", h=8)
        va = far(8000, 1024).rearrange("p (t h c) -> p t h c", t=2, h=8)
        qbT = far(9024, 1024).rearrange("p (h c) -> p h c", h=4)
        kbT = far(10048, 512).rearrange("p (h c) -> p h c", h=2)
        kp = far(10560, 192).rearrange("p (t c) -> p t c", t=2)
        gqk = far(10816, 640)
        cqh = rar(0, 512).rearrange("p (k c) -> p k c", k=2)
        cql = rar(512, 512).rearrange("p (k c) -> p k c", k=2)
        ckh = rar(1024, 256).rearrange("p (k c) -> p k c", k=1)
        ckl = rar(1280, 256).rearrange("p (k c) -> p k c", k=1)

        zt = []
        for c, bs in ((0, (4, 5)), (1, (6, 7))):
            t0 = wide_a(f"z{c}", hh, hl, bs, n1)
            for t in range(2):
                y = act(z[:, t, 512 * c:512 * c + 512], ps[bs[t]][:, :], ACT.Copy, t0)
                free[bs[t]] = [y]
                zt.append(y)
        t0 = gemm_a("z2", hh, hl, range(8), 160, [[ps[0][:, 0:160]], [ps[1][:, 0:160]]], True, True, free[0], free[1])
        for t in range(2):
            y = act(z[:, t, 1024:1184], ps[t][:, 0:160], ACT.Copy, t0)
            free[t] = [y]
            zt.append(y)
        ncq = norm_t(lambda t: z[:, t, 0:256], 256, G("g_qa"), cqh, cql, zt, banks=(2,))
        nck = norm_t(lambda t: z[:, t, 256:384], 128, G("g_kva"), ckh, ckl, zt, (PE.sem, PE.n), banks=(3,))

        outs = [[ps[4][:, :], ps[5][:, 0:256]], [ps[6][:, :], ps[7][:, 0:256]]]
        t0 = gemm_a("wqb", cqh, cql, range(2), 768, outs, True, True, ncq, [free[b] for b in (4, 5, 6, 7)])
        qt = []
        SCA = float(np.float32(96 ** -0.5))
        for t in range(2):
            b = 4 + 2 * t
            y = act(qa[:, t, 0:512], ps[b][:, :], ACT.Copy, t0, scale=SCA)
            free[b] = [y]
            y2 = act(qa[:, t, 512:768], ps[b + 1][:, 0:256], ACT.Copy, t0, scale=SCA)
            free[b + 1] = [y2]
            qt += [y, y2]

        i = take("wkvb")
        s = i % NHL
        for h in range(8):
            b = (0, 1, 2, 3)[h // 2]
            t0 = mm3(ps[b][:, 256 * (h % 2):256 * (h % 2) + 256], whi[:, s, 128 * h:128 * h + 128],
                     wlo[:, s, 128 * h:128 * h + 128], ckh[:, 0, :], ckl[:, 0, :], True, True, ready[i], nck, free[b],
                     mark=(h % 2 == 1))
            if h % 2:
                y = act(kaT[0:64, h - 1:h + 1, :], ps[b][0:64, :].rearrange("p (h c) -> p h c", h=2), ACT.Copy, t0)
                free[b] = [y]
                qt.append(y)
        for t in range(2):
            for c in range(2):
                b = 4 + 2 * t + c
                t0 = mm3(ps[b][:, :], ckh[:, 0, 128 * t:128 * t + 128], ckl[:, 0, 128 * t:128 * t + 128],
                         whi[:, s, 512 * c:512 * c + 512], wlo[:, s, 512 * c:512 * c + 512], True, True, free[b],
                         mark=True)
                y = vcopy(va[:, t, 4 * c:4 * c + 4, :],
                          ps[b][:, :].rearrange("p (h c) -> p h c", h=4)[:, :, 64:128], t0)
                free[b] = [y]
                qt.append(y)
        done(i, t0)

        def rope(x, n, cos, sin, t1, t2, *w):
            a = vtt(t1, x, cos, ALU.mult, *w)
            b = vtt(t2[:, :, 0, :], x[:, :, 1, :], sin[:, :, 0, :], ALU.mult, *w)
            c = vtt(t2[:, :, 1, :], x[:, :, 0, :], sin[:, :, 1, :], ALU.mult, *w)
            return vtt(x, t1, t2, ALU.add, a, b, c)

        vz = vset(kp[:, :, 0:64], 0.0)
        kt = []
        tmp = xnf
        wx = [vz, ncq, nck, qt]
        for t in range(2):
            src = z[:, t, 384:416].rearrange("p (n c d) -> p n c d", n=1, c=2)
            dst = kp[:, t, 64:96].rearrange("p (n c d) -> p n c d", n=1, c=2)
            co = C("cosA")[:, 32 * t:32 * t + 32].rearrange("p (n c d) -> p n c d", n=1, c=2)
            si = C("sinA")[:, 32 * t:32 * t + 32].rearrange("p (n c d) -> p n c d", n=1, c=2)
            cp = vcopy(dst, src, zt)
            r = rope(dst, 1, co, si, tmp[:, 0:32].rearrange("p (n c d) -> p n c d", n=1, c=2),
                     tmp[:, 32:64].rearrange("p (n c d) -> p n c d", n=1, c=2), cp, wx)
            wx = [r]
            kt.append(r)
            qv = qa[:, t, :].rearrange("p (h c) -> p h c", c=96)[:, :, 64:96]
            t1 = tmp[:, 0:256].rearrange("p (h c) -> p h c", h=8)
            t2 = tmp[:, 256:512].rearrange("p (h c) -> p h c", h=8)
            cb = C("cosA")[:, 32 * t:32 * t + 32].unsqueeze(1).to_broadcast([128, 8, 32])
            sb0 = C("sinA")[:, 32 * t:32 * t + 16].unsqueeze(1).to_broadcast([128, 8, 16])
            sb1 = C("sinA")[:, 32 * t + 16:32 * t + 32].unsqueeze(1).to_broadcast([128, 8, 16])
            a = vtt(t1, qv, cb, ALU.mult, qt, wx)
            b = vtt(t2[:, :, 0:16], qv[:, :, 16:32], sb0, ALU.mult)
            c = vtt(t2[:, :, 16:32], qv[:, :, 0:16], sb1, ALU.mult)
            r = vtt(qv, t1, t2, ALU.add, a, b, c)
            wx = [r]
            kt.append(r)
        for t in range(2):
            t0 = tp(ps[0][0:96, 128 * t:128 * t + 128], kp[:, t, :], kt, free[0], mark=(t == 1))
        y = vcopy(kaT[64:96, :, :], ps[0][64:96, 0:256].unsqueeze(1).to_broadcast([32, 8, 256]), t0)
        free[0] = [y]
        att = [y]
        for h in range(8):
            b = (4, 5, 6, 7)[h // 2]
            for t in range(2):
                c = 256 * (h % 2) + 128 * t
                t0 = tp(ps[b][0:96, c:c + 128], qa[:, t, 96 * h:96 * h + 96], kt, free[b], mark=(h % 2 == 1 and t == 1))
            if h % 2:
                y = act(qaT[0:96, h - 1:h + 1, :], ps[b][0:96, :].rearrange("p (h c) -> p h c", h=2), ACT.Copy, t0)
                free[b] = [y]
                att.append(y)

        qk = [z[:, t, 416:1056].rearrange("p (h c) -> p h c", c=64) for t in range(2)]
        sq = tmp[:, 0:1280].rearrange("p (t c) -> p t c", t=2)
        toks = []
        for t in range(2):
            a = vtt(sq[:, t, :], z[:, t, 416:1056], z[:, t, 416:1056], ALU.mult, wx, kt)
            toks.append(vred(st[:, 64 + 10 * t:74 + 10 * t], sq[:, t, :].rearrange("p (h c) -> p h c", c=64), ALU.add, a))
        m = vts(st[:, 84:104], st[:, 64:84], 1.0 / 64, EPS, ALU.mult, ALU.add, toks)
        r = ppow(st[:, 104:124], st[:, 84:104], 20, m)
        kd = tmp[:, 1280:1792].rearrange("p (t c) -> p t c", t=2)
        kdt = []
        for t in range(2):
            rb = st[:, 104 + 10 * t:114 + 10 * t].unsqueeze(2).to_broadcast([128, 10, 64])
            a = vtt(qk[t], qk[t], rb, ALU.mult, r)
            a = vtt(z[:, t, 416:1056], z[:, t, 416:1056], gqk, ALU.mult, a, IN)
            co = C("cosB")[:, 64 * t:64 * t + 64].unsqueeze(1).to_broadcast([128, 10, 64])
            t1 = tmp[:, 0:640].rearrange("p (h c) -> p h c", c=64)
            t2 = tmp[:, 640:1280].rearrange("p (h c) -> p h c", c=64)
            b = vtt(t1, qk[t], co, ALU.mult, a, toks)
            ws = [b]
            for half in range(2):
                x4 = qk[t].rearrange("p h (r c d) -> p h r c d", r=2, c=2)
                t4 = t2.rearrange("p h (r c d) -> p h r c d", r=2, c=2)
                s4 = C("sinB")[:, 64 * t:64 * t + 64].rearrange("p (r c d) -> p r c d", r=2, c=2)
                for rc in range(2):
                    sn = s4[:, rc, half, :].unsqueeze(1).to_broadcast([128, 10, 16])
                    ws.append(vtt(t4[:, :, rc, half, :], x4[:, :, rc, 1 - half, :], sn, ALU.mult, a))
            a = vtt(qk[t], t1, t2, ALU.add, ws)
            toks = [a]
            for j in range(2):
                for d in range(2):
                    kdt.append(vcopy(kd[:, t, 128 * j + 64 * d:128 * j + 64 * d + 64],
                                     z[:, t, 928 + 64 * j:992 + 64 * j], a))
        for j in range(2):
            b = 1 + j
            for pr in range(2):
                for t in range(2):
                    q0 = 416 + 256 * j + 128 * pr
                    t0 = tp(ps[b][:, 256 * pr + 128 * t:256 * pr + 128 * t + 128], z[:, t, q0:q0 + 128], kdt, free[b],
                            mark=(pr == 1 and t == 1))
            y = act(qbT[:, 2 * j:2 * j + 2, :], ps[b][:, :].rearrange("p (h c) -> p h c", h=2), ACT.Copy, t0, scale=0.125)
            free[b] = [y]
            att.append(y)
        for j in range(2):
            for t in range(2):
                c = 256 * j + 128 * t
                t0 = tp(ps[3][:, c:c + 128], kd[:, t, 128 * j:128 * j + 128], kdt, free[3], mark=(j == 1 and t == 1))
        y = act(kbT[:, :, :], ps[3][:, :].rearrange("p (h c) -> p h c", h=2), ACT.Copy, t0)
        free[3] = [y]
        att.append(y)

        def head_a(h):
            return dict(q=lambda t: qaT[0:96, h, 128 * t:128 * t + 128], k=lambda n: kaT[0:96, h, 0:n],
                        v=lambda k: va[:, k, h, :])

        def head_b(h):
            lo = 64 * (h % 2)
            g = h // 4
            return dict(q=lambda t: qbT[lo:lo + 64, h // 2, 128 * t:128 * t + 128],
                        k=lambda n: kbT[lo:lo + 64, g, 0:n],
                        v=lambda k: z[:, k, 1056 + 64 * g:1120 + 64 * g])

        oh = rar(0, 2048).rearrange("p (k c) -> p k c", k=8)
        ol = rar(2048, 2048).rearrange("p (k c) -> p k c", k=8)
        at1 = attention([head_a(h) for h in range(8)] + [head_b(h) for h in range(8)], False,
                        lambda j: oh[:, j, :], lambda j: ol[:, j, :], att, qt)

        now = all_now()
        sg = far(0, 4096).rearrange("p (k c) -> p k c", k=16)
        gt = []
        for g in range(8):
            b = g % 4
            t0 = gemm_b(f"gate{g}", hh, hl, 8, 256, [ps[b][:, 0:256], ps[b][:, 256:512]], n1, free[b])
            y = act(sg[:, 2 * g:2 * g + 2, :], ps[b][:, :].rearrange("p (h c) -> p h c", h=2), ACT.Sigmoid, t0, now)
            free[b] = [y]
            gt.append(y)
        mt = []
        ma = far(4096, 2048).rearrange("p (s c) -> p s c", s=4)
        last_g = (PE.sem, PE.n)
        for c in range(2):
            toks = []
            for n, nm in enumerate(("oa", "ob")):
                i = take(f"{nm}{c}")
                s = i % NHL
                for f in range(4):
                    b = (4, 5)[f // 2] if n == 0 else (6, 7)[f // 2]
                    for k in range(4):
                        a = k * 512 + f * 128
                        t0 = mm3(ps[b][:, 256 * (f % 2):256 * (f % 2) + 256], whi[:, s, a:a + 128], wlo[:, s, a:a + 128],
                                 oh[:, 4 * n + k, :], ol[:, 4 * n + k, :], k == 0, k == 3, ready[i], at1, free[b],
                                 mark=(k == 3 and f % 2 == 1))
                    if f % 2:
                        toks.append(t0)
                done(i, t0)
            for f2 in range(2):
                fs = 4 * c + 2 * f2
                m1, m2 = ma[:, 2 * f2, :], ma[:, 2 * f2 + 1, :]
                a = vtt(m1, ps[4 + f2][:, :], sg[:, fs:fs + 2, :].rearrange("p a b -> p (a b)"), ALU.mult, toks[f2], gt, now, mt)
                b = vtt(m2, ps[6 + f2][:, :], sg[:, 8 + fs:10 + fs, :].rearrange("p a b -> p (a b)"), ALU.mult, toks[2 + f2])
                free[4 + f2], free[6 + f2] = [a], [b]
                a = vtt(m1, m1, m2, ALU.add, a, b)
                hv = hh[:, fs:fs + 2, :].rearrange("p a b -> p (a b)")
                b = act(hv, m1, ACT.Copy, a, last_g)
                mt.append(vtt(hl[:, fs:fs + 2, :].rearrange("p a b -> p (a b)"), m1, hv.bitcast(F), ALU.subtract, b))
        wide_a("o0", hh, hl, (0, 2), mt)
        t0 = wide_a("o1", hh, hl, (1, 3))
        xr = residual([[0, 1], [2, 3]], 1.0, t0)

        ACC = [[0, 1], [2, 3]]

        def grouped(n_groups, first, second):
            for g in range(n_groups + 1):
                if g < n_groups:
                    first(g)
                if g >= 1:
                    second(g - 1)

        uh = rar(0, 1024).rearrange("p (s c) -> p s c", s=2)
        ul = rar(1024, 1024).rearrange("p (s c) -> p s c", s=2)
        fr = far(0, 1024).rearrange("p (s c) -> p s c", s=2)
        fu = far(1024, 1024).rearrange("p (s c) -> p s c", s=2)
        accs = [[ps[b][:, :] for b in r] for r in ACC]

        nm = norm_t(lambda t: X[:, t, :], D, G("g_mlp"), hh, hl, xr, (PE.sem, PE.n), banks=(4, 5, 6, 7))
        now = all_now()
        ud, ut = {}, {}

        def down(tag, g, n_groups):
            u2 = [uh[:, g % 2, :].rearrange("p (k c) -> p k c", k=2), ul[:, g % 2, :].rearrange("p (k c) -> p k c", k=2)]
            ud[g] = gemm_a(f"{tag}{g}", u2[0], u2[1], range(2), 1024, accs, g == 0, g == n_groups - 1, ut[g],
                           [free[b] for b in range(4)])

        def up1(g):
            b = 4 + g % 4
            s = g % 2
            t0 = gemm_b(f"up{g}", hh, hl, 8, 256, [ps[b][:, 0:256], ps[b][:, 256:512]], nm, free[b])
            y = act(fr[:, s, :], ps[b][:, :], ACT.Relu, t0, now, ut.get(g - 2))
            free[b] = [y]
            y = vtt(fu[:, s, :], fr[:, s, :], fr[:, s, :], ALU.mult, y)
            a = act(uh[:, s, :], fu[:, s, :], ACT.Copy, y, ud.get(g - 2))
            ut[g] = vtt(ul[:, s, :], fu[:, s, :], uh[:, s, :].bitcast(F), ALU.subtract, a)

        grouped(16, up1, lambda g: down("dn", g, 16))
        xr = residual(ACC, 1.0, ud[15])

        nm = norm_t(lambda t: X[:, t, :], D, G("g_ple"), hh, hl, xr, (PE.sem, PE.n), banks=(4, 5, 6, 7))
        now = all_now()
        pf = far(2048, 512).rearrange("p (k c) -> p k c", k=2)
        pd = PO.dma(pf, PT_IN.rearrange("(k p) c -> p k c", p=128), s_misc, 16, now)
        gf = far(4096, 1024)
        gfd = PO.dma(gf, GFIN.partition_broadcast(128), s_gf, 16, now)
        ph = rar(0, 512).rearrange("p (k c) -> p k c", k=2)
        pl = rar(512, 512).rearrange("p (k c) -> p k c", k=2)
        a = act(ph, pf, ACT.Copy, pd)
        pt0 = vtt(pl, pf, ph.bitcast(F), ALU.subtract, a)
        t0 = gemm_a("ple", ph, pl, range(2), 1024, accs, True, True, pt0, [free[b] for b in range(4)])
        gs = far(0, 2048).rearrange("p (t d) -> p t d", t=2)
        xr = []
        for c in range(2):
            bs = (4, 5) if c == 0 else (6, 7)
            t1 = wide_a(f"pg{c}", hh, hl, bs, nm)
            for t in range(2):
                sl = slice(512 * c, 512 * c + 512)
                y = act(gs[:, t, sl], ps[bs[t]][:, :], ACT.Sigmoid, t1, now)
                free[bs[t]] = [y]
                y = vtt(gs[:, t, sl], ps[ACC[t][c]][:, :], gs[:, t, sl], ALU.mult, y, t0)
                free[ACC[t][c]] = [y]
                xr.append(vtt(X[:, t, sl], X[:, t, sl], gs[:, t, sl], ALU.add, y))

        def final_norm(gd, dst, *w):
            r = norm_stat(lambda t: X[:, t, :], D, lambda t: xn[:, t, :], st[:, 4:6], *w)
            return [vstt(dst[:, t, :], X[:, t, :], st[:, 4 + t:5 + t], gf, ALU.mult, ALU.mult, r, gd) for t in range(2)]

        xr = final_norm(gfd, X, xr)

        def swiglu(layer, half, gain, *w):
            nm = norm_t(lambda t: X[:, t, :], D, G(gain), hh, hl, *w, (PE.sem, PE.n), banks=(4, 5, 6, 7))
            now = all_now()
            ud.clear()
            ut.clear()

            def up(g):
                s = g % 2
                b = 4 + 2 * s
                o = [[ps[b + j][:, 0:256], ps[b + j][:, 256:512]] for j in range(2)]
                ta = gemm_b(f"fa{layer}{half}.{g}", hh, hl, 8, 256, o[0], nm, free[b])
                y = act(fr[:, s, :], ps[b][:, :], ACT.Silu, ta, now, ut.get(g - 2))
                free[b] = [y]
                tb = gemm_b(f"fb{layer}{half}.{g}", hh, hl, 8, 256, o[1], free[b + 1])
                y = vtt(fu[:, s, :], fr[:, s, :], ps[b + 1][:, :], ALU.mult, y, tb)
                free[b + 1] = [y]
                a = act(uh[:, s, :], fu[:, s, :], ACT.Copy, y, ud.get(g - 2))
                ut[g] = vtt(ul[:, s, :], fu[:, s, :], uh[:, s, :].bitcast(F), ALU.subtract, a)

            grouped(11, up, lambda g: down(f"fd{layer}{half}.", g, 11))
            return residual(ACC, 0.5, ud[10])

        xr = swiglu(0, 0, "n00", xr)

        nm = norm_t(lambda t: X[:, t, :], D, G("n01"), hh, hl, xr, (PE.sem, PE.n), banks=(4, 5, 6, 7))
        now = all_now()
        sm_ = far(0, 48).rearrange("p (t c) -> p t c", t=2)
        glT = fa[0:17, 48:304]
        gk = far(304, 512).rearrange("p (t c) -> p t c", t=2)
        ga, ge = far(816, 512), far(1328, 512)
        lf = far(1840, 16).rearrange("p (t c) -> p t c", t=2)
        la, lb = far(1856, 16), far(1872, 16)
        vg = far(1888, 1024).rearrange("p (t c) -> p t c", t=2)
        go = far(2912, 1024)
        GT = far(3936, 512).rearrange("p (r c) -> p r c", r=2)
        eG = far(4448, 512).rearrange("p (r c) -> p r c", r=2)
        enG = far(4960, 512).rearrange("p (r c) -> p r c", r=2)
        eE = far(5472, 512).rearrange("p (r c) -> p r c", r=2)
        qd = far(5984, 512).rearrange("p (r c) -> p r c", r=2)
        kdc = far(6496, 512).rearrange("p (r c) -> p r c", r=2)
        ke = far(7008, 512).rearrange("p (r c) -> p r c", r=2)
        ktk = far(7520, 512).rearrange("p (r t c) -> p r t c", r=2, t=2)
        AT = far(8032, 1024).rearrange("p (s r t c) -> p s r t c", s=2, r=2, t=2)
        sts = far(9056, 1536).rearrange("p (n r c) -> p n r c", n=3, r=2)
        nFT = fa[0:8, 10592:10848]
        Ft = far(10848, 16).rearrange("p (t c) -> p t c", t=2)
        mh = rar(0, 2048).rearrange("p (k c) -> p k c", k=8)
        ml = rar(2048, 2048).rearrange("p (k c) -> p k c", k=8)

        t0 = gemm_a("small", hh, hl, range(8), 24, [[ps[0][:, 0:24]], [ps[1][:, 0:24]]], True, True, nm, free[0], free[1])
        sy = []
        for t in range(2):
            y = act(sm_[:, t, :], ps[t][:, 0:24], ACT.Copy, t0, now)
            free[t] = [y]
            sy.append(y)
        g1 = vset(glT, 1.0, now)
        for t in range(2):
            t0 = tp(ps[2][0:16, 128 * t:128 * t + 128], sm_[:, t, 0:16], sy, free[2], mark=(t == 1))
        g1 = vcopy(glT[0:16, :], ps[2][0:16, 0:256], t0, g1)
        free[2] = [g1]
        for t in range(2):
            t0 = mm(ps[3][:, 256 * t:256 * t + 256], glT[:, 128 * t:128 * t + 128], gw[:, :], True, True, g1, IN, free[3],
                    mark=(t == 1))

        def log_sigmoid(o, x, a, b, t):
            y = act(a, x, ACT.Abs, t)
            y = act(b, a, ACT.Exp, y, scale=-1.0)
            y = act(a, b, ACT.Ln, y, bias=C("ones")[:, 0:1])
            return vstt(o, x, 0.0, a, ALU.min, ALU.subtract, y)

        fx = [vtt(sm_[:, t, 16:24], sm_[:, t, 16:24], fb8[:, :], ALU.add, sy, IN) for t in range(2)]
        lg = log_sigmoid(gk.rearrange("p t c -> p (t c)"), ps[3][:, :], ga, ge, t0)
        free[3] = [lg]
        la3 = la.rearrange("p (t c) -> p t c", t=2)
        lb3 = lb.rearrange("p (t c) -> p t c", t=2)
        lff = log_sigmoid(lf, sm_[:, :, 16:24], la3, lb3, fx)

        t0 = wide_a("vg", hh, hl, (4, 5))
        vt = []
        for t in range(2):
            y = act(vg[:, t, :], ps[4 + t][:, :], ACT.Copy, t0, now)
            free[4 + t] = [y]
            vt.append(y)
        for g in range(2):
            t0 = gemm_b(f"go{g}", hh, hl, 8, 256, [ps[6 + g][:, 0:256], ps[6 + g][:, 256:512]], free[6 + g])
            y = act(go[:, 512 * g:512 * g + 512], ps[6 + g][:, :], ACT.Silu, t0, now)
            free[6 + g] = [y]
            vt.append(y)
        for p in range(2):
            for t in range(2):
                t0 = mm(ps[2][:, 256 * p + 128 * t:256 * p + 128 * t + 128], gk[:, t, 128 * p:128 * p + 128], C("tri64"),
                        True, True, lg, free[2], mark=(p == 1 and t == 1))
        y = vcopy(GT, ps[2][:, :].rearrange("p (r c) -> p r c", r=2), t0)
        free[2] = [y]
        e1 = act(eG, GT, ACT.Exp, y)
        e2 = act(enG, GT, ACT.Exp, y, scale=-1.0)
        for p in range(2):
            for c in range(4):
                e3 = act(eE[:, p, 64 * c:64 * c + 64], GT[:, p, 64 * c:64 * c + 64], ACT.Exp, y, scale=-1.0,
                         bias=GT[:, p, 64 * c + 63:64 * c + 64])
        t0 = gemm_b("qg", hh, hl, 8, 256, [ps[0][:, 0:256], ps[0][:, 256:512]], free[0])
        yq = vstt(qd.rearrange("p r c -> p (r c)"), ps[0][:, :], 0.125, eG.rearrange("p r c -> p (r c)"),
                  ALU.mult, ALU.mult, t0, e1)
        free[0] = [yq]
        t0 = gemm_b("kg", hh, hl, 8, 256, [ps[1][:, 0:256], ps[1][:, 256:512]], free[1])
        yk = vtt(kdc.rearrange("p r c -> p (r c)"), ps[1][:, :], enG.rearrange("p r c -> p (r c)"), ALU.mult, t0, e2)
        ye = vtt(ke.rearrange("p r c -> p (r c)"), ps[1][:, :], eE.rearrange("p r c -> p (r c)"), ALU.mult, e3)
        free[1] = [ye]

        mm(ps[3][0:8, 0:256], lf[:, 0, :], cst[:, CONST["tri"][0]:CONST["tri"][0] + 256], True, False, lff, free[3])
        t0 = mm(ps[3][0:8, 128:256], lf[:, 1, :], C("tri"), False, True, mark=True)
        yf = vts(nFT, ps[3][0:8, 0:256], -1.0, None, ALU.mult, None, t0)
        free[3] = [yf]
        mm(ps[3][:, 0:8], C("tri"), lf[:, 0, :], True, True, free[3])
        mm(ps[3][:, 8:16], C("ones"), lf[:, 0, :], True, False)
        t0 = mm(ps[3][:, 8:16], C("tri"), lf[:, 1, :], False, True, mark=True)
        yF = vcopy(Ft, ps[3][:, 0:16].rearrange("p (t c) -> p t c", t=2), t0)
        free[3] = [yF]

        for p in range(2):
            for t in range(2):
                for par in range(2):
                    r0 = 64 * par
                    tk = slice(128 * t, 128 * t + 128)
                    c = 256 * p + 128 * t
                    t0 = mm(ps[4 + par][:, c:c + 128], kdc[r0:r0 + 64, p, tk], qd[r0:r0 + 64, p, tk], True, True, yq, yk,
                            free[4 + par], mark=True)
        m64 = C("m64").unsqueeze(1).to_broadcast([128, 4, 128])
        ya = []
        for par in range(2):
            y = vtt(AT[:, par].rearrange("p r t c -> p (r t) c"), ps[4 + par][:, :].rearrange("p (g c) -> p g c", g=4), m64,
                    ALU.mult, t0)
            free[4 + par] = [y]
            ya.append(y)
        for p in range(2):
            for t in range(2):
                c = 256 * p + 128 * t
                t0 = tp(ps[6][:, c:c + 128], ke[:, p, 128 * t:128 * t + 128], ye, free[6], mark=(p == 1 and t == 1))
        y = act(ktk, ps[6][:, :].rearrange("p (r t c) -> p r t c", r=2, t=2), ACT.Copy, t0)
        free[6] = [y]
        kb = (7, 0, 1)
        for c in range(3):
            t, r0 = c // 2, 64 * (c % 2)
            for p in range(2):
                t0 = mm(ps[kb[c]][:, 256 * p:256 * p + 256], ktk[r0:r0 + 64, p, t, :], vg[r0:r0 + 64, t, 256 * p:256 * p + 256],
                        True, True, y, vt, free[kb[c]], mark=(p == 1))
            if c == 0:
                ys = vcopy(sts[:, 0].rearrange("p r c -> p (r c)"), ps[kb[0]][:, :], t0)
            else:
                for p in range(2):
                    ys = vstt(sts[:, c, p, :], sts[:, c - 1, p, :], eG[:, p, 64 * c + 63:64 * c + 64],
                              ps[kb[c]][:, 256 * p:256 * p + 256], ALU.mult, ALU.add, t0, ys)
            free[kb[c]] = [ys]
        gm = []
        og, ov = xnf[:, 0:1024].rearrange("p (s c) -> p s c", s=2), xnf[:, 1024:2048].rearrange("p (s c) -> p s c", s=2)
        gov = go.rearrange("p (r s c) -> p s r c", r=2, s=2)
        mhv, mlv = (a[:, 0:4, :].rearrange("p (r s) c -> p s r c", s=2) for a in (mh, ml))
        for par in range(2):
            b = 2 + par
            r0 = 64 * par
            for p in range(2):
                h = 2 * p + par
                for t in range(2):
                    o = ps[b][:, 256 * p + 128 * t:256 * p + 128 * t + 128]
                    mm(o, vg[:, t, 128 * h:128 * h + 128], AT[:, par, p, t, :], True, False, ya, vt, free[b])
                    for c in range(2 * t, 2 * t + 2):
                        if c >= 1:
                            t0 = mm(o[:, 64 * (c % 2):64 * (c % 2) + 64], sts[r0:r0 + 64, c - 1, p, 128 * par:128 * par + 128],
                                    qd[r0:r0 + 64, p, 64 * c:64 * c + 64], False, True, ys,
                                    mark=(p == 1 and c == 3))
            y = act(og[:, par, :], ps[b][:, :], ACT.Square, t0)
            tq = mm(ps[4 + par][:, :], C("ones"), og[:, par, :], True, True, y, free[4 + par], mark=True)
            y = vts(ov[:, par, :], ps[4 + par][:, :], 1.0 / 128, EPS, ALU.mult, ALU.add, tq)
            free[4 + par] = [y]
            y = act(ov[:, par, :], ov[:, par, :], ACT.Ln, y)
            y = act(ov[:, par, :], ov[:, par, :], ACT.Exp, y, scale=-0.5)
            y = vstt(ov[:, par, :], ps[b][:, :], G("g_gla")[:, 0:1], ov[:, par, :], ALU.mult, ALU.mult, y)
            free[b] = [y]
            o2 = ov[:, par, :].rearrange("p (r c) -> p r c", r=2)
            y = vtt(o2, o2, gov[:, par], ALU.mult, y, vt)
            a = act(mhv[:, par], o2, ACT.Copy, y, now)
            gm.append(vtt(mlv[:, par], o2, mhv[:, par].bitcast(F), ALU.subtract, a))

        now = all_now()
        qf = far(0, 1024).rearrange("p (k c) -> p k c", k=4)
        kf = far(1024, 1024).rearrange("p (k c) -> p k c", k=4)
        vf = far(2048, 1024).rearrange("p (t c) -> p t c", t=2)
        ft = [now]
        for n, (nme, dst, sc) in enumerate((("qf", qf, 0.125), ("kf", kf, 1.0))):
            for g in range(2):
                b = 2 * n + g
                t0 = gemm_b(f"{nme}{g}", hh, hl, 8, 256, [ps[b][:, 0:256], ps[b][:, 256:512]], free[b])
                y = act(dst[:, 2 * g:2 * g + 2, :], ps[b][:, :].rearrange("p (h c) -> p h c", h=2), ACT.Copy, t0, now,
                        scale=sc)
                free[b] = [y]
                ft.append(y)
        t0 = wide_a("vf", hh, hl, (4, 5))
        for t in range(2):
            y = act(vf[:, t, :], ps[4 + t][:, :], ACT.Copy, t0, now)
            free[4 + t] = [y]
            ft.append(y)
        cm = C("cm")

        def head_f(h):
            lo = 64 * (h % 2)

            def ev(bank, src, t, w):
                vstt(src[:, 0:128], bank[:, 0:128], Ft[:, 0, h:h + 1], cm[:, 128:256], ALU.add, ALU.add, t, w)
                return vstt(src[:, 128:384], bank[:, 128:384], Ft[:, 1, h:h + 1], cm, ALU.add, ALU.add)

            return dict(q=lambda t: qf[lo:lo + 64, h // 2, 128 * t:128 * t + 128],
                        k=lambda n: kf[lo:lo + 64, h // 2, 0:n],
                        v=lambda k: vf[:, k, 64 * h:64 * h + 64],
                        more=lambda t: (C("sel", 8)[:, 128 * h:128 * h + 128], nFT[:, 0:128 + 128 * t]), ev=ev)

        at2 = attention([head_f(h) for h in range(8)], True, lambda j: mh[:, 4 + j, :], lambda j: ml[:, 4 + j, :], ft)
        wide_a("eo0", mh, ml, (0, 2), gm, at2)
        t0 = wide_a("eo1", mh, ml, (1, 3))
        xr = residual(ACC, 1.0, t0)
        xr = swiglu(0, 1, "n02", xr)
        xr = swiglu(1, 0, "n10", xr)

        nm = norm_t(lambda t: X[:, t, :], D, G("n11"), hh, hl, xr, (PE.sem, PE.n), banks=(4, 5, 6, 7))
        now = all_now()
        qT = far(0, 2048).rearrange("p (k c) -> p k c", k=8)
        kT = far(2048, 2048).rearrange("p (k c) -> p k c", k=8)
        vv = far(4096, 2048).rearrange("p (t c) -> p t c", t=2)
        ck = far(6144, 512).rearrange("p (t c) -> p t c", t=2)
        qiT = far(6656, 1024).rearrange("p (k c) -> p k c", k=4)
        kiT = far(7680, 256)
        ki = far(7936, 256).rearrange("p (t c) -> p t c", t=2)
        wi = far(8192, 16).rearrange("p (t c) -> p t c", t=2)
        acc = far(8208, 384)
        wk = far(8592, 384)
        msk = far(8976, 384)
        rl = far(9360, 1024).rearrange("p (s c) -> p s c", s=2)
        top = [st[:, 200 + 8 * t:208 + 8 * t] for t in range(2)]
        bring = far(9360, 768).rearrange("p (s c) -> p s c", s=3)
        bsum = far(10128, 1152).rearrange("p (s c) -> p s c", s=3)

        t0 = mm(ps[0][0:16, :], t5s[:, :], C("hot", 32), True, True, IN, free[0], mark=True)
        y = vcopy(fa[0:16, 10592:11104], ps[0][0:16, :], t0, now)
        free[0] = [y]
        t5w = PO.dma(scratch.ap(), fa[0:16, 10592:11104], s_t5w, 16, [y])

        t0 = gemm_a("ckv", hh, hl, range(8), 256, [[ps[1][:, 0:256]], [ps[2][:, 0:256]]], True, True, nm, free[1], free[2])
        cy = []
        for t in range(2):
            y = act(ck[:, t, :], ps[1 + t][:, 0:256], ACT.Copy, t0, now)
            free[1 + t] = [y]
            cy.append(y)
        t0 = gemm_a("kwi", hh, hl, range(8), 72, [[ps[3][:, 0:72]], [ps[0][:, 0:72]]], True, True, free[3], free[0])
        wy = []
        for t, b in enumerate((3, 0)):
            for d in range(2):
                y = act(ki[:, t, 64 * d:64 * d + 64], ps[b][:, 0:64], ACT.Copy, t0, now)
            y = act(wi[:, t, :], ps[b][:, 64:72], ACT.Copy, t0, now, scale=float(np.float32(8 ** -0.5)))
            free[b] = [y]
            wy.append(y)
        qy = []
        for g in range(2):
            t0 = gemm_b(f"qi{g}", hh, hl, 8, 256, [ps[1 + g][:, 0:256], ps[1 + g][:, 256:512]], free[1 + g])
            y = act(qiT[:, 2 * g:2 * g + 2, :], ps[1 + g][:, :].rearrange("p (h c) -> p h c", h=2), ACT.Copy, t0, now,
                    scale=0.125)
            free[1 + g] = [y]
            qy.append(y)
        for t in range(2):
            t0 = tp(ps[3][:, 128 * t:128 * t + 128], ki[:, t, :], wy, free[3], mark=(t == 1))
        y = act(kiT, ps[3][:, 0:256], ACT.Copy, t0, now)
        free[3] = [y]
        qy.append(y)
        ch = rar(0, 512).rearrange("p (k c) -> p k c", k=2)
        cl = rar(512, 512).rearrange("p (k c) -> p k c", k=2)
        nc_ = norm_t(lambda t: ck[:, t, :], 256, G("g_ckv"), ch, cl, cy, now, banks=(4,))

        OFF, KL = (0, 128), (128, 256)
        av, rt = None, {}

        def index_head(h):
            nonlocal av
            b = 5 + h % 3
            lo = 64 * (h % 2)
            for t in range(2):
                t0 = mm(ps[b][:, OFF[t]:OFF[t] + KL[t]], qiT[lo:lo + 64, h // 2, 128 * t:128 * t + 128],
                        kiT[lo:lo + 64, 0:KL[t]], True, True, qy, free[b], mark=(t == 1))
            s = h % 2
            y = act(rl[:, s, 0:384], ps[b][:, 0:384], ACT.Relu, t0, now, rt.get(h - 2))
            free[b] = [y]
            for t in range(2):
                a = acc[:, OFF[t]:OFF[t] + KL[t]]
                r = rl[:, s, OFF[t]:OFF[t] + KL[t]]
                if h == 0:
                    av = vts(a, r, wi[:, t, h:h + 1], None, ALU.mult, None, y, wy, now)
                else:
                    av = vstt(a, r, wi[:, t, h:h + 1], a, ALU.mult, ALU.add, y, av)
            rt[h] = av

        for h in range(8):
            index_head(h)
        a = [vtt(wk[:, 0:128], acc[:, 0:128], cm[:, 128:256], ALU.add, av, now),
             vtt(wk[:, 128:384], acc[:, 128:384], cm, ALU.add)]
        for r in range(8):
            for t in range(2):
                w_ = wk[:, OFF[t]:OFF[t] + KL[t]]
                a[t] = VE.add(lambda e, w_=w_, t=t: e.max(top[t], w_), [a[t]])
            for t in range(2):
                w_ = wk[:, OFF[t]:OFF[t] + KL[t]]
                a[t] = VE.add(lambda e, w_=w_, t=t: e.match_replace(w_, top[t], w_, GONE), [a[t]])
        y = vts(msk, wk, GONE, 1.0, ALU.is_equal, ALU.subtract, a)
        y = vts(msk, msk, -NEG, None, ALU.mult, None, y)
        y1 = vtt(msk[:, 0:128], msk[:, 0:128], cm[:, 128:256], ALU.add, y)
        y2 = vtt(msk[:, 128:384], msk[:, 128:384], cm, ALU.add, y)
        mk = [y1, y2]

        dt = [now]
        for g in range(4):
            b = g
            t0 = gemm_b(f"q{g}", hh, hl, 8, 256, [ps[b][:, 0:256], ps[b][:, 256:512]], free[b])
            y = act(qT[:, 2 * g:2 * g + 2, :], ps[b][:, :].rearrange("p (h c) -> p h c", h=2), ACT.Copy, t0, now, scale=0.125)
            free[b] = [y]
            dt.append(y)
        i = take("uk")
        s = i % NHL
        for f in range(8):
            b = 4 + f // 2
            for k in range(2):
                a = k * 1024 + f * 128
                t0 = mm3(ps[b][:, 256 * (f % 2):256 * (f % 2) + 256], whi[:, s, a:a + 128], wlo[:, s, a:a + 128],
                         ch[:, k, :], cl[:, k, :], k == 0, k == 1, ready[i], nc_, free[b], mark=(k == 1 and f % 2 == 1))
            if f % 2:
                y = act(kT[:, f - 1:f + 1, :], ps[b][:, :].rearrange("p (h c) -> p h c", h=2), ACT.Copy, t0, now)
                free[b] = [y]
                dt.append(y)
        done(i, t0)
        t0 = gemm_a("uv", ch, cl, range(2), 1024, accs, True, True, [free[b] for b in range(4)])
        for t in range(2):
            for c in range(2):
                b = ACC[t][c]
                y = act(vv[:, t, 512 * c:512 * c + 512], ps[b][:, :], ACT.Copy, t0, now)
                free[b] = [y]
                dt.append(y)
        uvt = t0

        ba, bu = {}, {}
        sapp = scratch.ap()

        def bias_load(h):
            k = h % 3
            src = bass.AP(sapp.tensor, 512 * h + 128, [[1, 128], [1, 256]])
            tk = PO.dma(bring[:, k, :], src, s_bias[k], 16 * (h // 3 + 1), [t5w, ba.get(h - 3), mk, uvt])
            for t in range(2):
                at0 = bring[:, k, KL[t] - 1:KL[t]]
                back = bass.AP(at0.tensor, at0.offset, [list(at0.ap[0]), [-1, KL[t]]])
                o, m_ = bsum[:, k, OFF[t]:OFF[t] + KL[t]], msk[:, OFF[t]:OFF[t] + KL[t]]
                ba[h] = PO.add(lambda e, o=o, back=back, m_=m_: e.tensor_tensor(o, back, m_, ALU.add),
                               [tk, mk, bu.get(h - 3)])

        def head_d(h):
            lo = 64 * (h % 2)

            def ev(bank, src, t, w):
                bu[h] = vtt(src, bank[:, 0:384], bsum[:, h % 3, :], ALU.add, t, w, ba[h])
                if h + 3 < 16:
                    bias_load(h + 3)
                return bu[h]

            return dict(q=lambda t: qT[lo:lo + 64, h // 2, 128 * t:128 * t + 128],
                        k=lambda n: kT[lo:lo + 64, h // 2, 0:n],
                        v=lambda k: vv[:, k, 64 * h:64 * h + 64], ev=ev)

        for h in range(3):
            bias_load(h)
        at3 = attention([head_d(h) for h in range(16)], True, lambda j: mh[:, j, :], lambda j: ml[:, j, :], dt, uvt)
        wide_a("oo0", mh, ml, (0, 2), at3)
        t0 = wide_a("oo1", mh, ml, (1, 3))
        xr = residual(ACC, 1.0, t0)
        now = all_now()
        xr = swiglu(1, 1, "n12", xr)
        now = all_now()
        gfd = PO.dma(gf, GFIN2.partition_broadcast(128), s_gf, 32, now)
        xr = final_norm(gfd, X, xr)
        out = SP.dma(OUT.rearrange("(t p) d -> p t d", p=128), X[:, :, :], s_out, 16, xr)
        assert at[0] == len(P)

        block = ctx.enter_context(nc.Block())

        @block.sync
        def _(e):
            SP.play(e)
            e.wait_ge(*out)
            e.wait_ge(*t5w)

        @block.tensor
        def _(e):
            PE.play(e)

        @block.scalar
        def _(e):
            AC.play(e)

        @block.vector
        def _(e):
            VE.play(e)

        @block.gpsimd
        def _(e):
            PO.play(e)


def layout(inputs):
    a = {k: np.asarray(v) for k, v in inputs.items()}
    w = {n: a[n][0] for n in ("w_in", "w_qb", "w_kvb", "w_oa", "w_ob", "w_o", "w_up", "w_down", "w_ple_gate", "w_ple")}
    for layer in range(2):
        for half in range(2):
            w[f"ffn_in{layer}{half}"] = a["ffn_w_in_2"][layer, half]
            w[f"ffn_out{layer}{half}"] = a["ffn_w_out_2"][layer, half]
    w["even_in"], w["even_out"] = a["even_w_in_2"][0], a["even_w_out_2"][0]
    w["odd_in"], w["odd_out"] = a["odd_w_in_2"][0], a["odd_w_out_2"][0]
    w["w_ukT"] = a["mla_w_uk_2"][0].transpose(2, 0, 1).reshape(256, 1024)
    w["w_uv"] = a["mla_w_uv_2"][0].transpose(1, 0, 2).reshape(256, 1024)
    P = plan()
    W = np.zeros((len(P), 128, CW), np.float32)
    for i, (_, pieces) in enumerate(P):
        c = 0
        for name, r0, c0, n in pieces:
            W[i, :, c:c + n] = w[name][r0:r0 + 128, c0:c0 + n]
            c += n

    gains = np.zeros((128, NGAIN), np.float32)
    ng = a["norm_g_2"]
    for name, g in dict(g_mix=a["g_mix"][0], g_qa=a["g_qa"][0], g_kva=a["g_kva"][0], g_mlp=a["g_mlp"][0],
                        g_ple=a["g_ple"][0], n00=ng[0, 0], n01=ng[0, 1], n02=ng[0, 2], n10=ng[1, 0], n11=ng[1, 1],
                        n12=ng[1, 2], g_gla=a["gla_norm_g_2"][0], g_ckv=a["mla_kv_norm_g_2"][0]).items():
        o, n = GAIN[name]
        gains[:, o:o + n] = g.reshape(n, 128).T
    return {
        "w_chunks": W,
        "x_in": np.ascontiguousarray(a["x"][0]),
        "p_t": np.ascontiguousarray(a["p"][0, 0].T),
        "consts": constants(),
        "gains": gains,
        "g_qk": np.concatenate([np.tile(a["g_qn"][0], 8), np.tile(a["g_kn"][0], 2)]),
        "g_fin": np.ascontiguousarray(a["g_final"]),
        "g_fin2": np.ascontiguousarray(a["final_norm_g_2"]),
        "gla_gate": np.concatenate([a["gla_w_gate_2"][0], a["gla_b_gate_2"]], 0),
        "fox_b": np.ascontiguousarray(a["fox_b_f_2"][0]),
        "t5": np.ascontiguousarray(a["t5_table_2"]),
    }


def kernel(**inputs):
    import concourse.bacc as _bacc
    from concourse.bass_utils import run_bass_kernel_spmd as _run

    nc = _bacc.Bacc("TRN2", target_bir_lowering=False, num_devices=1)
    arrays = layout(inputs)
    args = [nc.dram_tensor(n, a.shape, mybir.dt.from_np(a.dtype), kind="ExternalInput").ap() for n, a in arrays.items()]
    args.append(nc.dram_tensor("out_dram", (S, D), F, kind="ExternalOutput").ap())
    program(nc, *args)
    r = _run(nc, [arrays], core_ids=[0])
    return r.results[0]["out_dram"].reshape(1, S, D)
```

```python
from contextlib import ExitStack

import concourse.bass as bass
from concourse import mybir
import numpy as np

F = mybir.dt.float32
R = mybir.dt.float32r
ACT = mybir.ActivationFunctionType
ALU = mybir.AluOpType
AX = mybir.AxisListType

S = 256
D = 1024
CW = 2048
NRAW = 4
HW = 1024
NHL = 4
EPS = 1e-6
NEG = -1e30
GONE = -3e38
H2 = 2816



def plan():
    out = []

    def cols(tag, w, k, c0, n, kts=None):
        out.append((tag, [(w, 128 * t, c0, n) for t in (kts or range(k))]))

    def wide(tag, w, c0):
        for part in range(2):
            cols(f"{tag}.{part}", w, 8, c0, 512, range(4 * part, 4 * part + 4))

    def halves(*tags):
        for part in range(2):
            for tag, w, c0 in tags:
                cols(f"{tag}.{part}", w, 8, c0, 512, range(4 * part, 4 * part + 4))

    def grouped(n, lag, ups, tag, w):
        for g in range(n):
            for u, src, c0 in ups:
                cols(f"{u}{g}", src, 8, c0 + 256 * g, 256)
            if lag <= g < n - 3 + lag:
                cols(f"{tag}{g - lag}", w, 0, 0, 1024, (2 * (g - lag), 2 * (g - lag) + 1))
        for g in range(n - 3, n):
            cols(f"{tag}{g}", w, 0, 0, 1024, (2 * g, 2 * g + 1))

    def gates(*gs):
        for g in gs:
            cols(f"gate{g}", "w_in", 8, 1184 + 256 * g, 256)

    halves(("z0", "w_in", 0), ("z1", "w_in", 512))
    cols("z2", "w_in", 8, 1024, 160)
    gates(0, 1)
    cols("wqb", "w_qb", 2, 0, 768)
    cols("wkvb", "w_kvb", 1, 0, 1024)
    gates(2, 3, 4, 5, 6, 7)
    for c in range(2):
        cols(f"oa{c}", "w_oa", 4, 512 * c, 512)
        cols(f"ob{c}", "w_ob", 4, 512 * c, 512)
    halves(("o0", "w_o", 0), ("o1", "w_o", 512))
    grouped(16, 2, [("up", "w_up", 0)], "dn", "w_down")
    cols("pg0.0", "w_ple_gate", 0, 0, 512, range(4))
    cols("pg1.0", "w_ple_gate", 0, 512, 512, range(4))
    cols("ple", "w_ple", 2, 0, 1024)
    cols("pg0.1", "w_ple_gate", 0, 0, 512, range(4, 8))
    cols("pg1.1", "w_ple_gate", 0, 512, 512, range(4, 8))

    def ffn(layer, half):
        a, b = f"ffn_in{layer}{half}", f"ffn_out{layer}{half}"
        grouped(11, 1, [(f"fa{layer}{half}.", a, 0), (f"fb{layer}{half}.", a, H2)], f"fd{layer}{half}.", b)

    ffn(0, 0)
    out.append(("small", [("even_in", 128 * t, c, n) for t in range(8) for c, n in ((1536, 16), (3088, 8))]))
    wide("vg", "even_in", 512)
    for g in range(2):
        cols(f"go{g}", "even_in", 8, 1024 + 256 * g, 256)
    cols("qg", "even_in", 8, 0, 256)
    cols("kg", "even_in", 8, 256, 256)
    for n, c0 in (("qf", 1552), ("kf", 2064)):
        for g in range(2):
            cols(f"{n}{g}", "even_in", 8, c0 + 256 * g, 256)
    wide("vf", "even_in", 2576)
    halves(("eo0", "even_out", 0), ("eo1", "even_out", 512))
    ffn(0, 1)
    ffn(1, 0)
    cols("ckv", "odd_in", 8, 1024, 256)
    cols("kwi", "odd_in", 8, 1792, 72)
    for g in range(2):
        cols(f"qi{g}", "odd_in", 8, 1280 + 256 * g, 256)
    for g in range(4):
        cols(f"q{g}", "odd_in", 8, 256 * g, 256)
    cols("uk", "w_ukT", 2, 0, 1024)
    cols("uv", "w_uv", 2, 0, 1024)
    halves(("oo0", "odd_out", 0), ("oo1", "odd_out", 512))
    ffn(1, 1)
    return out



CONST = dict(ident=(0, 128), tri=(128, 128), ones=(256, 128), tri64=(384, 128), m64=(512, 128), cm=(640, 256),
             cosA=(896, 64), sinA=(960, 64), cosB=(1024, 128), sinB=(1152, 128), hot=(1280, 512), sel=(1792, 1024),
             mhalf=(2816, 16))
NCONST = 2832
GAIN = dict(g_mix=(0, 8), g_qa=(8, 2), g_kva=(10, 1), g_mlp=(11, 8), g_ple=(19, 8), n00=(27, 8), n01=(35, 8),
            n02=(43, 8), n10=(51, 8), n11=(59, 8), n12=(67, 8), g_gla=(75, 1), g_ckv=(76, 2))
NGAIN = 78


def constants():
    c = np.zeros((128, NCONST), np.float32)

    def put(name, a):
        o, n = CONST[name]
        a = np.asarray(a, np.float32)
        c[:a.shape[0], o:o + n] = a.reshape(a.shape[0], n)

    p = np.arange(128)
    le = p[:, None] <= p[None, :]
    same = (p[:, None] // 64) == (p[None, :] // 64)
    put("ident", np.eye(128))
    put("tri", le)
    put("ones", np.ones((128, 128)))
    put("tri64", (le & same) / 16.0)
    put("m64", le & same)
    put("cm", np.concatenate([np.zeros((128, 128)), np.where(p[None, :] <= p[:, None], 0.0, NEG)], 1))
    inv = np.float32(10000.0) ** (-np.arange(0, 32, 2, dtype=np.float32) / np.float32(32))

    def angles(pos):
        a = (pos.astype(np.float32)[:, None] * inv[None, :]).astype(np.float32).astype(np.float64)
        co, si = np.cos(a), np.sin(a)
        return np.concatenate([co, co], 1), np.concatenate([-si, si], 1)

    t = np.arange(S)
    ca, sa = angles(t)
    cr, sr = angles(t // 64)
    cc, sc = angles(t % 64)

    def tok(a):
        return a.reshape(2, 128, -1).transpose(1, 0, 2)

    put("cosA", tok(ca))
    put("sinA", tok(sa))
    put("cosB", tok(np.concatenate([cr, cc], 1)))
    put("sinB", tok(np.concatenate([sr, sc], 1)))
    dist = np.maximum(np.arange(512) - 255, 0)
    d = np.maximum(dist, 1).astype(np.float32)
    large = 16 + (np.log(d / np.float32(16)).astype(np.float32) / np.float32(np.log(8.0)) * np.float32(16)).astype(np.int32)
    bucket = np.where(dist < 16, dist, np.minimum(large, 31))
    put("hot", np.arange(32)[:, None] == bucket[None, :])
    sel = np.zeros((8, 8, 128))
    sel[np.arange(8), np.arange(8)] = 1.0
    put("sel", sel)
    put("mhalf", np.full((128, 16), -0.5))
    return c


class Lane:

    def __init__(self, sem):
        self.sem, self.n, self.q, self.seen = sem, 0, [], {}

    def add(self, fn, after, mark=True):
        waits = []
        todo = list(after)
        while todo:
            w = todo.pop(0)
            if isinstance(w, list):
                todo += w
            elif w is not None and self.seen.get(w[0].name, 0) < w[1]:
                self.seen[w[0].name] = w[1]
                waits.append(w)
        self.q.append((waits, fn, self.sem if mark else None, 1))
        if mark:
            self.n += 1
            return (self.sem, self.n)
        return None

    def dma(self, out, in_, sem, value, after):
        self.add(lambda e: e.dma_start(out, in_), after, mark=False)
        waits, fn, _, _ = self.q.pop()
        self.q.append((waits, fn, sem, 16))
        return (sem, value)

    def play(self, eng):
        for waits, fn, sem, by in self.q:
            for s, v in waits:
                eng.wait_ge(s, v)
            ins = fn(eng)
            if sem is not None:
                ins.then_inc(sem, by)


def program(nc, W, XIN, PT_IN, CST, GNS, GQK, GFIN, GFIN2, GLAG, FOXB, T5, OUT):
    P = plan()
    with ExitStack() as ctx:
        def sb(name, shape, dt=F):
            return ctx.enter_context(nc.sbuf_tensor(name, shape, dt))

        def sem(name):
            return ctx.enter_context(nc.semaphore(name))

        ps = [ctx.enter_context(nc.psum_tensor(f"ps{i}", [128, 512], F)) for i in range(8)]
        raw = sb("raw", [128, NRAW, HW])
        whi = sb("whi", [128, NHL, CW], R)
        wlo = sb("wlo", [128, NHL, CW], R)
        X = sb("X", [128, 2, D])
        xn = sb("xn", [128, 2, D])
        xnf = xn[:, :, :].rearrange("p t d -> p (t d)")
        hh = sb("hh", [128, 8, S], R)
        hl = sb("hl", [128, 8, S], R)
        cst = sb("cst", [128, NCONST])
        gns = sb("gns", [128, NGAIN])
        pbuf = sb("pbuf", [128, 3, 512])
        ptb = sb("ptb", [128, 2, 512])
        ra = sb("ra", [128, 4096], R)
        fa = sb("fa", [128, 11456])
        st = sb("st", [128, 256])
        rbb = sb("rbb", [128, 2, 256])
        fx = sb("fx", [128, 2048])
        gw = sb("gw", [17, 256])
        fb8 = sb("fb8", [128, 8])
        t5s = sb("t5s", [32, 16])
        scratch = nc.dram_tensor("t5_rows", [16, 512], F, kind="Internal")

        PE, AC, VE, PO, SP = [Lane(sem(n)) for n in ("s_pe", "s_act", "s_dve", "s_pool", "s_sp")]
        s_raw = [sem(f"s_raw{i}") for i in range(NRAW)]
        s_in = sem("s_in")
        s_first = sem("s_first")
        s_x = [sem(f"s_x{i}") for i in range(2)]
        s_misc = sem("s_misc")
        s_t5w = sem("s_t5w")
        s_bias = [sem(f"s_bias{i}") for i in range(3)]
        s_gf = sem("s_gf")
        s_out = sem("s_out")

        def C(name, rows=128):
            o, n = CONST[name]
            return cst[0:rows, o:o + n]

        def G(name):
            o, n = GAIN[name]
            return gns[:, o:o + n]

        def far(o, n):
            return fa[:, o:o + n]

        def rar(o, n):
            return ra[:, o:o + n]

        def vcopy(o, i, *w):
            return VE.add(lambda e: e.tensor_copy(o, i), w)

        def vtt(o, a, b, op, *w):
            return VE.add(lambda e: e.tensor_tensor(o, a, b, op), w)

        def vts(o, a, s1, s2, op0, op1, *w):
            if s2 is None:
                return VE.add(lambda e: e.tensor_scalar(o, a, s1, None, op0), w)
            return VE.add(lambda e: e.tensor_scalar(o, a, s1, s2, op0, op1), w)

        def vstt(o, a, s, b, op0, op1, *w):
            return VE.add(lambda e: e.scalar_tensor_tensor(out=o, in0=a, scalar=s, in1=b, op0=op0, op1=op1), w)

        def vred(o, a, op, *w, negate=False):
            return VE.add(lambda e: e.tensor_reduce(o, a, AX.X, op, negate=negate), w)

        def vrecip(o, a, *w):
            return VE.add(lambda e: e.reciprocal(o, a), w)

        def vset(o, v, *w):
            return VE.add(lambda e: e.memset(o, v), w)

        def act(o, i, f, *w, scale=1.0, bias=None, accum=None):
            if bias is None and accum is None:
                return AC.add(lambda e: e.activation(o, i, f, scale=scale), w)
            if accum is None:
                return AC.add(lambda e: e.activation(o, i, f, bias=bias, scale=scale), w)
            if bias is None:
                return AC.add(lambda e: e.activation(o, i, f, scale=scale, accum_out=accum), w)
            return AC.add(lambda e: e.activation(o, i, f, bias=bias, scale=scale, accum_out=accum), w)

        def ppow(o, a, n, *w):
            ex = C("mhalf")[:, 0:1].to_broadcast([128, n])
            return PO.add(lambda e: e.tensor_tensor(o, a, ex, ALU.pow), w)

        def mm(o, l, r, first, last, *w, mark=False):
            return PE.add(lambda e: e.matmul(o, l, r, start=first, stop=last, skip_group_check=True), w, mark)

        def tp(o, i, *w, mark=False):
            n = i.shape[0]
            ident = C("ident")[0:n, 0:n]
            return PE.add(lambda e: e.transpose(o, i, ident), w, mark)

        free = {b: [] for b in range(8)}

        def all_now():
            return [(l.sem, l.n) for l in (PE, AC, VE, PO) if l.n]

        ready, used, loaded = {}, {}, {}
        halves_of, parts = [], []
        for i, (_, pieces) in enumerate(P):
            n = sum(p[3] for p in pieces)
            halves_of.append(range(len(parts), len(parts) + (n + HW - 1) // HW))
            parts += [(i, c, min(HW, n - c)) for c in range(0, n, HW)]

        def load(j):
            if j < len(parts):
                i, c, n = parts[j]
                k = j % NRAW
                loaded[j] = SP.dma(raw[:, k, 0:n], W[i, :, c:c + n], s_raw[k], 16 * (j // NRAW + 1), [loaded.get(("s", j - NRAW))])

        def split_half(j):
            i, c, n = parts[j]
            r, h, l = raw[:, j % NRAW, 0:n], whi[:, i % NHL, c:c + n], wlo[:, i % NHL, c:c + n]
            t = act(h, r, ACT.Copy, loaded[j], used.get(i - NHL))
            ready[i] = loaded["s", j] = vtt(l, r, h.bitcast(F), ALU.subtract, t)
            load(j + NRAW)

        held = []

        def release(n=99):
            while held and n:
                split_half(held.pop(0))
                n -= 1

        def split(i, hold=False):
            if i < len(P):
                held.extend(halves_of[i])
            if not hold:
                release()

        at = [0]

        def take(tag):
            i = at[0]
            assert P[i][0] == tag, (P[i][0], tag)
            at[0] += 1
            return i

        def done(i, tok, hold=False):
            used[i] = tok
            split(i + NHL, hold)

        def mm3(o, lh, ll, rh, rl, first, last, *w, mark=False):
            mm(o, lh, rh, first, False, *w)
            mm(o, lh, rl, False, False)
            return mm(o, ll, rh, False, last, mark=mark)

        def gemm_b(tag, xh, xl, nk, wd, outs, *w, hold=False):
            i = take(tag)
            s = i % NHL
            w = (ready[i],) + w
            for f, o in enumerate(outs):
                for k in range(nk):
                    c = k * wd + f * 128
                    t = mm3(o, whi[:, s, c:c + 128], wlo[:, s, c:c + 128], xh[:, k, :], xl[:, k, :],
                            k == 0, k == nk - 1, *w, mark=(f == len(outs) - 1 and k == nk - 1))
                    w = ()
            done(i, t, hold)
            return t

        def gemm_a(tag, xh, xl, ks, wd, outs, first, last, *w, hold=False):
            i = take(tag)
            s = i % NHL
            w = (ready[i],) + w
            for n, k in enumerate(ks):
                for t in range(2):
                    tk = slice(128 * t, 128 * t + 128)
                    for c, o in enumerate(outs[t]):
                        a = n * wd + c * 512
                        b = min(a + 512, (n + 1) * wd)
                        tok = mm3(o, xh[:, k, tk], xl[:, k, tk], whi[:, s, a:b], wlo[:, s, a:b],
                                  first and n == 0, last and n == len(ks) - 1, *w,
                                  mark=(n == len(ks) - 1 and t == 1 and c == len(outs[t]) - 1))
                        w = ()
            done(i, tok, hold)
            return tok

        def wide_a(tag, xh, xl, banks, *w):
            outs = [[ps[b][:, :]] for b in banks]
            gemm_a(tag + ".0", xh, xl, range(4), 512, outs, True, False, *w, [free[b] for b in banks])
            return gemm_a(tag + ".1", xh, xl, range(4, 8), 512, outs, False, True)

        def norm_stat(src, d, junk, o, *w):
            ss = [act(junk(t), src(t), ACT.Square, *w, accum=st[:, t:t + 1]) for t in range(2)]
            m = vts(st[:, 2:4], st[:, 0:2], 1.0 / d, EPS, ALU.mult, ALU.add, *ss)
            return ppow(o, st[:, 2:4], 2, m)

        def norm_t(src, d, gain, oh, ol, *w, banks=(0, 1, 2, 3)):
            nk = d // 128
            r = norm_stat(src, d, lambda t: xn[:, t, 0:d], st[:, 4:6], *w)
            y = [vts(xn[:, t, 0:d], src(t), st[:, 4 + t:5 + t], None, ALU.mult, None, r) for t in range(2)]
            toks = []
            for k0 in range(0, nk, 2):
                b = banks[(k0 // 2) % len(banks)]
                kk = range(k0, min(k0 + 2, nk))
                for k in kk:
                    for t in range(2):
                        c = (k - k0) * 256 + t * 128
                        tr = tp(ps[b][:, c:c + 128], xn[:, t, k * 128:(k + 1) * 128], y, free[b],
                                mark=(k == kk[-1] and t == 1))
                hs = [act(oh[:, k, :], ps[b][:, (k - k0) * 256:(k - k0 + 1) * 256], ACT.Copy, tr, *w,
                          scale=gain[:, k:k + 1]) for k in kk]
                for k in kk:
                    lo = vstt(ol[:, k, :], ps[b][:, (k - k0) * 256:(k - k0 + 1) * 256], gain[:, k:k + 1],
                              oh[:, k, :].bitcast(F), ALU.mult, ALU.subtract, hs, *w)
                free[b] = [lo]
                toks.append(lo)
            return toks

        ACC = [[0, 1], [2, 3]]
        accs = [[ps[b][:, :] for b in r] for r in ACC]
        joins = [0]
        junk = {}

        def add_half(c, scale, tok):
            out = []
            for t in range(2):
                b = ACC[t][c]
                xs = X[:, t, c * 512:(c + 1) * 512]
                r = vstt(xs, ps[b][:, :], scale, xs, ALU.mult, ALU.add, tok)
                free[b] = [r]
                out.append(r)
            return out

        def square_half(q, c, rt):
            out = []
            for t in range(2):
                sl = slice(c * 512, (c + 1) * 512)
                junk[t, c] = act(xn[:, t, sl], X[:, t, sl], ACT.Square, rt[t], junk.get((t, c)),
                                 accum=st[:, q + 2 * c + t:q + 2 * c + t + 1])
                out.append(junk[t, c])
            return out

        def turn_half(c, gain, rt, src=X):
            toks = []
            for p in range(2):
                b = ACC[p][c]
                for k in range(4 * c + 2 * p, 4 * c + 2 * p + 2):
                    for t in range(2):
                        o = (k % 2) * 256 + t * 128
                        tr = tp(ps[b][:, o:o + 128], src[:, t, k * 128:(k + 1) * 128], rt, free[b],
                                mark=(k % 2 == 1 and t == 1))
                kk = [(k, ps[b][:, (k % 2) * 256:(k % 2 + 1) * 256]) for k in range(4 * c + 2 * p, 4 * c + 2 * p + 2)]
                hi = [act(hh[:, k, :], pk, ACT.Copy, tr, scale=gain[:, k:k + 1]) for k, pk in kk]
                for k, pk in kk:
                    lo = vstt(hl[:, k, :], pk, gain[:, k:k + 1], hh[:, k, :].bitcast(F), ALU.mult, ALU.subtract, hi)
                    toks.append(lo)
                free[b] = [lo]
            return toks

        def rms_inv(o, q, *w):
            m = vtt(st[:, q + 4:q + 6], st[:, q:q + 2], st[:, q + 2:q + 4], ALU.add, *w)
            m = vts(st[:, q + 4:q + 6], st[:, q + 4:q + 6], 1.0 / D, EPS, ALU.mult, ALU.add, m)
            return ppow(o, st[:, q + 4:q + 6], 2, m)

        def diagonal(r, tok):
            return [vts(rbb[:, 1, 128 * t:128 * t + 128], C("ident"), r[:, t:t + 1], None, ALU.mult, None, tok, rbd[0])
                    for t in range(2)]

        rbd, rb_read = [None], [None]

        def spread(dg, b):
            for t in range(2):
                y = mm(ps[b][:, 128 * t:128 * t + 128], C("ones"), rbb[:, 1, 128 * t:128 * t + 128], True, True, dg,
                       free[b], mark=(t == 1))
            rbd[0] = y
            y = act(rbb[:, 0, :], ps[b][:, 0:256], ACT.Copy, y, rb_read[0])
            free[b] = [y]
            return y

        def join(c0, c1, scale, gain):
            q = 128 + 16 * (joins[0] % 4)
            joins[0] += 1
            rb_read[0] = all_now()
            rt0 = add_half(0, scale, c0())
            tok = c1[0]()
            sq = square_half(q, 0, rt0)
            n0 = turn_half(0, gain, rt0)
            for f in c1[1:]:
                tok = f()
            rt1 = add_half(1, scale, tok)
            sq += square_half(q, 1, rt1)
            r = st[:, q + 6:q + 8]
            rtok = rms_inv(r, q, sq)

            def second():
                n1 = turn_half(1, gain, rt1)
                dg = diagonal(r, rtok)
                release()
                return n1, dg

            return dict(x=rt0 + rt1, n0=n0, second=second, r=r, rtok=rtok)

        def proj_halves(tag, xh, xl, w0, w1):
            for c in range(2):
                gemm_a(f"{tag}{c}.0", xh, xl, range(4), 512, [[accs[0][c]], [accs[1][c]]], True, False, w0,
                       [free[ACC[t][c]] for t in range(2)])

            def c0():
                return gemm_a(f"{tag}0.1", xh, xl, range(4, 8), 512, [[accs[0][0]], [accs[1][0]]], False, True, w1,
                              hold=True)

            i1 = []

            def c1(ks):
                def f():
                    if not i1:
                        i1.append(take(f"{tag}1.1"))
                    i = i1[0]
                    s = i % NHL
                    for n in ks:
                        for t in range(2):
                            tk = slice(128 * t, 128 * t + 128)
                            tok = mm3(accs[t][1], xh[:, 4 + n, tk], xl[:, 4 + n, tk], whi[:, s, 512 * n:512 * n + 512],
                                      wlo[:, s, 512 * n:512 * n + 512], False, n == 3, ready[i],
                                      mark=(n == ks[-1] and t == 1))
                    if ks[-1] == 3:
                        done(i, tok, hold=True)
                    return tok
                return f

            return c0, [c1((0, 1)), c1((2, 3))]

        def b_part(i, ks, outs, first, last, *w):
            s = i % NHL
            w = (ready[i],) + w
            for f, o in enumerate(outs):
                for k in ks:
                    c = k * 256 + f * 128
                    t = mm3(o, whi[:, s, c:c + 128], wlo[:, s, c:c + 128], hh[:, k, :], hl[:, k, :],
                            first and f == 0 and k == ks[0], last and k == ks[-1], *w,
                            mark=(f == 1 and k == ks[-1]))
                    w = ()
            return t

        def opening(tags, banks, J):
            ii = [take(t) for t in tags]
            late = J.get("late")
            o = [[ps[b][:, 0:256], ps[b][:, 256:512]] for b in banks]
            b_part(ii[0], range(4), o[0], True, False, J["n0"], free[banks[0]])
            if late is None:
                n1, dg = J["second"]()
            b_part(ii[1], range(4), o[1], True, False, free[banks[1]])
            if late is not None:
                n1, dg = J["second"]()
                late()
            ta = b_part(ii[0], range(4, 8), o[0], False, True, n1)
            done(ii[0], ta, hold=True)
            rbt = spread(dg, 0)
            tb = b_part(ii[1], range(4, 8), o[1], False, True)
            done(ii[1], tb, hold=True)
            return ta, tb, rbt

        def attention(heads, causal, oh, ol, *w, fill=lambda n: None, outs=None):
            n = len(heads)
            stt = xnf[:, 0:1024].rearrange("p (s c) -> p s c", s=2)
            off = (0, 128) if causal else (0, 256)
            kl = (128, 256) if causal else (256, 256)
            tot = off[1] + kl[1]
            s1, s2, p3, pt, pv, ex = {}, {}, {}, {}, {}, {}
            outs = [] if outs is None else outs

            def scores(h):
                hd = heads[h]
                b = h % 2
                for t in range(2):
                    o = ps[b][:, off[t]:off[t] + kl[t]]
                    more = hd.get("more")
                    s1[h] = mm(o, hd["q"](t), hd["k"](kl[t]), True, more is None, *w, free[b],
                               mark=(t == 1 and more is None))
                    if more is not None:
                        s1[h] = mm(o, more(t)[0], more(t)[1], False, True, mark=(t == 1))

            def soft(h):
                hd = heads[h]
                b = h % 2
                sl = h % 3
                if hd.get("ev") is not None:
                    src = stt[:, h % 2, 0:tot]
                    e = hd["ev"](ps[b], src, s1[h], ex.get(h - 2))
                    free[b] = [e]
                else:
                    src = ps[b][:, 0:tot]
                    e = s1[h]
                c = 16 + 6 * (h % 8)
                nm, sm, rs = st[:, c:c + 2], st[:, c + 2:c + 4], st[:, c + 4:c + 6]
                if causal:
                    m = [vred(nm[:, t:t + 1], src[:, off[t]:off[t] + kl[t]], ALU.max, e, ex.get(h - 8), negate=True)
                         for t in range(2)]
                else:
                    m = vred(nm, src.rearrange("p (t k) -> p t k", t=2), ALU.max, e, ex.get(h - 8), negate=True)
                for t in range(2):
                    ex[h] = act(pbuf[:, sl, off[t]:off[t] + kl[t]], src[:, off[t]:off[t] + kl[t]], ACT.Exp, m,
                                p3.get(h - 3), s2.get(h - 8), bias=nm[:, t:t + 1], accum=sm[:, t:t + 1])
                if hd.get("ev") is None:
                    free[b] = [ex[h]]
                r = vrecip(rs, sm, ex[h])
                for t in range(2):
                    s2[h] = vts(pbuf[:, sl, off[t]:off[t] + kl[t]], pbuf[:, sl, off[t]:off[t] + kl[t]], rs[:, t:t + 1],
                                None, ALU.mult, None, r)

            def turn(h):
                b = 3 + h % 2
                sl = h % 3
                for t in range(2):
                    for k in range(kl[t] // 128):
                        c = 256 * k + 128 * (t - k if causal else t)
                        p3[h] = tp(ps[b][:, c:c + 128], pbuf[:, sl, off[t] + 128 * k:off[t] + 128 * k + 128], s2[h],
                                   free[b], mark=(t == 1 and k == kl[t] // 128 - 1))
                pt[h] = act(ptb[:, h % 2, 0:tot], ps[b][:, 0:tot], ACT.Copy, p3[h], pv.get(h - 2))
                free[b] = [pt[h]]

            def weigh(h):
                hd = heads[h]
                pr, par = divmod(h, 2)
                b = 5 + pr % 2
                o = ps[b][64 * par:64 * par + 64, 0:256]
                mm(o, hd["v"](0), ptb[:, h % 2, 0:256], True, False, pt[h], free[b])
                if causal:
                    pv[h] = mm(o[:, 128:256], hd["v"](1), ptb[:, h % 2, 256:384], False, True, mark=True)
                else:
                    pv[h] = mm(o, hd["v"](1), ptb[:, h % 2, 256:512], False, True, mark=True)
                if par:
                    t = act(oh(pr), ps[b][:, 0:256], ACT.Copy, pv[h])
                    t = vtt(ol(pr), ps[b][:, 0:256], oh(pr).bitcast(F), ALU.subtract, t)
                    free[b] = [t]
                    outs.append(t)

            for i in range(n + 3):
                if i < n:
                    scores(i)
                    soft(i)
                    fill(2)
                if 2 <= i < n + 2:
                    turn(i - 2)
                    fill(1)
                if i >= 3:
                    weigh(i - 3)
                    fill(2)
            return outs

        xv = XIN.rearrange("(t p) d -> p t d", p=128)
        XT = [[SP.dma(X[:, :, 512 * c:512 * c + 512], xv[:, :, 512 * c:512 * c + 512], s_x[c], 16, [])] * 2
              for c in range(2)]
        n = CONST["ident"][1]
        AC.dma(cst[:, 0:n], CST[:, 0:n], s_first, 16, [])
        FIRST = AC.dma(gns[:, :], GNS, s_first, 32, [])
        for i in range(NRAW):
            load(i)
        k = 0
        for o, a in ((cst[:, n:NCONST], CST[:, n:NCONST]), (fa[:, 10816:11456], GQK.partition_broadcast(128)),
                     (gw[:, :], GLAG), (fb8[:, :], FOXB.partition_broadcast(128)), (t5s[:, :], T5)):
            k += 16
            PO.dma(o, a, s_in, k, [])
        IN = (s_in, k)

        q = 128
        joins[0] = 1
        n0 = turn_half(0, G("g_mix"), [XT[0][0], FIRST])
        n1 = turn_half(1, G("g_mix"), [XT[1][0], FIRST])
        sq = square_half(q, 0, XT[0]) + square_half(q, 1, XT[1])
        for i in range(NHL):
            split(i)
        rX = st[:, q + 6:q + 8]
        rXt = rms_inv(rX, q, sq, IN)
        dg = diagonal(rX, rXt)
        z = far(0, 2368).rearrange("p (t c) -> p t c", t=2)
        qa = far(2368, 1536).rearrange("p (t c) -> p t c", t=2)
        qaT = far(3904, 2048).rearrange("p (h c) -> p h c", h=8)
        kaT = far(5952, 2048).rearrange("p (h c) -> p h c", h=8)
        va = far(8000, 1024).rearrange("p (t h c) -> p t h c", t=2, h=8)
        qbT = far(9024, 1024).rearrange("p (h c) -> p h c", h=4)
        kbT = far(10048, 512).rearrange("p (h c) -> p h c", h=2)
        kp = far(10560, 192).rearrange("p (t c) -> p t c", t=2)
        gqk = far(10816, 640)
        cqh = rar(0, 512).rearrange("p (k c) -> p k c", k=2)
        cql = rar(512, 512).rearrange("p (k c) -> p k c", k=2)
        ckh = rar(1024, 256).rearrange("p (k c) -> p k c", k=1)
        ckl = rar(1280, 256).rearrange("p (k c) -> p k c", k=1)

        zt = []
        ZB = [[4, 6], [5, 7]]
        for part in range(2):
            for c in range(2):
                tz = gemm_a(f"z{c}.{part}", hh, hl, range(4 * part, 4 * part + 4), 512,
                            [[ps[ZB[t][c]][:, :]] for t in range(2)], part == 0, part == 1, (n0, n1)[part],
                            [free[ZB[t][c]] for t in range(2)] if part == 0 else None)
                if part == 0:
                    continue
                for t in range(2):
                    b = ZB[t][c]
                    y = act(z[:, t, 512 * c:512 * c + 512], ps[b][:, :], ACT.Copy, tz, rXt, scale=rX[:, t:t + 1])
                    free[b] = [y]
                    zt.append(y)
        rbt = spread(dg, 2)
        t0 = gemm_a("z2", hh, hl, range(8), 160, [[ps[0][:, 0:160]], [ps[1][:, 0:160]]], True, True, free[0], free[1])
        for t in range(2):
            y = act(z[:, t, 1024:1184], ps[t][:, 0:160], ACT.Copy, t0, scale=rX[:, t:t + 1])
            free[t] = [y]
            zt.append(y)

        sg = [fx[:, 512 * g:512 * g + 512] for g in range(4)] + [xnf[:, 512 * g:512 * g + 512] for g in range(4)]
        gt = {}
        rbc = rbb[:, 0, :].unsqueeze(1).to_broadcast([128, 2, 256])

        def two(a):
            return a.rearrange("p (h c) -> p h c", h=2)

        def gate(g, b, *w):
            i = take(f"gate{g}")
            s = i % NHL
            for f in range(2):
                for k in range(8):
                    c = k * 256 + f * 128
                    t0 = mm3(ps[b][:, 256 * f:256 * f + 256], whi[:, s, c:c + 128], wlo[:, s, c:c + 128], hh[:, k, :],
                             hl[:, k, :], k == 0, k == 7, ready[i], free[b], mark=(f == 1 and k == 7))
                    if (f, k) != (1, 7):
                        yield
            y = vtt(two(sg[g]), two(ps[b][:, :]), rbc, ALU.mult, t0, rbt, *w)
            free[b] = [y]
            gt[g] = act(sg[g], sg[g], ACT.Tanh, y, scale=0.5)
            done(i, t0, hold=True)
            yield

        for t in range(2):
            a0 = act(xnf[:, 384 * t:384 * t + 256], z[:, t, 0:256], ACT.Square, zt, sq, accum=st[:, t:t + 1])
            a1 = act(xnf[:, 384 * t + 256:384 * t + 384], z[:, t, 256:384], ACT.Square, accum=st[:, 2 + t:3 + t])
        m = [vts(st[:, 4:6], st[:, 0:2], 1.0 / 256, EPS, ALU.mult, ALU.add, a1),
             vts(st[:, 6:8], st[:, 2:4], 1.0 / 128, EPS, ALU.mult, ALU.add)]
        r = ppow(st[:, 8:12], st[:, 4:8], 4, m)
        qk = [z[:, t, 416:1056].rearrange("p (h c) -> p h c", c=64) for t in range(2)]
        pb = pbuf[:, :, :].rearrange("p s c -> p (s c)")
        hsq = []
        for t in range(2):
            a = act(pb[:, 640 * t:640 * t + 640], z[:, t, 416:1056], ACT.Square, zt)
            hsq.append(a)
        yn = []
        for t in range(2):
            yn.append(vts(xnf[:, 384 * t:384 * t + 256], z[:, t, 0:256], st[:, 8 + t:9 + t], None, ALU.mult, None, r))
            yn.append(vts(xnf[:, 384 * t + 256:384 * t + 384], z[:, t, 256:384], st[:, 10 + t:11 + t], None, ALU.mult, None))
        hs = [vred(st[:, 64 + 10 * t:74 + 10 * t], pb[:, 640 * t:640 * t + 640].rearrange("p (h c) -> p h c", c=64),
                   ALU.add, hsq[t]) for t in range(2)]
        m = vts(st[:, 84:104], st[:, 64:84], 1.0 / 64, EPS, ALU.mult, ALU.add, hs)
        rh = ppow(st[:, 104:124], st[:, 84:104], 20, m)

        for _ in gate(0, 6):
            pass
        release()
        for k in range(2):
            for t in range(2):
                c = k * 256 + t * 128
                tq = tp(ps[2][:, c:c + 128], xnf[:, 384 * t + 128 * k:384 * t + 128 * k + 128], yn, free[2],
                        mark=(k == 1 and t == 1))
        for t in range(2):
            tk = tp(ps[3][:, 128 * t:128 * t + 128], xnf[:, 384 * t + 256:384 * t + 384], free[3], mark=(t == 1))
        ncq = []
        hs = [act(cqh[:, k, :], ps[2][:, 256 * k:256 * k + 256], ACT.Copy, tq, scale=G("g_qa")[:, k:k + 1]) for k in range(2)]
        for k in range(2):
            ncq.append(vstt(cql[:, k, :], ps[2][:, 256 * k:256 * k + 256], G("g_qa")[:, k:k + 1], cqh[:, k, :].bitcast(F),
                            ALU.mult, ALU.subtract, hs))
        free[2] = [ncq[-1]]
        a = act(ckh[:, 0, :], ps[3][:, 0:256], ACT.Copy, tk, scale=G("g_kva")[:, 0:1])
        nck = vstt(ckl[:, 0, :], ps[3][:, 0:256], G("g_kva")[:, 0:1], ckh[:, 0, :].bitcast(F), ALU.mult, ALU.subtract, a)
        free[3] = [nck]
        ytr = [ncq, nck]

        kd = ptb[:, :, 0:256]
        kdt = []

        def by_head(t, *w):
            rb = st[:, 104 + 10 * t:114 + 10 * t].unsqueeze(2).to_broadcast([128, 10, 64])
            a = vtt(qk[t], qk[t], rb, ALU.mult, rh)
            return vtt(z[:, t, 416:1056], z[:, t, 416:1056], gqk, ALU.mult, a, IN)

        def axes(t, a, *w):
            def ptt(o, x, y, op, *w):
                return PO.add(lambda e: e.tensor_tensor(o, x, y, op), w)

            co = C("cosB")[:, 64 * t:64 * t + 64].unsqueeze(1).to_broadcast([128, 10, 64])
            t1 = pb[:, 0:640].rearrange("p (h c) -> p h c", c=64)
            t2 = pb[:, 640:1280].rearrange("p (h c) -> p h c", c=64)
            ws = [ptt(t1, qk[t], co, ALU.mult, a, *w)]
            x4 = qk[t].rearrange("p h (r c d) -> p h r c d", r=2, c=2)
            t4 = t2.rearrange("p h (r c d) -> p h r c d", r=2, c=2)
            s4 = C("sinB")[:, 64 * t:64 * t + 64].rearrange("p (r c d) -> p r c d", r=2, c=2)
            for half in range(2):
                for rc in range(2):
                    sn = s4[:, rc, half, :].unsqueeze(1).to_broadcast([128, 10, 16])
                    ws.append(ptt(t4[:, :, rc, half, :], x4[:, :, rc, 1 - half, :], sn, ALU.mult))
            return ws

        def axes_end(t, ws):
            t1 = pb[:, 0:640].rearrange("p (h c) -> p h c", c=64)
            t2 = pb[:, 640:1280].rearrange("p (h c) -> p h c", c=64)
            a = vtt(qk[t], t1, t2, ALU.add, ws)
            for j in range(2):
                for d in range(2):
                    kdt.append(vcopy(kd[:, t, 128 * j + 64 * d:128 * j + 64 * d + 64],
                                     z[:, t, 928 + 64 * j:992 + 64 * j], a))
            return a

        def rope(x, n, cos, sin, t1, t2, *w):
            a = vtt(t1, x, cos, ALU.mult, *w)
            b = vtt(t2[:, :, 0, :], x[:, :, 1, :], sin[:, :, 0, :], ALU.mult, *w)
            c = vtt(t2[:, :, 1, :], x[:, :, 0, :], sin[:, :, 1, :], ALU.mult, *w)
            return vtt(x, t1, t2, ALU.add, a, b, c)

        a = by_head(0)
        ws = axes(0, a, hs)
        vz = vset(kp[:, :, 0:64], 0.0)
        kt = []
        tmp = xnf
        wx = [vz, ytr, IN]
        for t in range(2):
            src = z[:, t, 384:416].rearrange("p (n c d) -> p n c d", n=1, c=2)
            dst = kp[:, t, 64:96].rearrange("p (n c d) -> p n c d", n=1, c=2)
            co = C("cosA")[:, 32 * t:32 * t + 32].rearrange("p (n c d) -> p n c d", n=1, c=2)
            si = C("sinA")[:, 32 * t:32 * t + 32].rearrange("p (n c d) -> p n c d", n=1, c=2)
            cp = vcopy(dst, src, zt)
            wx = [rope(dst, 1, co, si, tmp[:, 0:32].rearrange("p (n c d) -> p n c d", n=1, c=2),
                       tmp[:, 32:64].rearrange("p (n c d) -> p n c d", n=1, c=2), cp, wx)]
            kt.append(wx)
        for _ in gate(1, 7):
            pass
        release()

        outs = [[ps[4][:, :], ps[5][:, 0:256]], [ps[6][:, :], ps[7][:, 0:256]]]
        t0 = gemm_a("wqb", cqh, cql, range(2), 768, outs, True, True, ncq, [free[b] for b in (4, 5, 6, 7)])
        qt = []
        SCA = float(np.float32(96 ** -0.5))
        for t in range(2):
            b = 4 + 2 * t
            y = act(qa[:, t, 0:512], ps[b][:, :], ACT.Copy, t0, scale=SCA)
            free[b] = [y]
            y2 = act(qa[:, t, 512:768], ps[b + 1][:, 0:256], ACT.Copy, t0, scale=SCA)
            free[b + 1] = [y2]
            qt += [y, y2]

        i = take("wkvb")
        s = i % NHL
        for h in range(8):
            b = (0, 1, 2, 3)[h // 2]
            t0 = mm3(ps[b][:, 256 * (h % 2):256 * (h % 2) + 256], whi[:, s, 128 * h:128 * h + 128],
                     wlo[:, s, 128 * h:128 * h + 128], ckh[:, 0, :], ckl[:, 0, :], True, True, ready[i], nck, free[b],
                     mark=(h % 2 == 1))
            if h % 2:
                y = act(kaT[0:64, h - 1:h + 1, :], ps[b][0:64, :].rearrange("p (h c) -> p h c", h=2), ACT.Copy, t0)
                free[b] = [y]
                qt.append(y)
        for t in range(2):
            for c in range(2):
                b = 4 + 2 * t + c
                t0 = mm3(ps[b][:, :], ckh[:, 0, 128 * t:128 * t + 128], ckl[:, 0, 128 * t:128 * t + 128],
                         whi[:, s, 512 * c:512 * c + 512], wlo[:, s, 512 * c:512 * c + 512], True, True, free[b],
                         mark=True)
                y = vcopy(va[:, t, 4 * c:4 * c + 4, :],
                          ps[b][:, :].rearrange("p (h c) -> p h c", h=4)[:, :, 64:128], t0)
                free[b] = [y]
                qt.append(y)
        done(i, t0)

        qrt = []
        for t in range(2):
            qv = qa[:, t, :].rearrange("p (h c) -> p h c", c=96)[:, :, 64:96]
            t1 = tmp[:, 0:256].rearrange("p (h c) -> p h c", h=8)
            t2 = tmp[:, 256:512].rearrange("p (h c) -> p h c", h=8)
            cb = C("cosA")[:, 32 * t:32 * t + 32].unsqueeze(1).to_broadcast([128, 8, 32])
            sb0 = C("sinA")[:, 32 * t:32 * t + 16].unsqueeze(1).to_broadcast([128, 8, 16])
            sb1 = C("sinA")[:, 32 * t + 16:32 * t + 32].unsqueeze(1).to_broadcast([128, 8, 16])
            a = vtt(t1, qv, cb, ALU.mult, qt, wx)
            b = vtt(t2[:, :, 0:16], qv[:, :, 16:32], sb0, ALU.mult)
            c = vtt(t2[:, :, 16:32], qv[:, :, 0:16], sb1, ALU.mult)
            r = vtt(qv, t1, t2, ALU.add, a, b, c)
            wx = [r]
            qrt.append(r)
        kt.append(qrt)
        a = axes_end(0, ws)
        b = by_head(1)
        ws = axes(1, b, a, kdt)
        for _ in gate(2, 2):
            pass
        release()
        for t in range(2):
            t0 = tp(ps[0][0:96, 128 * t:128 * t + 128], kp[:, t, :], kt, free[0], mark=(t == 1))
        y = vcopy(kaT[64:96, :, :], ps[0][64:96, 0:256].unsqueeze(1).to_broadcast([32, 8, 256]), t0)
        free[0] = [y]
        att = [y]
        for h in range(8):
            b = (4, 5, 6, 7)[h // 2]
            for t in range(2):
                c = 256 * (h % 2) + 128 * t
                t0 = tp(ps[b][0:96, c:c + 128], qa[:, t, 96 * h:96 * h + 96], kt, free[b], mark=(h % 2 == 1 and t == 1))
            if h % 2:
                y = act(qaT[0:96, h - 1:h + 1, :], ps[b][0:96, :].rearrange("p (h c) -> p h c", h=2), ACT.Copy, t0)
                free[b] = [y]
                att.append(y)

        axes_end(1, ws)
        for _ in gate(3, 3):
            pass
        release()
        for j in range(2):
            b = 1 + j
            for pr in range(2):
                for t in range(2):
                    q0 = 416 + 256 * j + 128 * pr
                    t0 = tp(ps[b][:, 256 * pr + 128 * t:256 * pr + 128 * t + 128], z[:, t, q0:q0 + 128], kdt, free[b],
                            mark=(pr == 1 and t == 1))
            y = act(qbT[:, 2 * j:2 * j + 2, :], ps[b][:, :].rearrange("p (h c) -> p h c", h=2), ACT.Copy, t0, scale=0.125)
            free[b] = [y]
            att.append(y)
        for j in range(2):
            for t in range(2):
                c = 256 * j + 128 * t
                t0 = tp(ps[3][:, c:c + 128], kd[:, t, 128 * j:128 * j + 128], kdt, free[3], mark=(j == 1 and t == 1))
        y = act(kbT[:, :, :], ps[3][:, :].rearrange("p (h c) -> p h c", h=2), ACT.Copy, t0)
        free[3] = [y]
        att.append(y)

        def head_a(h):
            return dict(q=lambda t: qaT[0:96, h, 128 * t:128 * t + 128], k=lambda n: kaT[0:96, h, 0:n],
                        v=lambda k: va[:, k, h, :])

        def head_b(h):
            lo = 64 * (h % 2)
            g = h // 4
            return dict(q=lambda t: qbT[lo:lo + 64, h // 2, 128 * t:128 * t + 128],
                        k=lambda n: kbT[lo:lo + 64, g, 0:n],
                        v=lambda k: z[:, k, 1056 + 64 * g:1120 + 64 * g])

        oh = rar(0, 2048).rearrange("p (k c) -> p k c", k=8)
        ol = rar(2048, 2048).rearrange("p (k c) -> p k c", k=8)
        ma = far(2368, 1024).rearrange("p (s c) -> p s c", s=2)
        at1 = []

        def out_half(nm, c, n, banks):
            i = take(f"{nm}{c}")
            s = i % NHL
            toks = []
            for f in range(4):
                b = banks[f // 2]
                for k in range(4):
                    a = k * 512 + f * 128
                    t0 = mm3(ps[b][:, 256 * (f % 2):256 * (f % 2) + 256], whi[:, s, a:a + 128], wlo[:, s, a:a + 128],
                             oh[:, 4 * n + k, :], ol[:, 4 * n + k, :], k == 0, k == 3, ready[i],
                             at1[4 * n:4 * n + 4], free[b], mark=(k == 3 and f % 2 == 1))
                    if (f, k) != (3, 3):
                        yield
                if f % 2:
                    toks.append(t0)
            done(i, t0, hold=True)
            out_tok[nm, c] = toks
            yield

        out_tok = {}

        def between():
            for g in range(4, 8):
                yield from gate(g, (2, 7)[g % 2], wx)
            yield from out_half("oa", 0, 0, (2, 7))

        other = between()

        def fill(n):
            release(1)
            for _ in range(n):
                next(other, None)

        attention([head_a(h) for h in range(8)] + [head_b(h) for h in range(8)], False,
                  lambda j: oh[:, j, :], lambda j: ol[:, j, :], att, qt, fill=fill, outs=at1)
        fill(200)
        release()

        last_g = (PE.sem, PE.n)
        for _ in out_half("ob", 0, 1, (0, 1)):
            pass
        mt = [[], []]

        def merge(c, ba, bb):
            for f2 in range(2):
                fs = 4 * c + 2 * f2
                g = 2 * c + f2
                m1, m2 = ma[:, 0, :], ma[:, 1, :]
                a = vstt(m1, sg[g], 1.0, ps[ba[f2]][:, :], ALU.add, ALU.mult, out_tok["oa", c][f2], gt[g], mt[0], mt[1], att, last_g)
                b = vstt(m2, sg[4 + g], 1.0, ps[bb[f2]][:, :], ALU.add, ALU.mult, out_tok["ob", c][f2], gt[4 + g])
                free[ba[f2]], free[bb[f2]] = [a], [b]
                a = vtt(m1, m1, m2, ALU.add, a, b)
                hv = hh[:, fs:fs + 2, :].rearrange("p a b -> p (a b)")
                b = act(hv, m1, ACT.Copy, a, last_g)
                mt[c].append(vtt(hl[:, fs:fs + 2, :].rearrange("p a b -> p (a b)"), m1, hv.bitcast(F), ALU.subtract, b))

        merge(0, (2, 7), (0, 1))
        release()
        for _ in out_half("oa", 1, 0, (3, 4)):
            pass
        release()
        for _ in out_half("ob", 1, 1, (5, 6)):
            pass
        merge(1, (3, 4), (5, 6))
        release()
        c0, c1 = proj_halves("o", hh, hl, mt[0], mt[1])
        J = join(c0, c1, 0.5, G("g_mlp"))

        uh = rar(0, 1536).rearrange("p (s c) -> p s c", s=3)
        ul = rar(1536, 1536).rearrange("p (s c) -> p s c", s=3)
        fr = far(0, 1024).rearrange("p (s c) -> p s c", s=2)
        fu = far(1024, 1024).rearrange("p (s c) -> p s c", s=2)
        ud, ut = {}, {}

        def u_split(g, y):
            s, s3 = g % 2, g % 3
            a = act(uh[:, s3, :], fu[:, s, :], ACT.Copy, y, ud.get(g - 3))
            ut[g] = vtt(ul[:, s3, :], fu[:, s, :], uh[:, s3, :].bitcast(F), ALU.subtract, a)

        def down(i, g, cs, first, last):
            s = i % NHL
            u2 = [a[:, g % 3, :].rearrange("p (k c) -> p k c", k=2) for a in (uh, ul)]
            w = (ready[i], ut[g], [free[b] for b in range(4)] if first else None)
            for k in range(2):
                for t in range(2):
                    tk = slice(128 * t, 128 * t + 128)
                    for c in cs:
                        a = k * 1024 + c * 512
                        tok = mm3(accs[t][c], u2[0][:, k, tk], u2[1][:, k, tk], whi[:, s, a:a + 512],
                                  wlo[:, s, a:a + 512], first and k == 0, last and k == 1, *w,
                                  mark=(k == 1 and t == 1 and c == cs[-1]))
                        w = ()
            ud[g] = tok
            return tok

        def layer_body(n, lag, open_, up, tag):
            ud.clear()
            ut.clear()
            g0 = open_()
            for g in range(n):
                if g >= g0:
                    up(g)
                if lag <= g < n - 3 + lag:
                    i = take(f"{tag}{g - lag}")
                    done(i, down(i, g - lag, (0, 1), g == lag, False))
            ii = {}

            def c0():
                for g in range(n - 3, n):
                    ii[g] = take(f"{tag}{g}")
                    tok = down(ii[g], g, (0,), False, g == n - 1)
                return tok

            def c1(g):
                def f():
                    tok = down(ii[g], g, (1,), False, g == n - 1)
                    done(ii[g], tok, hold=(g == n - 1))
                    return tok
                return f

            return c0, [c1(g) for g in range(n - 3, n)]

        def up1_end(g, t0, now, rbt):
            b = 4 + g % 4
            s = g % 2
            y = vstt(two(fr[:, s, :]), two(ps[b][:, :]), 0.0, rbc, ALU.max, ALU.mult, t0, now, rbt, ut.get(g - 2))
            free[b] = [y]
            u_split(g, act(fu[:, s, :], fr[:, s, :], ACT.Square, y, ut.get(g - 2)))

        def mlp(J):
            now = all_now()
            rbt = None

            def open_():
                nonlocal rbt
                ta, tb, rbt = opening(("up0", "up1"), (4, 5), J)
                up1_end(0, ta, now, rbt)
                release(2)
                up1_end(1, tb, now, rbt)
                release()
                return 2

            def up(g):
                b = 4 + g % 4
                t0 = gemm_b(f"up{g}", hh, hl, 8, 256, [ps[b][:, 0:256], ps[b][:, 256:512]], free[b], hold=True)
                up1_end(g, t0, now, rbt)
                release()

            return layer_body(16, 2, open_, up, "dn")

        now = all_now()
        pf = far(2048, 512).rearrange("p (k c) -> p k c", k=2)
        pd = PO.dma(pf, PT_IN.rearrange("(k p) c -> p k c", p=128), s_misc, 16, now)
        gf = far(4096, 1024)
        gfd = PO.dma(gf, GFIN.partition_broadcast(128), s_gf, 16, now)
        ph = rar(3072, 512).rearrange("p (k c) -> p k c", k=2)
        pl = rar(3584, 512).rearrange("p (k c) -> p k c", k=2)
        c0, c1 = mlp(J)
        a = act(ph, pf, ACT.Copy, pd)
        pt0 = vtt(pl, pf, ph.bitcast(F), ALU.subtract, a)
        J = join(c0, c1, 1.0, G("g_ple"))

        now = all_now()
        gs = far(0, 2048).rearrange("p (t d) -> p t d", t=2)
        q = 128 + 16 * (joins[0] % 4)
        joins[0] += 1
        PG = [[4, 6], [5, 7]]

        def pg(c, part, *w):
            o = [[ps[PG[t][c]][:, :]] for t in range(2)]
            return gemm_a(f"pg{c}.{part}", hh, hl, range(4 * part, 4 * part + 4), 512, o, part == 0, part == 1, *w,
                          [free[PG[t][c]] for t in range(2)] if part == 0 else None, hold=(part == 1))

        pg(0, 0, J["n0"])
        n1, _ = J["second"]()
        pg(1, 0)
        t0 = gemm_a("ple", ph, pl, range(2), 1024, accs, True, True, pt0, [free[b] for b in range(4)])
        tg = [pg(0, 1, n1)]
        Y = far(5120, 2048).rearrange("p (t d) -> p t d", t=2)
        rh2 = st[:, q + 12:q + 14]
        half = vts(rh2, J["r"], 0.5, None, ALU.mult, None, J["rtok"])

        def ple_half(c, tg):
            xt, yt = [], []
            sl = slice(512 * c, 512 * c + 512)
            sg = []
            for t in range(2):
                sg.append(act(gs[:, t, sl], ps[PG[t][c]][:, :], ACT.Tanh, tg, now, half, scale=rh2[:, t:t + 1]))
                free[PG[t][c]] = [sg[t]]
            for t in range(2):
                y = vstt(gs[:, t, sl], gs[:, t, sl], 1.0, ps[ACC[t][c]][:, :], ALU.add, ALU.mult, sg[t], t0)
                free[ACC[t][c]] = [y]
                xt.append(vstt(X[:, t, sl], gs[:, t, sl], 0.5, X[:, t, sl], ALU.mult, ALU.add, y, J["x"], n1))
                yt.append(vtt(Y[:, t, sl], X[:, t, sl], gf[:, sl], ALU.mult, xt[t], gfd, now))
            return xt, yt

        def ple_squares(c, xt, yt):
            out = square_half(q, c, xt)
            for t in range(2):
                sl = slice(c * 512, (c + 1) * 512)
                junk[t, c] = act(xn[:, t, sl], Y[:, t, sl], ACT.Square, yt[t], junk[t, c],
                                 accum=st[:, q + 8 + 2 * c + t:q + 8 + 2 * c + t + 1])
                out.append(junk[t, c])
            return out

        xt0, yt0 = ple_half(0, tg)
        tok = pg(1, 1)
        n0 = turn_half(0, G("n00"), yt0, Y)
        release(2)
        sq = ple_squares(0, xt0, yt0)
        xt1, yt1 = ple_half(1, tok)
        sq += ple_squares(1, xt1, yt1)
        r1, r12 = st[:, q + 6:q + 8], st[:, q + 14:q + 16]
        r1t = rms_inv(r1, q, sq)
        a = vtt(st[:, q + 4:q + 6], r1, r1, ALU.mult, r1t)
        m = vtt(st[:, q + 12:q + 14], st[:, q + 8:q + 10], st[:, q + 10:q + 12], ALU.add, sq)
        m = vtt(st[:, q + 12:q + 14], st[:, q + 12:q + 14], st[:, q + 4:q + 6], ALU.mult, a, m)
        m = vts(st[:, q + 12:q + 14], st[:, q + 12:q + 14], 1.0 / D, EPS, ALU.mult, ALU.add, m)
        m = ppow(r12, st[:, q + 12:q + 14], 2, m)
        m = vtt(r12, r12, r1, ALU.mult, m)

        def second():
            n1 = turn_half(1, G("n00"), yt1, Y)
            dg = diagonal(r12, m)
            release()
            return n1, dg

        xs = []

        def late():
            for t in range(2):
                xs.append(vts(X[:, t, :], Y[:, t, :], r1[:, t:t + 1], None, ALU.mult, None, r1t, yt0, yt1, sq))

        J = dict(n0=n0, second=second, r=r12, rtok=m, late=late)

        def swiglu(layer, half, J):
            now = all_now()
            rbt = None
            a, b = f"fa{layer}{half}.", f"fb{layer}{half}."

            def end_a(g, ta):
                s = g % 2
                bk = 4 + 2 * s
                y = vtt(two(fr[:, s, :]), two(ps[bk][:, :]), rbc, ALU.mult, ta, rbt, now, ut.get(g - 2))
                free[bk] = [y]
                return act(fr[:, s, :], fr[:, s, :], ACT.Silu, y)

            def end_b(g, ya, tb):
                s = g % 2
                bk = 5 + 2 * s
                y = vtt(two(fu[:, s, :]), two(ps[bk][:, :]), rbc, ALU.mult, tb, rbt, now, ut.get(g - 2))
                free[bk] = [y]
                u_split(g, vtt(fu[:, s, :], fu[:, s, :], fr[:, s, :], ALU.mult, y, ya))

            def open_():
                nonlocal rbt
                ta, tb, rbt = opening((a + "0", b + "0"), (4, 5), J)
                ya = end_a(0, ta)
                release(2)
                end_b(0, ya, tb)
                release()
                return 1

            def up(g):
                bk = 4 + 2 * (g % 2)
                o = [[ps[bk + j][:, 0:256], ps[bk + j][:, 256:512]] for j in range(2)]
                ya = end_a(g, gemm_b(f"{a}{g}", hh, hl, 8, 256, o[0], free[bk], hold=True))
                release()
                end_b(g, ya, gemm_b(f"{b}{g}", hh, hl, 8, 256, o[1], free[bk + 1], hold=True))
                release()

            return layer_body(11, 1, open_, up, f"fd{layer}{half}.")

        c0, c1 = swiglu(0, 0, J)

        def plain_join(c0, c1, scale, *w):
            xr = add_half(0, scale, [c0(), *w])
            for f in c1:
                tok = f()
            xr += add_half(1, scale, tok)
            release()
            return xr

        xr = plain_join(c0, c1, 0.5, xs)

        nm = norm_t(lambda t: X[:, t, :], D, G("n01"), hh, hl, xr, (PE.sem, PE.n), banks=(4, 5, 6, 7))
        now = all_now()
        sm_ = far(0, 48).rearrange("p (t c) -> p t c", t=2)
        glT = fa[0:17, 48:304]
        gk = far(304, 512).rearrange("p (t c) -> p t c", t=2)
        ga, ge = far(816, 512), far(1328, 512)
        lf = far(1840, 16).rearrange("p (t c) -> p t c", t=2)
        la, lb = far(1856, 16), far(1872, 16)
        vg = far(1888, 1024).rearrange("p (t c) -> p t c", t=2)
        go = far(2912, 1024)
        GT = far(3936, 512).rearrange("p (r c) -> p r c", r=2)
        eG = far(4448, 512).rearrange("p (r c) -> p r c", r=2)
        enG = far(4960, 512).rearrange("p (r c) -> p r c", r=2)
        eE = far(5472, 512).rearrange("p (r c) -> p r c", r=2)
        qd = far(5984, 512).rearrange("p (r c) -> p r c", r=2)
        kdc = far(6496, 512).rearrange("p (r c) -> p r c", r=2)
        ke = far(7008, 512).rearrange("p (r c) -> p r c", r=2)
        ktk = far(7520, 512).rearrange("p (r t c) -> p r t c", r=2, t=2)
        AT = far(8032, 1024).rearrange("p (s r t c) -> p s r t c", s=2, r=2, t=2)
        sts = far(9056, 1536).rearrange("p (n r c) -> p n r c", n=3, r=2)
        nFT = fa[0:8, 10592:10848]
        Ft = far(10848, 16).rearrange("p (t c) -> p t c", t=2)
        mh = rar(0, 2048).rearrange("p (k c) -> p k c", k=8)
        ml = rar(2048, 2048).rearrange("p (k c) -> p k c", k=8)

        t0 = gemm_a("small", hh, hl, range(8), 24, [[ps[0][:, 0:24]], [ps[1][:, 0:24]]], True, True, nm, free[0], free[1])
        sy = []
        for t in range(2):
            y = act(sm_[:, t, :], ps[t][:, 0:24], ACT.Copy, t0, now)
            free[t] = [y]
            sy.append(y)
        g1 = vset(glT, 1.0, now)
        for t in range(2):
            t0 = tp(ps[2][0:16, 128 * t:128 * t + 128], sm_[:, t, 0:16], sy, free[2], mark=(t == 1))
        g1 = vcopy(glT[0:16, :], ps[2][0:16, 0:256], t0, g1)
        free[2] = [g1]
        for t in range(2):
            t0 = mm(ps[3][:, 256 * t:256 * t + 256], glT[:, 128 * t:128 * t + 128], gw[:, :], True, True, g1, IN, free[3],
                    mark=(t == 1))

        def log_sigmoid(o, x, a, b, t):
            y = act(a, x, ACT.Abs, t)
            y = act(b, a, ACT.Exp, y, scale=-1.0)
            y = act(a, b, ACT.Ln, y, bias=C("ones")[:, 0:1])
            return vstt(o, x, 0.0, a, ALU.min, ALU.subtract, y)

        fx = [vtt(sm_[:, t, 16:24], sm_[:, t, 16:24], fb8[:, :], ALU.add, sy, IN) for t in range(2)]
        lg = log_sigmoid(gk.rearrange("p t c -> p (t c)"), ps[3][:, :], ga, ge, t0)
        free[3] = [lg]
        la3 = la.rearrange("p (t c) -> p t c", t=2)
        lb3 = lb.rearrange("p (t c) -> p t c", t=2)
        lff = log_sigmoid(lf, sm_[:, :, 16:24], la3, lb3, fx)

        t0 = wide_a("vg", hh, hl, (4, 5))
        vt = []
        for t in range(2):
            y = act(vg[:, t, :], ps[4 + t][:, :], ACT.Copy, t0, now)
            free[4 + t] = [y]
            vt.append(y)
        for g in range(2):
            t0 = gemm_b(f"go{g}", hh, hl, 8, 256, [ps[6 + g][:, 0:256], ps[6 + g][:, 256:512]], free[6 + g])
            y = act(go[:, 512 * g:512 * g + 512], ps[6 + g][:, :], ACT.Silu, t0, now)
            free[6 + g] = [y]
            vt.append(y)
        for p in range(2):
            for t in range(2):
                t0 = mm(ps[2][:, 256 * p + 128 * t:256 * p + 128 * t + 128], gk[:, t, 128 * p:128 * p + 128], C("tri64"),
                        True, True, lg, free[2], mark=(p == 1 and t == 1))
        y = vcopy(GT, ps[2][:, :].rearrange("p (r c) -> p r c", r=2), t0)
        free[2] = [y]
        e1 = act(eG, GT, ACT.Exp, y)
        e2 = act(enG, GT, ACT.Exp, y, scale=-1.0)
        for p in range(2):
            for c in range(4):
                e3 = act(eE[:, p, 64 * c:64 * c + 64], GT[:, p, 64 * c:64 * c + 64], ACT.Exp, y, scale=-1.0,
                         bias=GT[:, p, 64 * c + 63:64 * c + 64])
        t0 = gemm_b("qg", hh, hl, 8, 256, [ps[0][:, 0:256], ps[0][:, 256:512]], free[0])
        yq = vstt(qd.rearrange("p r c -> p (r c)"), ps[0][:, :], 0.125, eG.rearrange("p r c -> p (r c)"),
                  ALU.mult, ALU.mult, t0, e1)
        free[0] = [yq]
        t0 = gemm_b("kg", hh, hl, 8, 256, [ps[1][:, 0:256], ps[1][:, 256:512]], free[1])
        yk = vtt(kdc.rearrange("p r c -> p (r c)"), ps[1][:, :], enG.rearrange("p r c -> p (r c)"), ALU.mult, t0, e2)
        ye = vtt(ke.rearrange("p r c -> p (r c)"), ps[1][:, :], eE.rearrange("p r c -> p (r c)"), ALU.mult, e3)
        free[1] = [ye]

        mm(ps[3][0:8, 0:256], lf[:, 0, :], cst[:, CONST["tri"][0]:CONST["tri"][0] + 256], True, False, lff, free[3])
        t0 = mm(ps[3][0:8, 128:256], lf[:, 1, :], C("tri"), False, True, mark=True)
        yf = vts(nFT, ps[3][0:8, 0:256], -1.0, None, ALU.mult, None, t0)
        free[3] = [yf]
        mm(ps[3][:, 0:8], C("tri"), lf[:, 0, :], True, True, free[3])
        mm(ps[3][:, 8:16], C("ones"), lf[:, 0, :], True, False)
        t0 = mm(ps[3][:, 8:16], C("tri"), lf[:, 1, :], False, True, mark=True)
        yF = vcopy(Ft, ps[3][:, 0:16].rearrange("p (t c) -> p t c", t=2), t0)
        free[3] = [yF]

        for p in range(2):
            for t in range(2):
                for par in range(2):
                    r0 = 64 * par
                    tk = slice(128 * t, 128 * t + 128)
                    c = 256 * p + 128 * t
                    t0 = mm(ps[4 + par][:, c:c + 128], kdc[r0:r0 + 64, p, tk], qd[r0:r0 + 64, p, tk], True, True, yq, yk,
                            free[4 + par], mark=True)
        m64 = C("m64").unsqueeze(1).to_broadcast([128, 4, 128])
        ya = []
        for par in range(2):
            y = vtt(AT[:, par].rearrange("p r t c -> p (r t) c"), ps[4 + par][:, :].rearrange("p (g c) -> p g c", g=4), m64,
                    ALU.mult, t0)
            free[4 + par] = [y]
            ya.append(y)
        for p in range(2):
            for t in range(2):
                c = 256 * p + 128 * t
                t0 = tp(ps[6][:, c:c + 128], ke[:, p, 128 * t:128 * t + 128], ye, free[6], mark=(p == 1 and t == 1))
        y = act(ktk, ps[6][:, :].rearrange("p (r t c) -> p r t c", r=2, t=2), ACT.Copy, t0)
        free[6] = [y]
        kb = (7, 0, 1)
        for c in range(3):
            t, r0 = c // 2, 64 * (c % 2)
            for p in range(2):
                t0 = mm(ps[kb[c]][:, 256 * p:256 * p + 256], ktk[r0:r0 + 64, p, t, :], vg[r0:r0 + 64, t, 256 * p:256 * p + 256],
                        True, True, y, vt, free[kb[c]], mark=(p == 1))
            if c == 0:
                ys = vcopy(sts[:, 0].rearrange("p r c -> p (r c)"), ps[kb[0]][:, :], t0)
            else:
                for p in range(2):
                    ys = vstt(sts[:, c, p, :], sts[:, c - 1, p, :], eG[:, p, 64 * c + 63:64 * c + 64],
                              ps[kb[c]][:, 256 * p:256 * p + 256], ALU.mult, ALU.add, t0, ys)
            free[kb[c]] = [ys]
        gm = []
        og, ov = xnf[:, 0:1024].rearrange("p (s c) -> p s c", s=2), xnf[:, 1024:2048].rearrange("p (s c) -> p s c", s=2)
        gov = go.rearrange("p (r s c) -> p s r c", r=2, s=2)
        mhv, mlv = (a[:, 0:4, :].rearrange("p (r s) c -> p s r c", s=2) for a in (mh, ml))
        for par in range(2):
            b = 2 + par
            r0 = 64 * par
            for p in range(2):
                h = 2 * p + par
                for t in range(2):
                    o = ps[b][:, 256 * p + 128 * t:256 * p + 128 * t + 128]
                    mm(o, vg[:, t, 128 * h:128 * h + 128], AT[:, par, p, t, :], True, False, ya, vt, free[b])
                    for c in range(2 * t, 2 * t + 2):
                        if c >= 1:
                            t0 = mm(o[:, 64 * (c % 2):64 * (c % 2) + 64], sts[r0:r0 + 64, c - 1, p, 128 * par:128 * par + 128],
                                    qd[r0:r0 + 64, p, 64 * c:64 * c + 64], False, True, ys,
                                    mark=(p == 1 and c == 3))
            y = act(og[:, par, :], ps[b][:, :], ACT.Square, t0)
            tq = mm(ps[4 + par][:, :], C("ones"), og[:, par, :], True, True, y, free[4 + par], mark=True)
            y = vts(ov[:, par, :], ps[4 + par][:, :], 1.0 / 128, EPS, ALU.mult, ALU.add, tq)
            free[4 + par] = [y]
            y = act(ov[:, par, :], ov[:, par, :], ACT.Ln, y)
            y = act(ov[:, par, :], ov[:, par, :], ACT.Exp, y, scale=-0.5)
            y = vstt(ov[:, par, :], ps[b][:, :], G("g_gla")[:, 0:1], ov[:, par, :], ALU.mult, ALU.mult, y)
            free[b] = [y]
            o2 = ov[:, par, :].rearrange("p (r c) -> p r c", r=2)
            y = vtt(o2, o2, gov[:, par], ALU.mult, y, vt)
            a = act(mhv[:, par], o2, ACT.Copy, y, now)
            gm.append(vtt(mlv[:, par], o2, mhv[:, par].bitcast(F), ALU.subtract, a))

        now = all_now()
        qf = far(0, 1024).rearrange("p (k c) -> p k c", k=4)
        kf = far(1024, 1024).rearrange("p (k c) -> p k c", k=4)
        vf = far(2048, 1024).rearrange("p (t c) -> p t c", t=2)
        ft = [now]
        for n, (nme, dst, sc) in enumerate((("qf", qf, 0.125), ("kf", kf, 1.0))):
            for g in range(2):
                b = 2 * n + g
                t0 = gemm_b(f"{nme}{g}", hh, hl, 8, 256, [ps[b][:, 0:256], ps[b][:, 256:512]], free[b])
                y = act(dst[:, 2 * g:2 * g + 2, :], ps[b][:, :].rearrange("p (h c) -> p h c", h=2), ACT.Copy, t0, now,
                        scale=sc)
                free[b] = [y]
                ft.append(y)
        t0 = wide_a("vf", hh, hl, (4, 5))
        for t in range(2):
            y = act(vf[:, t, :], ps[4 + t][:, :], ACT.Copy, t0, now)
            free[4 + t] = [y]
            ft.append(y)
        cm = C("cm")

        def head_f(h):
            lo = 64 * (h % 2)

            def ev(bank, src, t, w):
                vstt(src[:, 0:128], bank[:, 0:128], Ft[:, 0, h:h + 1], cm[:, 128:256], ALU.add, ALU.add, t, w)
                return vstt(src[:, 128:384], bank[:, 128:384], Ft[:, 1, h:h + 1], cm, ALU.add, ALU.add)

            return dict(q=lambda t: qf[lo:lo + 64, h // 2, 128 * t:128 * t + 128],
                        k=lambda n: kf[lo:lo + 64, h // 2, 0:n],
                        v=lambda k: vf[:, k, 64 * h:64 * h + 64],
                        more=lambda t: (C("sel", 8)[:, 128 * h:128 * h + 128], nFT[:, 0:128 + 128 * t]), ev=ev)

        at2 = attention([head_f(h) for h in range(8)], True, lambda j: mh[:, 4 + j, :], lambda j: ml[:, 4 + j, :], ft)
        c0, c1 = proj_halves("eo", mh, ml, gm, at2)
        J = join(c0, c1, 1.0, G("n02"))
        c0, c1 = swiglu(0, 1, J)
        J = join(c0, c1, 0.5, G("n10"))
        c0, c1 = swiglu(1, 0, J)
        xr = plain_join(c0, c1, 0.5)

        nm = norm_t(lambda t: X[:, t, :], D, G("n11"), hh, hl, xr, (PE.sem, PE.n), banks=(4, 5, 6, 7))
        now = all_now()
        qT = far(0, 2048).rearrange("p (k c) -> p k c", k=8)
        kT = far(2048, 2048).rearrange("p (k c) -> p k c", k=8)
        vv = far(4096, 2048).rearrange("p (t c) -> p t c", t=2)
        ck = far(6144, 512).rearrange("p (t c) -> p t c", t=2)
        qiT = far(6656, 1024).rearrange("p (k c) -> p k c", k=4)
        kiT = far(7680, 256)
        ki = far(7936, 256).rearrange("p (t c) -> p t c", t=2)
        wi = far(8192, 16).rearrange("p (t c) -> p t c", t=2)
        acc = far(8208, 384)
        wk = far(8592, 384)
        msk = far(8976, 384)
        rl = far(9360, 1024).rearrange("p (s c) -> p s c", s=2)
        top = [st[:, 200 + 8 * t:208 + 8 * t] for t in range(2)]
        bring = far(9360, 768).rearrange("p (s c) -> p s c", s=3)
        bsum = far(10128, 1152).rearrange("p (s c) -> p s c", s=3)

        t0 = mm(ps[0][0:16, :], t5s[:, :], C("hot", 32), True, True, IN, free[0], mark=True)
        y = vcopy(fa[0:16, 10592:11104], ps[0][0:16, :], t0, now)
        free[0] = [y]
        t5w = PO.dma(scratch.ap(), fa[0:16, 10592:11104], s_t5w, 16, [y])

        t0 = gemm_a("ckv", hh, hl, range(8), 256, [[ps[1][:, 0:256]], [ps[2][:, 0:256]]], True, True, nm, free[1], free[2])
        cy = []
        for t in range(2):
            y = act(ck[:, t, :], ps[1 + t][:, 0:256], ACT.Copy, t0, now)
            free[1 + t] = [y]
            cy.append(y)
        t0 = gemm_a("kwi", hh, hl, range(8), 72, [[ps[3][:, 0:72]], [ps[0][:, 0:72]]], True, True, free[3], free[0])
        wy = []
        for t, b in enumerate((3, 0)):
            for d in range(2):
                y = act(ki[:, t, 64 * d:64 * d + 64], ps[b][:, 0:64], ACT.Copy, t0, now)
            y = act(wi[:, t, :], ps[b][:, 64:72], ACT.Copy, t0, now, scale=float(np.float32(8 ** -0.5)))
            free[b] = [y]
            wy.append(y)
        qy = []
        for g in range(2):
            t0 = gemm_b(f"qi{g}", hh, hl, 8, 256, [ps[1 + g][:, 0:256], ps[1 + g][:, 256:512]], free[1 + g])
            y = act(qiT[:, 2 * g:2 * g + 2, :], ps[1 + g][:, :].rearrange("p (h c) -> p h c", h=2), ACT.Copy, t0, now,
                    scale=0.125)
            free[1 + g] = [y]
            qy.append(y)
        for t in range(2):
            t0 = tp(ps[3][:, 128 * t:128 * t + 128], ki[:, t, :], wy, free[3], mark=(t == 1))
        y = act(kiT, ps[3][:, 0:256], ACT.Copy, t0, now)
        free[3] = [y]
        qy.append(y)
        ch = rar(0, 512).rearrange("p (k c) -> p k c", k=2)
        cl = rar(512, 512).rearrange("p (k c) -> p k c", k=2)
        nc_ = norm_t(lambda t: ck[:, t, :], 256, G("g_ckv"), ch, cl, cy, now, banks=(4,))

        OFF, KL = (0, 128), (128, 256)
        av, rt = None, {}

        def index_head(h):
            nonlocal av
            b = 5 + h % 3
            lo = 64 * (h % 2)
            for t in range(2):
                t0 = mm(ps[b][:, OFF[t]:OFF[t] + KL[t]], qiT[lo:lo + 64, h // 2, 128 * t:128 * t + 128],
                        kiT[lo:lo + 64, 0:KL[t]], True, True, qy, free[b], mark=(t == 1))
            s = h % 2
            y = act(rl[:, s, 0:384], ps[b][:, 0:384], ACT.Relu, t0, now, rt.get(h - 2))
            free[b] = [y]
            for t in range(2):
                a = acc[:, OFF[t]:OFF[t] + KL[t]]
                r = rl[:, s, OFF[t]:OFF[t] + KL[t]]
                if h == 0:
                    av = vts(a, r, wi[:, t, h:h + 1], None, ALU.mult, None, y, wy, now)
                else:
                    av = vstt(a, r, wi[:, t, h:h + 1], a, ALU.mult, ALU.add, y, av)
            rt[h] = av

        for h in range(8):
            index_head(h)
        a = [vtt(wk[:, 0:128], acc[:, 0:128], cm[:, 128:256], ALU.add, av, now),
             vtt(wk[:, 128:384], acc[:, 128:384], cm, ALU.add)]
        for r in range(8):
            for t in range(2):
                w_ = wk[:, OFF[t]:OFF[t] + KL[t]]
                a[t] = VE.add(lambda e, w_=w_, t=t: e.max(top[t], w_), [a[t]])
            for t in range(2):
                w_ = wk[:, OFF[t]:OFF[t] + KL[t]]
                a[t] = VE.add(lambda e, w_=w_, t=t: e.match_replace(w_, top[t], w_, GONE), [a[t]])
        y = vts(msk, wk, GONE, 1.0, ALU.is_equal, ALU.subtract, a)
        y = vts(msk, msk, -NEG, None, ALU.mult, None, y)
        y1 = vtt(msk[:, 0:128], msk[:, 0:128], cm[:, 128:256], ALU.add, y)
        y2 = vtt(msk[:, 128:384], msk[:, 128:384], cm, ALU.add, y)
        mk = [y1, y2]

        dt = [now]
        for g in range(4):
            b = g
            t0 = gemm_b(f"q{g}", hh, hl, 8, 256, [ps[b][:, 0:256], ps[b][:, 256:512]], free[b])
            y = act(qT[:, 2 * g:2 * g + 2, :], ps[b][:, :].rearrange("p (h c) -> p h c", h=2), ACT.Copy, t0, now, scale=0.125)
            free[b] = [y]
            dt.append(y)
        i = take("uk")
        s = i % NHL
        for f in range(8):
            b = 4 + f // 2
            for k in range(2):
                a = k * 1024 + f * 128
                t0 = mm3(ps[b][:, 256 * (f % 2):256 * (f % 2) + 256], whi[:, s, a:a + 128], wlo[:, s, a:a + 128],
                         ch[:, k, :], cl[:, k, :], k == 0, k == 1, ready[i], nc_, free[b], mark=(k == 1 and f % 2 == 1))
            if f % 2:
                y = act(kT[:, f - 1:f + 1, :], ps[b][:, :].rearrange("p (h c) -> p h c", h=2), ACT.Copy, t0, now)
                free[b] = [y]
                dt.append(y)
        done(i, t0)
        t0 = gemm_a("uv", ch, cl, range(2), 1024, accs, True, True, [free[b] for b in range(4)])
        for t in range(2):
            for c in range(2):
                b = ACC[t][c]
                y = act(vv[:, t, 512 * c:512 * c + 512], ps[b][:, :], ACT.Copy, t0, now)
                free[b] = [y]
                dt.append(y)
        uvt = t0

        ba, bu = {}, {}
        sapp = scratch.ap()

        def bias_load(h):
            k = h % 3
            src = bass.AP(sapp.tensor, 512 * h + 128, [[1, 128], [1, 256]])
            tk = PO.dma(bring[:, k, :], src, s_bias[k], 16 * (h // 3 + 1), [t5w, ba.get(h - 3), mk, uvt])
            for t in range(2):
                at0 = bring[:, k, KL[t] - 1:KL[t]]
                back = bass.AP(at0.tensor, at0.offset, [list(at0.ap[0]), [-1, KL[t]]])
                o, m_ = bsum[:, k, OFF[t]:OFF[t] + KL[t]], msk[:, OFF[t]:OFF[t] + KL[t]]
                ba[h] = PO.add(lambda e, o=o, back=back, m_=m_: e.tensor_tensor(o, back, m_, ALU.add),
                               [tk, mk, bu.get(h - 3)])

        def head_d(h):
            lo = 64 * (h % 2)

            def ev(bank, src, t, w):
                bu[h] = vtt(src, bank[:, 0:384], bsum[:, h % 3, :], ALU.add, t, w, ba[h])
                if h + 3 < 16:
                    bias_load(h + 3)
                return bu[h]

            return dict(q=lambda t: qT[lo:lo + 64, h // 2, 128 * t:128 * t + 128],
                        k=lambda n: kT[lo:lo + 64, h // 2, 0:n],
                        v=lambda k: vv[:, k, 64 * h:64 * h + 64], ev=ev)

        for h in range(3):
            bias_load(h)
        at3 = attention([head_d(h) for h in range(16)], True, lambda j: mh[:, j, :], lambda j: ml[:, j, :], dt, uvt)
        c0, c1 = proj_halves("oo", mh, ml, at3, at3)
        J = join(c0, c1, 1.0, G("n12"))
        c0, c1 = swiglu(1, 1, J)
        gfd = PO.dma(gf, GFIN2.partition_broadcast(128), s_gf, 32, all_now())
        q = 128 + 16 * (joins[0] % 4)
        rt0 = add_half(0, 0.5, c0())
        sq = square_half(q, 0, rt0)
        for f in c1:
            tok = f()
        rt1 = add_half(1, 0.5, tok)
        sq += square_half(q, 1, rt1)
        r = st[:, q + 6:q + 8]
        rt = rms_inv(r, q, sq)
        ov = OUT.rearrange("(t p) d -> p t d", p=128)
        for t in range(2):
            y = vstt(X[:, t, :], X[:, t, :], r[:, t:t + 1], gf, ALU.mult, ALU.mult, rt, gfd)
            out = SP.dma(ov[:, t, :], X[:, t, :], s_out, 16 * t + 16, [y])
        assert at[0] == len(P)

        block = ctx.enter_context(nc.Block())

        @block.sync
        def _(e):
            SP.play(e)
            e.wait_ge(*out)
            e.wait_ge(*t5w)

        @block.tensor
        def _(e):
            PE.play(e)

        @block.scalar
        def _(e):
            AC.play(e)

        @block.vector
        def _(e):
            VE.play(e)

        @block.gpsimd
        def _(e):
            PO.play(e)


def layout(inputs):
    a = {k: np.asarray(v) for k, v in inputs.items()}
    w = {n: a[n][0] for n in ("w_in", "w_qb", "w_kvb", "w_oa", "w_ob", "w_o", "w_up", "w_down", "w_ple_gate", "w_ple")}
    for layer in range(2):
        for half in range(2):
            w[f"ffn_in{layer}{half}"] = a["ffn_w_in_2"][layer, half]
            w[f"ffn_out{layer}{half}"] = a["ffn_w_out_2"][layer, half]
    w["even_in"], w["even_out"] = a["even_w_in_2"][0], a["even_w_out_2"][0]
    w["odd_in"], w["odd_out"] = a["odd_w_in_2"][0], a["odd_w_out_2"][0]
    w["w_ukT"] = a["mla_w_uk_2"][0].transpose(2, 0, 1).reshape(256, 1024)
    w["w_uv"] = a["mla_w_uv_2"][0].transpose(1, 0, 2).reshape(256, 1024)
    P = plan()
    W = np.zeros((len(P), 128, CW), np.float32)
    for i, (_, pieces) in enumerate(P):
        c = 0
        for name, r0, c0, n in pieces:
            W[i, :, c:c + n] = w[name][r0:r0 + 128, c0:c0 + n]
            c += n

    gains = np.zeros((128, NGAIN), np.float32)
    ng = a["norm_g_2"]
    for name, g in dict(g_mix=a["g_mix"][0], g_qa=a["g_qa"][0], g_kva=a["g_kva"][0], g_mlp=a["g_mlp"][0],
                        g_ple=a["g_ple"][0], n00=ng[0, 0], n01=ng[0, 1], n02=ng[0, 2], n10=ng[1, 0], n11=ng[1, 1],
                        n12=ng[1, 2], g_gla=a["gla_norm_g_2"][0], g_ckv=a["mla_kv_norm_g_2"][0]).items():
        o, n = GAIN[name]
        gains[:, o:o + n] = g.reshape(n, 128).T
    return {
        "w_chunks": W,
        "x_in": np.ascontiguousarray(a["x"][0]),
        "p_t": np.ascontiguousarray(a["p"][0, 0].T),
        "consts": constants(),
        "gains": gains,
        "g_qk": np.concatenate([np.tile(a["g_qn"][0], 8), np.tile(a["g_kn"][0], 2)]),
        "g_fin": np.ascontiguousarray(a["g_final"]),
        "g_fin2": np.ascontiguousarray(a["final_norm_g_2"]),
        "gla_gate": np.concatenate([a["gla_w_gate_2"][0], a["gla_b_gate_2"]], 0),
        "fox_b": np.ascontiguousarray(a["fox_b_f_2"][0]),
        "t5": np.ascontiguousarray(a["t5_table_2"]),
    }


def kernel(**inputs):
    import concourse.bacc as _bacc
    from concourse.bass_utils import run_bass_kernel_spmd as _run

    nc = _bacc.Bacc("TRN2", target_bir_lowering=False, num_devices=1)
    arrays = layout(inputs)
    args = [nc.dram_tensor(n, a.shape, mybir.dt.from_np(a.dtype), kind="ExternalInput").ap() for n, a in arrays.items()]
    args.append(nc.dram_tensor("out_dram", (S, D), F, kind="ExternalOutput").ap())
    program(nc, *args)
    r = _run(nc, [arrays], core_ids=[0])
    return r.results[0]["out_dram"].reshape(1, S, D)
```

```python
from contextlib import ExitStack

import concourse.bass as bass
from concourse import mybir
import numpy as np

F = mybir.dt.float32
R = mybir.dt.float32r
ACT = mybir.ActivationFunctionType
ALU = mybir.AluOpType
AX = mybir.AxisListType

S = 256
D = 1024
CW = 2048
NRAW = 5
HW = 1024
NHL = 4
EPS = 1e-6
NEG = -1e30
GONE = -3e38
H2 = 2816



def plan():
    out = []

    def cols(tag, w, k, c0, n, kts=None):
        out.append((tag, [(w, 128 * t, c0, n) for t in (kts or range(k))]))

    def wide(tag, w, c0):
        for part in range(2):
            cols(f"{tag}.{part}", w, 8, c0, 512, range(4 * part, 4 * part + 4))

    def halves(*tags, parts=(0, 1)):
        for part in parts:
            for tag, w, c0 in tags:
                cols(f"{tag}.{part}", w, 8, c0, 512, range(4 * part, 4 * part + 4))

    def grouped(n, lag, ups, tag, w):
        for g in range(n):
            for u, src, c0 in ups:
                cols(f"{u}{g}", src, 8, c0 + 256 * g, 256)
            if lag <= g < n - 3 + lag:
                cols(f"{tag}{g - lag}", w, 0, 0, 1024, (2 * (g - lag), 2 * (g - lag) + 1))
        for g in range(n - 3, n):
            cols(f"{tag}{g}", w, 0, 0, 1024, (2 * g, 2 * g + 1))

    def gates(*gs):
        for g in gs:
            cols(f"gate{g}", "w_in", 8, 1184 + 256 * g, 256)

    halves(("z0", "w_in", 0), ("z1", "w_in", 512))
    cols("z2", "w_in", 8, 1024, 160)
    gates(0, 1)
    cols("wqb", "w_qb", 2, 0, 768)
    cols("wkvb", "w_kvb", 1, 0, 1024)
    gates(2, 3, 4, 5, 6, 7)
    for c in range(2):
        cols(f"oa{c}", "w_oa", 4, 512 * c, 512)
        cols(f"ob{c}", "w_ob", 4, 512 * c, 512)
    halves(("o0", "w_o", 0), ("o1", "w_o", 512))
    grouped(16, 2, [("up", "w_up", 0)], "dn", "w_down")
    cols("pg0.0", "w_ple_gate", 0, 0, 512, range(4))
    cols("pg1.0", "w_ple_gate", 0, 512, 512, range(4))
    cols("pg0.1", "w_ple_gate", 0, 0, 512, range(4, 8))
    cols("pg1.1", "w_ple_gate", 0, 512, 512, range(4, 8))
    cols("ple", "w_ple", 2, 0, 1024)

    def ffn(layer, half):
        a, b = f"ffn_in{layer}{half}", f"ffn_out{layer}{half}"
        grouped(11, 1, [(f"fa{layer}{half}.", a, 0), (f"fb{layer}{half}.", a, H2)], f"fd{layer}{half}.", b)

    ffn(0, 0)
    cols("vg.0", "even_in", 0, 512, 512, range(4))
    cols("qf0", "even_in", 8, 1552, 256)
    cols("vg.1", "even_in", 0, 512, 512, range(4, 8))
    out.append(("small", [("even_in", 128 * t, c, n) for t in range(8) for c, n in ((1536, 32), (3088, 8))]))
    cols("qf1", "even_in", 8, 1808, 256)
    cols("kf0", "even_in", 8, 2064, 256)
    cols("kf1", "even_in", 8, 2320, 256)
    wide("vf", "even_in", 2576)
    cols("qg", "even_in", 8, 0, 256)
    cols("kg", "even_in", 8, 256, 256)
    for g in range(2):
        cols(f"go{g}", "even_in", 8, 1024 + 256 * g, 256)
    halves(("eo0", "even_out", 0), ("eo1", "even_out", 512), parts=(1, 0))
    ffn(0, 1)
    ffn(1, 0)
    cols("kwi", "odd_in", 8, 1792, 72)
    cols("qi0", "odd_in", 8, 1280, 256)
    cols("qi1", "odd_in", 8, 1536, 256)
    cols("ckv", "odd_in", 8, 1024, 256)
    cols("q0", "odd_in", 8, 0, 256)
    cols("q1", "odd_in", 8, 256, 256)
    cols("uk", "w_ukT", 2, 0, 1024)
    cols("uv", "w_uv", 2, 0, 1024)
    cols("q2", "odd_in", 8, 512, 256)
    cols("q3", "odd_in", 8, 768, 256)
    halves(("oo0", "odd_out", 0), ("oo1", "odd_out", 512))
    ffn(1, 1)
    return out



CONST = dict(ident=(0, 128), tri=(128, 128), ones=(256, 128), tri64=(384, 128), m64=(512, 128), cm=(640, 256),
             cosA=(896, 64), sinA=(960, 64), cosB=(1024, 128), sinB=(1152, 128), hot=(1280, 512), mhalf=(1792, 16))
NCONST = 1808
GAIN = dict(g_mix=(0, 8), g_qa=(8, 2), g_kva=(10, 1), g_mlp=(11, 8), g_ple=(19, 8), n00=(27, 8), n01=(35, 8),
            n02=(43, 8), n10=(51, 8), n11=(59, 8), n12=(67, 8), g_gla=(75, 1), g_ckv=(76, 2))
NGAIN = 78


def constants():
    c = np.zeros((128, NCONST), np.float32)

    def put(name, a):
        o, n = CONST[name]
        a = np.asarray(a, np.float32)
        c[:a.shape[0], o:o + n] = a.reshape(a.shape[0], n)

    p = np.arange(128)
    le = p[:, None] <= p[None, :]
    same = (p[:, None] // 64) == (p[None, :] // 64)
    put("ident", np.eye(128))
    put("tri", le)
    put("ones", np.ones((128, 128)))
    put("tri64", (le & same) / 16.0)
    put("m64", le & same)
    put("cm", np.concatenate([np.zeros((128, 128)), np.where(p[None, :] <= p[:, None], 0.0, NEG)], 1))
    inv = np.float32(10000.0) ** (-np.arange(0, 32, 2, dtype=np.float32) / np.float32(32))

    def angles(pos):
        a = (pos.astype(np.float32)[:, None] * inv[None, :]).astype(np.float32).astype(np.float64)
        co, si = np.cos(a), np.sin(a)
        return np.concatenate([co, co], 1), np.concatenate([-si, si], 1)

    t = np.arange(S)
    ca, sa = angles(t)
    cr, sr = angles(t // 64)
    cc, sc = angles(t % 64)

    def tok(a):
        return a.reshape(2, 128, -1).transpose(1, 0, 2)

    put("cosA", tok(ca))
    put("sinA", tok(sa))
    put("cosB", tok(np.concatenate([cr, cc], 1)))
    put("sinB", tok(np.concatenate([sr, sc], 1)))
    dist = np.maximum(np.arange(512) - 255, 0)
    d = np.maximum(dist, 1).astype(np.float32)
    large = 16 + (np.log(d / np.float32(16)).astype(np.float32) / np.float32(np.log(8.0)) * np.float32(16)).astype(np.int32)
    bucket = np.where(dist < 16, dist, np.minimum(large, 31))
    put("hot", np.arange(32)[:, None] == bucket[None, :])
    put("mhalf", np.full((128, 16), -0.5))
    return c


class Lane:

    def __init__(self, sem):
        self.sem, self.n, self.q, self.seen = sem, 0, [], {}

    def add(self, fn, after, mark=True):
        waits = []
        todo = list(after)
        while todo:
            w = todo.pop(0)
            if isinstance(w, list):
                todo += w
            elif w is not None and self.seen.get(w[0].name, 0) < w[1]:
                self.seen[w[0].name] = w[1]
                waits.append(w)
        self.q.append((waits, fn, self.sem if mark else None, 1))
        if mark:
            self.n += 1
            return (self.sem, self.n)
        return None

    def dma(self, out, in_, sem, value, after):
        self.add(lambda e: e.dma_start(out, in_), after, mark=False)
        waits, fn, _, _ = self.q.pop()
        self.q.append((waits, fn, sem, 16))
        return (sem, value)

    def play(self, eng):
        for waits, fn, sem, by in self.q:
            for s, v in waits:
                eng.wait_ge(s, v)
            ins = fn(eng)
            if sem is not None:
                ins.then_inc(sem, by)


def program(nc, W, XIN, PT_IN, CST, GNS, GQK, GFIN, GFIN2, GLAG, FOXB, T5, OUT):
    P = plan()
    with ExitStack() as ctx:
        def sb(name, shape, dt=F):
            return ctx.enter_context(nc.sbuf_tensor(name, shape, dt))

        def sem(name):
            return ctx.enter_context(nc.semaphore(name))

        ps = [ctx.enter_context(nc.psum_tensor(f"ps{i}", [128, 512], F)) for i in range(8)]
        raw = sb("raw", [128, NRAW, HW])
        whi = sb("whi", [128, NHL, CW], R)
        wlo = sb("wlo", [128, NHL, CW], R)
        X = sb("X", [128, 2, D])
        xn = sb("xn", [128, 2, D])
        xnf = xn[:, :, :].rearrange("p t d -> p (t d)")
        hh = sb("hh", [128, 8, S], R)
        hl = sb("hl", [128, 8, S], R)
        cst = sb("cst", [128, NCONST])
        gns = sb("gns", [128, NGAIN])
        pbuf = sb("pbuf", [128, 3, 512])
        ptb = sb("ptb", [128, 2, 512])
        ra = sb("ra", [128, 4096], R)
        fa = sb("fa", [128, 11456])
        st = sb("st", [128, 256])
        rbb = sb("rbb", [128, 2, 256])
        fx = sb("fx", [128, 2048])
        gw = sb("gw", [17, 256])
        fb8 = sb("fb8", [128, 8])
        t5s = sb("t5s", [32, 16])
        fscratch = nc.dram_tensor("f_rows", [8, 256], F, kind="Internal")
        scratch = nc.dram_tensor("t5_rows", [16, 512], F, kind="Internal")

        PE, AC, VE, PO, SP = [Lane(sem(n)) for n in ("s_pe", "s_act", "s_dve", "s_pool", "s_sp")]
        s_raw = [sem(f"s_raw{i}") for i in range(NRAW)]
        s_in = sem("s_in")
        s_first = sem("s_first")
        s_x = [sem(f"s_x{i}") for i in range(2)]
        s_misc = sem("s_misc")
        s_t5w = sem("s_t5w")
        s_fw = sem("s_fw")
        s_fr = [sem(f"s_fr{i}") for i in range(3)]
        s_bias = [sem(f"s_bias{i}") for i in range(3)]
        s_gf = sem("s_gf")
        s_ki = sem("s_ki")
        s_out = sem("s_out")

        def C(name, rows=128):
            o, n = CONST[name]
            return cst[0:rows, o:o + n]

        def G(name):
            o, n = GAIN[name]
            return gns[:, o:o + n]

        def far(o, n):
            return fa[:, o:o + n]

        def rar(o, n):
            return ra[:, o:o + n]

        def vcopy(o, i, *w):
            return VE.add(lambda e: e.tensor_copy(o, i), w)

        def vtt(o, a, b, op, *w):
            return VE.add(lambda e: e.tensor_tensor(o, a, b, op), w)

        def vts(o, a, s1, s2, op0, op1, *w):
            if s2 is None:
                return VE.add(lambda e: e.tensor_scalar(o, a, s1, None, op0), w)
            return VE.add(lambda e: e.tensor_scalar(o, a, s1, s2, op0, op1), w)

        def vstt(o, a, s, b, op0, op1, *w):
            return VE.add(lambda e: e.scalar_tensor_tensor(out=o, in0=a, scalar=s, in1=b, op0=op0, op1=op1), w)

        def vred(o, a, op, *w, negate=False):
            return VE.add(lambda e: e.tensor_reduce(o, a, AX.X, op, negate=negate), w)

        def vrecip(o, a, *w):
            return VE.add(lambda e: e.reciprocal(o, a), w)

        def vset(o, v, *w):
            return VE.add(lambda e: e.memset(o, v), w)

        def act(o, i, f, *w, scale=1.0, bias=None, accum=None):
            if bias is None and accum is None:
                return AC.add(lambda e: e.activation(o, i, f, scale=scale), w)
            if accum is None:
                return AC.add(lambda e: e.activation(o, i, f, bias=bias, scale=scale), w)
            if bias is None:
                return AC.add(lambda e: e.activation(o, i, f, scale=scale, accum_out=accum), w)
            return AC.add(lambda e: e.activation(o, i, f, bias=bias, scale=scale, accum_out=accum), w)

        def ppow(o, a, n, *w):
            ex = C("mhalf")[:, 0:1].to_broadcast([128, n])
            return PO.add(lambda e: e.tensor_tensor(o, a, ex, ALU.pow), w)

        def mm(o, l, r, first, last, *w, mark=False):
            return PE.add(lambda e: e.matmul(o, l, r, start=first, stop=last, skip_group_check=True), w, mark)

        def tp(o, i, *w, mark=False):
            n = i.shape[0]
            ident = C("ident")[0:n, 0:n]
            return PE.add(lambda e: e.transpose(o, i, ident), w, mark)

        free = {b: [] for b in range(8)}

        def all_now():
            return [(l.sem, l.n) for l in (PE, AC, VE, PO) if l.n]

        ready, used, loaded = {}, {}, {}
        halves_of, parts = [], []
        for i, (_, pieces) in enumerate(P):
            n = sum(p[3] for p in pieces)
            halves_of.append(range(len(parts), len(parts) + (n + HW - 1) // HW))
            parts += [(i, c, min(HW, n - c)) for c in range(0, n, HW)]

        def load(j):
            if j < len(parts):
                i, c, n = parts[j]
                k = j % NRAW
                loaded[j] = SP.dma(raw[:, k, 0:n], W[i, :, c:c + n], s_raw[k], 16 * (j // NRAW + 1), [loaded.get(("s", j - NRAW))])

        def split_half(j):
            i, c, n = parts[j]
            r, h, l = raw[:, j % NRAW, 0:n], whi[:, i % NHL, c:c + n], wlo[:, i % NHL, c:c + n]
            t = act(h, r, ACT.Copy, loaded[j], used.get(i - NHL))

            def low():
                y = loaded["s", j] = vtt(l, r, h.bitcast(F), ALU.subtract, t)
                if j == halves_of[i][-1]:
                    ready[i] = y
                load(j + NRAW)

            return low

        held, lows = [], []

        def release(n=99, later=False):
            while lows:
                lows.pop(0)()
            while held and n:
                while lows:
                    lows.pop(0)()
                lows.append(split_half(held.pop(0)))
                n -= 1
            while lows and not later:
                lows.pop(0)()

        def split(i, hold=False):
            if i < len(P):
                held.extend(halves_of[i])
            if not hold:
                release()

        at = [0]

        def take(tag):
            i = at[0]
            assert P[i][0] == tag, (P[i][0], tag)
            at[0] += 1
            return i

        def done(i, tok, hold=False):
            used[i] = tok
            split(i + NHL, hold)

        def mm3(o, lh, ll, rh, rl, first, last, *w, mark=False):
            mm(o, lh, rh, first, False, *w)
            mm(o, lh, rl, False, False)
            return mm(o, ll, rh, False, last, mark=mark)

        def gemm_b(tag, xh, xl, nk, wd, outs, *w, hold=False):
            i = take(tag)
            s = i % NHL
            w = (ready[i],) + w
            for f, o in enumerate(outs):
                for k in range(nk):
                    c = k * wd + f * 128
                    t = mm3(o, whi[:, s, c:c + 128], wlo[:, s, c:c + 128], xh[:, k, :], xl[:, k, :],
                            k == 0, k == nk - 1, *w, mark=(f == len(outs) - 1 and k == nk - 1))
                    w = ()
            done(i, t, hold)
            return t

        def gemm_a(tag, xh, xl, ks, wd, outs, first, last, *w, hold=False, i=None):
            i = take(tag) if i is None else i
            s = i % NHL
            w = (ready[i],) + w
            for n, k in enumerate(ks):
                for t in range(2):
                    tk = slice(128 * t, 128 * t + 128)
                    for c, o in enumerate(outs[t]):
                        a = n * wd + c * 512
                        b = min(a + 512, (n + 1) * wd)
                        tok = mm3(o, xh[:, k, tk], xl[:, k, tk], whi[:, s, a:b], wlo[:, s, a:b],
                                  first and n == 0, last and n == len(ks) - 1, *w,
                                  mark=(n == len(ks) - 1 and t == 1 and c == len(outs[t]) - 1))
                        w = ()
            done(i, tok, hold)
            return tok

        def wide_a(tag, xh, xl, banks, *w):
            outs = [[ps[b][:, :]] for b in banks]
            gemm_a(tag + ".0", xh, xl, range(4), 512, outs, True, False, *w, [free[b] for b in banks])
            return gemm_a(tag + ".1", xh, xl, range(4, 8), 512, outs, False, True)

        def norm_stat(src, d, junk, o, *w):
            ss = [act(junk(t), src(t), ACT.Square, *w, accum=st[:, t:t + 1]) for t in range(2)]
            m = vts(st[:, 2:4], st[:, 0:2], 1.0 / d, EPS, ALU.mult, ALU.add, *ss)
            return ppow(o, st[:, 2:4], 2, m)

        def norm_t(src, d, gain, oh, ol, *w, banks=(0, 1, 2, 3)):
            nk = d // 128
            r = norm_stat(src, d, lambda t: xn[:, t, 0:d], st[:, 4:6], *w)
            y = [vts(xn[:, t, 0:d], src(t), st[:, 4 + t:5 + t], None, ALU.mult, None, r) for t in range(2)]
            toks = []
            for k0 in range(0, nk, 2):
                b = banks[(k0 // 2) % len(banks)]
                kk = range(k0, min(k0 + 2, nk))
                for k in kk:
                    for t in range(2):
                        c = (k - k0) * 256 + t * 128
                        tr = tp(ps[b][:, c:c + 128], xn[:, t, k * 128:(k + 1) * 128], y, free[b],
                                mark=(k == kk[-1] and t == 1))
                hs = [act(oh[:, k, :], ps[b][:, (k - k0) * 256:(k - k0 + 1) * 256], ACT.Copy, tr, *w,
                          scale=gain[:, k:k + 1]) for k in kk]
                for k in kk:
                    lo = vstt(ol[:, k, :], ps[b][:, (k - k0) * 256:(k - k0 + 1) * 256], gain[:, k:k + 1],
                              oh[:, k, :].bitcast(F), ALU.mult, ALU.subtract, hs, *w)
                free[b] = [lo]
                toks.append(lo)
            return toks

        ACC = [[0, 1], [2, 3]]
        accs = [[ps[b][:, :] for b in r] for r in ACC]
        joins = [0]
        junk = {}

        def add_half(c, scale, tok):
            out = []
            for t in range(2):
                b = ACC[t][c]
                xs = X[:, t, c * 512:(c + 1) * 512]
                r = vstt(xs, ps[b][:, :], scale, xs, ALU.mult, ALU.add, tok)
                free[b] = [r]
                out.append(r)
            return out

        def square_half(q, c, rt):
            out = []
            for t in range(2):
                sl = slice(c * 512, (c + 1) * 512)
                junk[t, c] = act(xn[:, t, sl], X[:, t, sl], ACT.Square, rt[t], junk.get((t, c)),
                                 accum=st[:, q + 2 * c + t:q + 2 * c + t + 1])
                out.append(junk[t, c])
            return out

        def turn_half(c, gain, rt, src=X):
            toks = []
            for p in range(2):
                b = ACC[p][c]
                for k in range(4 * c + 2 * p, 4 * c + 2 * p + 2):
                    for t in range(2):
                        o = (k % 2) * 256 + t * 128
                        tr = tp(ps[b][:, o:o + 128], src[:, t, k * 128:(k + 1) * 128], rt, free[b],
                                mark=(k % 2 == 1 and t == 1))
                kk = [(k, ps[b][:, (k % 2) * 256:(k % 2 + 1) * 256]) for k in range(4 * c + 2 * p, 4 * c + 2 * p + 2)]
                hi = [act(hh[:, k, :], pk, ACT.Copy, tr, scale=gain[:, k:k + 1]) for k, pk in kk]
                for k, pk in kk:
                    lo = vstt(hl[:, k, :], pk, gain[:, k:k + 1], hh[:, k, :].bitcast(F), ALU.mult, ALU.subtract, hi)
                    toks.append(lo)
                free[b] = [lo]
            return toks

        def rms_inv(o, q, *w):
            m = vtt(st[:, q + 4:q + 6], st[:, q:q + 2], st[:, q + 2:q + 4], ALU.add, *w)
            m = vts(st[:, q + 4:q + 6], st[:, q + 4:q + 6], 1.0 / D, EPS, ALU.mult, ALU.add, m)
            return ppow(o, st[:, q + 4:q + 6], 2, m)

        def diagonal(r, tok):
            return [vts(rbb[:, 1, 128 * t:128 * t + 128], C("ident"), r[:, t:t + 1], None, ALU.mult, None, tok, rbd[0])
                    for t in range(2)]

        rbd, rb_read = [None], [None]

        def spread(dg, b):
            for t in range(2):
                y = mm(ps[b][:, 128 * t:128 * t + 128], C("ones"), rbb[:, 1, 128 * t:128 * t + 128], True, True, dg,
                       free[b], mark=(t == 1))
            rbd[0] = y
            y = act(rbb[:, 0, :], ps[b][:, 0:256], ACT.Copy, y, rb_read[0])
            free[b] = [y]
            return y

        def join(c0, c1, scale, gain, *w):
            q = 128 + 16 * (joins[0] % 4)
            joins[0] += 1
            rb_read[0] = all_now()
            rt0 = add_half(0, scale, [c0(), *w])
            tok = c1[0]()
            sq = square_half(q, 0, rt0)
            n0 = turn_half(0, gain, rt0)
            for f in c1[1:]:
                tok = f()
            rt1 = add_half(1, scale, tok)
            sq += square_half(q, 1, rt1)
            r = st[:, q + 6:q + 8]
            rtok = rms_inv(r, q, sq)

            def second():
                n1 = turn_half(1, gain, rt1)
                dg = diagonal(r, rtok)
                release()
                return n1, dg

            return dict(x=rt0 + rt1, n0=n0, second=second, r=r, rtok=rtok)

        def proj_start(tag, c, part, xh, xl, *w, hold=False):
            gemm_a(f"{tag}{c}.{part}", xh, xl, range(4 * part, 4 * part + 4), 512, [[accs[0][c]], [accs[1][c]]], True, False,
                   *w, [free[ACC[t][c]] for t in range(2)], hold=hold)

        def proj_end(tag, part, xh, xl, *w):
            def c0():
                return gemm_a(f"{tag}0.{part}", xh, xl, range(4 * part, 4 * part + 4), 512, [[accs[0][0]], [accs[1][0]]],
                              False, True, *w, hold=True)

            i1 = []

            def c1(ks):
                def f():
                    if not i1:
                        i1.append(take(f"{tag}1.{part}"))
                    i = i1[0]
                    s = i % NHL
                    for n in ks:
                        k = 4 * part + n
                        for t in range(2):
                            tk = slice(128 * t, 128 * t + 128)
                            tok = mm3(accs[t][1], xh[:, k, tk], xl[:, k, tk], whi[:, s, 512 * n:512 * n + 512],
                                      wlo[:, s, 512 * n:512 * n + 512], False, n == 3, ready[i],
                                      mark=(n == ks[-1] and t == 1))
                    if ks[-1] == 3:
                        done(i, tok, hold=True)
                    return tok
                return f

            return c0, [c1((0, 1)), c1((2, 3))]

        def b_part(i, ks, outs, first, last, *w):
            s = i % NHL
            w = (ready[i],) + w
            for f, o in enumerate(outs):
                for k in ks:
                    c = k * 256 + f * 128
                    t = mm3(o, whi[:, s, c:c + 128], wlo[:, s, c:c + 128], hh[:, k, :], hl[:, k, :],
                            first and f == 0 and k == ks[0], last and k == ks[-1], *w,
                            mark=(f == 1 and k == ks[-1]))
                    w = ()
            return t

        def opening(tags, banks, J):
            ii = [take(t) for t in tags]
            late = J.get("late")
            o = [[ps[b][:, 0:256], ps[b][:, 256:512]] for b in banks]
            b_part(ii[0], range(4), o[0], True, False, J["n0"], free[banks[0]])
            if late is None:
                n1, dg = J["second"]()
            if late is None:
                b_part(ii[1], range(4), o[1], True, False, free[banks[1]])
            else:
                b_part(ii[1], range(2), o[1], True, False, free[banks[1]])
                n1, dg = J["second"]()
                b_part(ii[1], range(2, 4), o[1], False, False)
                late()
            ta = b_part(ii[0], range(4, 8), o[0], False, True, n1)
            done(ii[0], ta, hold=True)
            if late is None:
                rbt = spread(dg, 0)
            tb = b_part(ii[1], range(4, 8), o[1], False, True)
            done(ii[1], tb, hold=True)
            if late is not None:
                rbt = spread(dg, 0)
            return ta, tb, rbt

        def attention(heads, causal, oh, ol, *w, fill=lambda n: None, outs=None, SB=(0, 1), TB=(3, 4), OB=(5, 6),
                      first=2):
            n = len(heads)
            stt = xnf[:, 0:1024].rearrange("p (s c) -> p s c", s=2)
            off = (0, 128) if causal else (0, 256)
            kl = (128, 256) if causal else (256, 256)
            tot = off[1] + kl[1]
            s1, s2, p3, pt, pv, ex = {}, {}, {}, {}, {}, {}
            outs = [] if outs is None else outs

            def scores(h):
                hd = heads[h]
                b = SB[h % 2]
                for t in range(2):
                    o = ps[b][:, off[t]:off[t] + kl[t]]
                    s1[h] = mm(o, hd["q"](t), hd["k"](kl[t]), True, True, *w, hd.get("after", list)(), free[b],
                               mark=(t == 1))

            def soft(h):
                hd = heads[h]
                b = SB[h % 2]
                sl = h % 3
                c = 16 + 6 * (h % 8)
                nm, sm, rs = st[:, c:c + 2], st[:, c + 2:c + 4], st[:, c + 4:c + 6]
                if causal:
                    src = stt[:, h % 2, 0:tot]
                    more, mt = hd["add"], hd["added"]
                    mx = st[:, 216 + 2 * (h % 8):218 + 2 * (h % 8)]
                    for t in range(2):
                        o, i_, a_ = src[:, off[t]:off[t] + kl[t]], ps[b][:, off[t]:off[t] + kl[t]], more[:, off[t]:off[t] + kl[t]]
                        e = VE.add(lambda e, o=o, i_=i_, a_=a_, t=t: e.tensor_tensor_reduce(
                            out=o, in0=i_, in1=a_, scale=1.0, scalar=GONE, op0=ALU.add, op1=ALU.max,
                            accum_out=mx[:, t:t + 1]), [s1[h], ex.get(h - 2), mt()])
                    free[b] = [e]
                    hd["used"](e)
                    if "row" in hd:
                        m = vtt(mx, mx, hd["row"], ALU.add, e)
                        m = vtt(nm, hd["row"], mx, ALU.subtract, m, ex.get(h - 8))
                    else:
                        m = vts(nm, mx, -1.0, None, ALU.mult, None, e, ex.get(h - 8))
                else:
                    src = ps[b][:, 0:tot]
                    m = vred(nm, src.rearrange("p (t k) -> p t k", t=2), ALU.max, s1[h], ex.get(h - 8), negate=True)
                for t in range(2):
                    ex[h] = act(pbuf[:, sl, off[t]:off[t] + kl[t]], src[:, off[t]:off[t] + kl[t]], ACT.Exp, m,
                                p3.get(h - 3), s2.get(h - 8), bias=nm[:, t:t + 1], accum=sm[:, t:t + 1])
                if not causal:
                    free[b] = [ex[h]]

            def share(h):
                sl = h % 3
                c = 16 + 6 * (h % 8)
                sm, rs = st[:, c + 2:c + 4], st[:, c + 4:c + 6]
                r = vrecip(rs, sm, ex[h])
                for t in range(2):
                    s2[h] = vts(pbuf[:, sl, off[t]:off[t] + kl[t]], pbuf[:, sl, off[t]:off[t] + kl[t]], rs[:, t:t + 1],
                                None, ALU.mult, None, r)

            def turn(h):
                b = TB[h % len(TB)]
                sl = h % 3
                for t in range(2):
                    for k in range(kl[t] // 128):
                        c = 256 * k + 128 * (t - k if causal else t)
                        p3[h] = tp(ps[b][:, c:c + 128], pbuf[:, sl, off[t] + 128 * k:off[t] + 128 * k + 128], s2[h],
                                   free[b], mark=(t == 1 and k == kl[t] // 128 - 1))
                pt[h] = act(ptb[:, h % 2, 0:tot], ps[b][:, 0:tot], ACT.Copy, p3[h], pv.get(h - 2))
                free[b] = [pt[h]]

            def weigh(h):
                hd = heads[h]
                pr, par = divmod(h, 2)
                b = OB[pr % len(OB)]
                o = ps[b][64 * par:64 * par + 64, 0:256]
                mm(o, hd["v"](0), ptb[:, h % 2, 0:256], True, False, pt[h], free[b])
                if causal:
                    pv[h] = mm(o[:, 128:256], hd["v"](1), ptb[:, h % 2, 256:384], False, True, mark=True)
                else:
                    pv[h] = mm(o, hd["v"](1), ptb[:, h % 2, 256:512], False, True, mark=True)
                if par:
                    t = act(oh(pr), ps[b][:, 0:256], ACT.Copy, pv[h])
                    t = vtt(ol(pr), ps[b][:, 0:256], oh(pr).bitcast(F), ALU.subtract, t)
                    free[b] = [t]
                    outs.append(t)

            for i in range(n + 3):
                if i < n:
                    scores(i)
                    soft(i)
                    fill(2 if i > 1 else first)
                if 1 <= i < n + 1:
                    share(i - 1)
                if 2 <= i < n + 2:
                    turn(i - 2)
                if 2 <= i < n + 2:
                    fill(1)
                if i >= 3:
                    weigh(i - 3)
                release(1, later=True)
                if i >= 3:
                    fill(2)
            return outs

        xv = XIN.rearrange("(t p) d -> p t d", p=128)
        XT = []
        for c in range(2):
            XT.append([SP.dma(X[:, :, 512 * c:512 * c + 512], xv[:, :, 512 * c:512 * c + 512], s_x[c], 16, [])] * 2)
            load(c)
        n = CONST["ident"][1]
        AC.dma(cst[:, 0:n], CST[:, 0:n], s_first, 16, [])
        FIRST = AC.dma(gns[:, :], GNS, s_first, 32, [])
        for i in range(2, NRAW):
            load(i)
        k = 0
        for o, a in ((cst[:, n:NCONST], CST[:, n:NCONST]), (fa[:, 10816:11456], GQK.partition_broadcast(128)),
                     (gw[:, :], GLAG), (fb8[:, :], FOXB.partition_broadcast(128)), (t5s[:, :], T5)):
            k += 16
            PO.dma(o, a, s_in, k, [XT[0][0], XT[1][0], FIRST])
        IN = (s_in, k)

        q = 128
        joins[0] = 1
        n0 = turn_half(0, G("g_mix"), [XT[0][0], FIRST])
        split(0)
        n1 = turn_half(1, G("g_mix"), [XT[1][0], FIRST])
        split(1)
        sq = square_half(q, 0, XT[0]) + square_half(q, 1, XT[1])
        for i in range(2, NHL):
            split(i)
        rX = st[:, q + 6:q + 8]
        rXt = rms_inv(rX, q, sq, IN)
        dg = diagonal(rX, rXt)
        z = far(0, 2368).rearrange("p (t c) -> p t c", t=2)
        qa = far(2368, 1536).rearrange("p (t c) -> p t c", t=2)
        qaT = far(3904, 2048).rearrange("p (h c) -> p h c", h=8)
        kaT = far(5952, 2048).rearrange("p (h c) -> p h c", h=8)
        va = far(8000, 1024).rearrange("p (t h c) -> p t h c", t=2, h=8)
        qbT = far(9024, 1024).rearrange("p (h c) -> p h c", h=4)
        kbT = far(10048, 512).rearrange("p (h c) -> p h c", h=2)
        kp = far(10560, 192).rearrange("p (t c) -> p t c", t=2)
        gqk = far(10816, 640)
        cqh = rar(0, 512).rearrange("p (k c) -> p k c", k=2)
        cql = rar(512, 512).rearrange("p (k c) -> p k c", k=2)
        ckh = rar(1024, 256).rearrange("p (k c) -> p k c", k=1)
        ckl = rar(1280, 256).rearrange("p (k c) -> p k c", k=1)

        zt = []
        ZB = [[4, 6], [5, 7]]
        for part in range(2):
            for c in range(2):
                tz = gemm_a(f"z{c}.{part}", hh, hl, range(4 * part, 4 * part + 4), 512,
                            [[ps[ZB[t][c]][:, :]] for t in range(2)], part == 0, part == 1, (n0, n1)[part],
                            [free[ZB[t][c]] for t in range(2)] if part == 0 else None)
                if part == 0:
                    continue
                for t in range(2):
                    b = ZB[t][c]
                    y = act(z[:, t, 512 * c:512 * c + 512], ps[b][:, :], ACT.Copy, tz, rXt, scale=rX[:, t:t + 1])
                    free[b] = [y]
                    zt.append(y)
        rbt = spread(dg, 2)
        t0 = gemm_a("z2", hh, hl, range(8), 160, [[ps[0][:, 0:160]], [ps[1][:, 0:160]]], True, True, free[0], free[1])
        for t in range(2):
            y = act(z[:, t, 1024:1184], ps[t][:, 0:160], ACT.Copy, t0, scale=rX[:, t:t + 1])
            free[t] = [y]
            zt.append(y)

        sg = [fx[:, 512 * g:512 * g + 512] for g in range(4)] + [xnf[:, 512 * g:512 * g + 512] for g in range(4)]
        gt = {}
        rbc = rbb[:, 0, :].unsqueeze(1).to_broadcast([128, 2, 256])

        def two(a):
            return a.rearrange("p (h c) -> p h c", h=2)

        def gate(g, b, *w):
            i = take(f"gate{g}")
            s = i % NHL
            for f in range(2):
                for k in range(8):
                    c = k * 256 + f * 128
                    t0 = mm3(ps[b][:, 256 * f:256 * f + 256], whi[:, s, c:c + 128], wlo[:, s, c:c + 128], hh[:, k, :],
                             hl[:, k, :], k == 0, k == 7, ready[i], free[b], mark=(f == 1 and k == 7))
                    if (f, k) != (1, 7):
                        yield
            y = vtt(two(sg[g]), two(ps[b][:, :]), rbc, ALU.mult, t0, rbt, *w)
            free[b] = [y]
            gt[g] = act(sg[g], sg[g], ACT.Tanh, y, scale=0.5)
            done(i, t0, hold=True)
            yield

        for t in range(2):
            a0 = act(xnf[:, 384 * t:384 * t + 256], z[:, t, 0:256], ACT.Square, zt, sq, accum=st[:, t:t + 1])
            a1 = act(xnf[:, 384 * t + 256:384 * t + 384], z[:, t, 256:384], ACT.Square, accum=st[:, 2 + t:3 + t])
        m = [vts(st[:, 4:6], st[:, 0:2], 1.0 / 256, EPS, ALU.mult, ALU.add, a1),
             vts(st[:, 6:8], st[:, 2:4], 1.0 / 128, EPS, ALU.mult, ALU.add)]
        r = ppow(st[:, 8:12], st[:, 4:8], 4, m)
        qk = [z[:, t, 416:1056].rearrange("p (h c) -> p h c", c=64) for t in range(2)]
        pb = pbuf[:, :, :].rearrange("p s c -> p (s c)")
        hsq = []
        for t in range(2):
            a = act(pb[:, 640 * t:640 * t + 640], z[:, t, 416:1056], ACT.Square, zt)
            hsq.append(a)
        yn = []
        for t in range(2):
            yn.append(vts(xnf[:, 384 * t:384 * t + 256], z[:, t, 0:256], st[:, 8 + t:9 + t], None, ALU.mult, None, r))
            yn.append(vts(xnf[:, 384 * t + 256:384 * t + 384], z[:, t, 256:384], st[:, 10 + t:11 + t], None, ALU.mult, None))
        hs = [vred(st[:, 64 + 10 * t:74 + 10 * t], pb[:, 640 * t:640 * t + 640].rearrange("p (h c) -> p h c", c=64),
                   ALU.add, hsq[t]) for t in range(2)]
        m = vts(st[:, 84:104], st[:, 64:84], 1.0 / 64, EPS, ALU.mult, ALU.add, hs)
        rh = ppow(st[:, 104:124], st[:, 84:104], 20, m)

        for _ in gate(0, 6):
            pass
        for k in range(2):
            for t in range(2):
                c = k * 256 + t * 128
                tq = tp(ps[2][:, c:c + 128], xnf[:, 384 * t + 128 * k:384 * t + 128 * k + 128], yn, free[2],
                        mark=(k == 1 and t == 1))
        for t in range(2):
            tk = tp(ps[3][:, 128 * t:128 * t + 128], xnf[:, 384 * t + 256:384 * t + 384], free[3], mark=(t == 1))
        ncq = []
        hs = [act(cqh[:, k, :], ps[2][:, 256 * k:256 * k + 256], ACT.Copy, tq, scale=G("g_qa")[:, k:k + 1]) for k in range(2)]
        for k in range(2):
            ncq.append(vstt(cql[:, k, :], ps[2][:, 256 * k:256 * k + 256], G("g_qa")[:, k:k + 1], cqh[:, k, :].bitcast(F),
                            ALU.mult, ALU.subtract, hs))
        free[2] = [ncq[-1]]
        a = act(ckh[:, 0, :], ps[3][:, 0:256], ACT.Copy, tk, scale=G("g_kva")[:, 0:1])
        nck = vstt(ckl[:, 0, :], ps[3][:, 0:256], G("g_kva")[:, 0:1], ckh[:, 0, :].bitcast(F), ALU.mult, ALU.subtract, a)
        free[3] = [nck]
        release()
        ytr = [ncq, nck]

        kd = ptb[:, :, 0:256]
        kdt = []

        def by_head(t, *w):
            rb = st[:, 104 + 10 * t:114 + 10 * t].unsqueeze(2).to_broadcast([128, 10, 64])
            a = vtt(qk[t], qk[t], rb, ALU.mult, rh)
            return vtt(z[:, t, 416:1056], z[:, t, 416:1056], gqk, ALU.mult, a, IN)

        turned = [[v[:, 640 * i:640 * i + 640].rearrange("p (h c) -> p h c", c=64) for i in range(2)]
                  for v in (pb, far(9024, 1280))]

        def axes(t, a, *w):
            def ptt(o, x, y, op, *w):
                return PO.add(lambda e: e.tensor_tensor(o, x, y, op), w)

            co = C("cosB")[:, 64 * t:64 * t + 64].unsqueeze(1).to_broadcast([128, 10, 64])
            t1, t2 = turned[t]
            ws = [ptt(t1, qk[t], co, ALU.mult, a, *w)]
            x4 = qk[t].rearrange("p h (r c d) -> p h r c d", r=2, c=2)
            t4 = t2.rearrange("p h (r c d) -> p h r c d", r=2, c=2)
            s4 = C("sinB")[:, 64 * t:64 * t + 64].rearrange("p (r c d) -> p r c d", r=2, c=2)
            for half in range(2):
                for rc in range(2):
                    sn = s4[:, rc, half, :].unsqueeze(1).to_broadcast([128, 10, 16])
                    ws.append(ptt(t4[:, :, rc, half, :], x4[:, :, rc, 1 - half, :], sn, ALU.mult))
            return ws

        def axes_end(t, ws):
            t1, t2 = turned[t]
            a = vtt(qk[t], t1, t2, ALU.add, ws)
            for j in range(2):
                for d in range(2):
                    kdt.append(vcopy(kd[:, t, 128 * j + 64 * d:128 * j + 64 * d + 64],
                                     z[:, t, 928 + 64 * j:992 + 64 * j], a))
            return a

        def rope(x, n, cos, sin, t1, t2, *w):
            a = vtt(t1, x, cos, ALU.mult, *w)
            b = vtt(t2[:, :, 0, :], x[:, :, 1, :], sin[:, :, 0, :], ALU.mult, *w)
            c = vtt(t2[:, :, 1, :], x[:, :, 0, :], sin[:, :, 1, :], ALU.mult, *w)
            return vtt(x, t1, t2, ALU.add, a, b, c)

        for _ in gate(1, 1):
            pass
        a = by_head(0)
        b = by_head(1)
        ws = [axes(0, a, hs), axes(1, b)]
        vz = vset(kp[:, :, 0:64], 0.0)
        kt = []
        tmp = xnf
        wx = [vz, ytr, IN]
        for t in range(2):
            src = z[:, t, 384:416].rearrange("p (n c d) -> p n c d", n=1, c=2)
            dst = kp[:, t, 64:96].rearrange("p (n c d) -> p n c d", n=1, c=2)
            co = C("cosA")[:, 32 * t:32 * t + 32].rearrange("p (n c d) -> p n c d", n=1, c=2)
            si = C("sinA")[:, 32 * t:32 * t + 32].rearrange("p (n c d) -> p n c d", n=1, c=2)
            cp = vcopy(dst, src, zt)
            wx = [rope(dst, 1, co, si, tmp[:, 0:32].rearrange("p (n c d) -> p n c d", n=1, c=2),
                       tmp[:, 32:64].rearrange("p (n c d) -> p n c d", n=1, c=2), cp, wx)]
            kt.append(wx)

        outs = [[ps[4][:, :], ps[5][:, 0:256]], [ps[6][:, :], ps[7][:, 0:256]]]
        t0 = gemm_a("wqb", cqh, cql, range(2), 768, outs, True, True, ncq, [free[b] for b in (4, 5, 6, 7)], hold=True)
        qt = []
        SCA = float(np.float32(96 ** -0.5))
        for t in range(2):
            b = 4 + 2 * t
            y = act(qa[:, t, 0:512], ps[b][:, :], ACT.Copy, t0, scale=SCA)
            free[b] = [y]
            y2 = act(qa[:, t, 512:768], ps[b + 1][:, 0:256], ACT.Copy, t0, scale=SCA)
            free[b + 1] = [y2]
            qt += [y, y2]
        release(2)

        i = take("wkvb")
        s = i % NHL
        for h in range(8):
            b = (0, 1, 2, 3)[h // 2]
            t0 = mm3(ps[b][:, 256 * (h % 2):256 * (h % 2) + 256], whi[:, s, 128 * h:128 * h + 128],
                     wlo[:, s, 128 * h:128 * h + 128], ckh[:, 0, :], ckl[:, 0, :], True, True, ready[i], nck, free[b],
                     mark=(h % 2 == 1))
            if h % 2:
                y = act(kaT[0:64, h - 1:h + 1, :], ps[b][0:64, :].rearrange("p (h c) -> p h c", h=2), ACT.Copy, t0)
                free[b] = [y]
                qt.append(y)
        for t in range(2):
            for c in range(2):
                b = 4 + 2 * t + c
                t0 = mm3(ps[b][:, :], ckh[:, 0, 128 * t:128 * t + 128], ckl[:, 0, 128 * t:128 * t + 128],
                         whi[:, s, 512 * c:512 * c + 512], wlo[:, s, 512 * c:512 * c + 512], True, True, free[b],
                         mark=True)
                y = vcopy(va[:, t, 4 * c:4 * c + 4, :],
                          ps[b][:, :].rearrange("p (h c) -> p h c", h=4)[:, :, 64:128], t0)
                free[b] = [y]
                qt.append(y)
        done(i, t0, hold=True)
        for t in range(2):
            tkp = tp(ps[0][0:96, 128 * t:128 * t + 128], kp[:, t, :], kt, free[0], mark=(t == 1))

        qrt = []
        for t in range(2):
            qv = qa[:, t, :].rearrange("p (h c) -> p h c", c=96)[:, :, 64:96]
            t1 = tmp[:, 0:256].rearrange("p (h c) -> p h c", h=8)
            t2 = tmp[:, 256:512].rearrange("p (h c) -> p h c", h=8)
            cb = C("cosA")[:, 32 * t:32 * t + 32].unsqueeze(1).to_broadcast([128, 8, 32])
            sb0 = C("sinA")[:, 32 * t:32 * t + 16].unsqueeze(1).to_broadcast([128, 8, 16])
            sb1 = C("sinA")[:, 32 * t + 16:32 * t + 32].unsqueeze(1).to_broadcast([128, 8, 16])
            a = vtt(t1, qv, cb, ALU.mult, qt, wx)
            b = vtt(t2[:, :, 0:16], qv[:, :, 16:32], sb0, ALU.mult)
            c = vtt(t2[:, :, 16:32], qv[:, :, 0:16], sb1, ALU.mult)
            r = vtt(qv, t1, t2, ALU.add, a, b, c)
            wx = [r]
            qrt.append(r)
        kt.append(qrt)
        for _ in gate(2, 2):
            pass
        y = vcopy(kaT[64:96, :, :], ps[0][64:96, 0:256].unsqueeze(1).to_broadcast([32, 8, 256]), tkp)
        free[0] = [y]
        att = [y]
        for h in range(8):
            b = (4, 5, 6, 7)[h // 2]
            for t in range(2):
                c = 256 * (h % 2) + 128 * t
                t0 = tp(ps[b][0:96, c:c + 128], qa[:, t, 96 * h:96 * h + 96], kt, free[b], mark=(h % 2 == 1 and t == 1))
            if h % 2:
                y = act(qaT[0:96, h - 1:h + 1, :], ps[b][0:96, :].rearrange("p (h c) -> p h c", h=2), ACT.Copy, t0)
                free[b] = [y]
                att.append(y)

        for t in range(2):
            axes_end(t, ws[t])
        release(2)
        gate3 = gate(3, 2, wx)
        for _ in range(9):
            next(gate3)
        att_b = []
        for j in range(2):
            b = (1, 7)[j]
            for pr in range(2):
                for t in range(2):
                    q0 = 416 + 256 * j + 128 * pr
                    t0 = tp(ps[b][:, 256 * pr + 128 * t:256 * pr + 128 * t + 128], z[:, t, q0:q0 + 128], kdt, free[b],
                            mark=(pr == 1 and t == 1))
            y = act(qbT[:, 2 * j:2 * j + 2, :], ps[b][:, :].rearrange("p (h c) -> p h c", h=2), ACT.Copy, t0, scale=0.125)
            free[b] = [y]
            att_b.append(y)
        for j in range(2):
            for t in range(2):
                c = 256 * j + 128 * t
                t0 = tp(ps[3][:, c:c + 128], kd[:, t, 128 * j:128 * j + 128], kdt, free[3], mark=(j == 1 and t == 1))
        y = act(kbT[:, :, :], ps[3][:, :].rearrange("p (h c) -> p h c", h=2), ACT.Copy, t0)
        free[3] = [y]
        att_b.append(y)

        def head_a(h):
            return dict(q=lambda t: qaT[0:96, h, 128 * t:128 * t + 128], k=lambda n: kaT[0:96, h, 0:n],
                        v=lambda k: va[:, k, h, :])

        def head_b(h):
            lo = 64 * (h % 2)
            g = h // 4
            return dict(after=lambda: att_b, q=lambda t: qbT[lo:lo + 64, h // 2, 128 * t:128 * t + 128],
                        k=lambda n: kbT[lo:lo + 64, g, 0:n],
                        v=lambda k: z[:, k, 1056 + 64 * g:1120 + 64 * g])

        oh = rar(0, 2048).rearrange("p (k c) -> p k c", k=8)
        ol = rar(2048, 2048).rearrange("p (k c) -> p k c", k=8)
        ma = far(2368, 1024).rearrange("p (s c) -> p s c", s=2)
        at1 = []

        def out_half(nm, c, n, banks):
            i = take(f"{nm}{c}")
            s = i % NHL
            toks = []
            for f in range(4):
                b = banks[f // 2]
                for k in range(4):
                    a = k * 512 + f * 128
                    t0 = mm3(ps[b][:, 256 * (f % 2):256 * (f % 2) + 256], whi[:, s, a:a + 128], wlo[:, s, a:a + 128],
                             oh[:, 4 * n + k, :], ol[:, 4 * n + k, :], k == 0, k == 3, ready[i],
                             at1[4 * n:4 * n + 4], free[b], mark=(k == 3 and f % 2 == 1))
                    if (f, k) != (3, 3):
                        yield
                if f % 2:
                    toks.append(t0)
            done(i, t0, hold=True)
            out_tok[nm, c] = toks
            yield

        out_tok = {}

        def between():
            yield from gate3
            for g in range(4, 8):
                yield from gate(g, (7, 2)[g % 2], wx)
            while len(at1) < 4:
                yield
            yield
            yield
            yield from out_half("oa", 0, 0, (2, 7))

        other = between()

        def fill(n):
            for _ in range(n):
                next(other, None)

        attention([head_a(h) for h in range(8)] + [head_b(h) for h in range(8)], False,
                  lambda j: oh[:, j, :], lambda j: ol[:, j, :], att, qt, fill=fill, outs=at1, first=6)
        fill(200)
        release()

        last_g = (PE.sem, PE.n)
        for _ in out_half("ob", 0, 1, (0, 1)):
            pass
        mt = [[], []]

        def merge(c, ba, bb):
            for f2 in range(2):
                fs = 4 * c + 2 * f2
                g = 2 * c + f2
                m1, m2 = ma[:, 0, :], ma[:, 1, :]
                a = vstt(m1, sg[g], 1.0, ps[ba[f2]][:, :], ALU.add, ALU.mult, out_tok["oa", c][f2], gt[g], mt[0], mt[1], att, att_b, last_g)
                b = vstt(m2, sg[4 + g], 1.0, ps[bb[f2]][:, :], ALU.add, ALU.mult, out_tok["ob", c][f2], gt[4 + g])
                free[ba[f2]], free[bb[f2]] = [a], [b]
                a = vtt(m1, m1, m2, ALU.add, a, b)
                hv = hh[:, fs:fs + 2, :].rearrange("p a b -> p (a b)")
                b = act(hv, m1, ACT.Copy, a, last_g)
                mt[c].append(vtt(hl[:, fs:fs + 2, :].rearrange("p a b -> p (a b)"), m1, hv.bitcast(F), ALU.subtract, b))

        merge(0, (2, 7), (0, 1))
        release()
        for _ in out_half("oa", 1, 0, (3, 4)):
            pass
        release()
        for _ in out_half("ob", 1, 1, (5, 6)):
            pass
        merge(1, (3, 4), (5, 6))
        release()
        for c in range(2):
            proj_start("o", c, 0, hh, hl, mt[0])
        c0, c1 = proj_end("o", 1, hh, hl, mt[1])
        J = join(c0, c1, 0.5, G("g_mlp"))

        uh = rar(0, 1536).rearrange("p (s c) -> p s c", s=3)
        ul = rar(1536, 1536).rearrange("p (s c) -> p s c", s=3)
        fr = far(0, 1024).rearrange("p (s c) -> p s c", s=2)
        fu = far(1024, 1024).rearrange("p (s c) -> p s c", s=2)
        ud, ut = {}, {}

        def u_split(g, y):
            s, s3 = g % 2, g % 3
            a = act(uh[:, s3, :], fu[:, s, :], ACT.Copy, y, ud.get(g - 3))
            ut[g] = vtt(ul[:, s3, :], fu[:, s, :], uh[:, s3, :].bitcast(F), ALU.subtract, a)

        def down(i, g, cs, first, last):
            s = i % NHL
            u2 = [a[:, g % 3, :].rearrange("p (k c) -> p k c", k=2) for a in (uh, ul)]
            w = (ready[i], ut[g], [free[b] for b in range(4)] if first else None)
            for k in range(2):
                for t in range(2):
                    tk = slice(128 * t, 128 * t + 128)
                    for c in cs:
                        a = k * 1024 + c * 512
                        tok = mm3(accs[t][c], u2[0][:, k, tk], u2[1][:, k, tk], whi[:, s, a:a + 512],
                                  wlo[:, s, a:a + 512], first and k == 0, last and k == 1, *w,
                                  mark=(k == 1 and t == 1 and c == cs[-1]))
                        w = ()
            ud[g] = tok
            return tok

        def layer_body(n, lag, open_, up, tag):
            ud.clear()
            ut.clear()
            g0 = open_()
            for g in range(n):
                if g >= g0:
                    up(g)
                if lag <= g < n - 3 + lag:
                    i = take(f"{tag}{g - lag}")
                    done(i, down(i, g - lag, (0, 1), g == lag, False))
            ii = {}

            def c0():
                for g in range(n - 3, n):
                    ii[g] = take(f"{tag}{g}")
                    tok = down(ii[g], g, (0,), False, g == n - 1)
                return tok

            def c1(g):
                def f():
                    tok = down(ii[g], g, (1,), False, g == n - 1)
                    done(ii[g], tok, hold=(g == n - 1))
                    return tok
                return f

            return c0, [c1(g) for g in range(n - 3, n)]

        def up1_end(g, t0, now, rbt):
            b = 4 + g % 4
            s = g % 2
            y = vstt(two(fr[:, s, :]), two(ps[b][:, :]), 0.0, rbc, ALU.max, ALU.mult, t0, now, rbt, ut.get(g - 2))
            free[b] = [y]
            u_split(g, act(fu[:, s, :], fr[:, s, :], ACT.Square, y, ut.get(g - 2)))

        def mlp(J):
            now = all_now()
            rbt = None

            def open_():
                nonlocal rbt
                ta, tb, rbt = opening(("up0", "up1"), (4, 5), J)
                up1_end(0, ta, now, rbt)
                release(2)
                up1_end(1, tb, now, rbt)
                release()
                return 2

            def up(g):
                b = 4 + g % 4
                t0 = gemm_b(f"up{g}", hh, hl, 8, 256, [ps[b][:, 0:256], ps[b][:, 256:512]], free[b], hold=True)
                up1_end(g, t0, now, rbt)
                release()

            return layer_body(16, 2, open_, up, "dn")

        now = all_now()
        pf = far(2048, 512).rearrange("p (k c) -> p k c", k=2)
        pd = PO.dma(pf, PT_IN.rearrange("(k p) c -> p k c", p=128), s_misc, 16, now)
        gf = far(4096, 1024)
        gfd = PO.dma(gf, GFIN.partition_broadcast(128), s_gf, 16, now)
        ph = rar(3072, 512).rearrange("p (k c) -> p k c", k=2)
        pl = rar(3584, 512).rearrange("p (k c) -> p k c", k=2)
        c0, c1 = mlp(J)
        a = act(ph, pf, ACT.Copy, pd)
        pt0 = vtt(pl, pf, ph.bitcast(F), ALU.subtract, a)
        J = join(c0, c1, 1.0, G("g_ple"))

        now = all_now()
        gs = far(0, 2048).rearrange("p (t d) -> p t d", t=2)
        q = 128 + 16 * (joins[0] % 4)
        joins[0] += 1
        PG = [[4, 6], [5, 7]]

        def pg(c, part, *w, i=None):
            o = [[ps[PG[t][c]][:, :]] for t in range(2)]
            return gemm_a(f"pg{c}.{part}", hh, hl, range(4 * part, 4 * part + 4), 512, o, part == 0, part == 1, *w,
                          [free[PG[t][c]] for t in range(2)] if part == 0 else None, hold=(part == 1), i=i)

        def emb(i, c, *w):
            s = i % NHL
            w = (ready[i],) + w
            for k in range(2):
                for t in range(2):
                    tk = slice(128 * t, 128 * t + 128)
                    a = 1024 * k + 512 * c
                    tok = mm3(accs[t][c], ph[:, k, tk], pl[:, k, tk], whi[:, s, a:a + 512], wlo[:, s, a:a + 512], k == 0,
                              k == 1, *w, free[ACC[t][c]], mark=(k == 1 and t == 1))
                    w = ()
            return tok

        pg(0, 0, J["n0"])
        n1, _ = J["second"]()
        pg(1, 0)
        tg = [pg(0, 1, n1)]
        ig, ie = take("pg1.1"), take("ple")
        Y = far(5120, 2048).rearrange("p (t d) -> p t d", t=2)
        rh2 = st[:, q + 12:q + 14]
        half = vts(rh2, J["r"], 0.5, None, ALU.mult, None, J["rtok"])

        def ple_gate(c, tg):
            sl = slice(512 * c, 512 * c + 512)
            sg = []
            for t in range(2):
                sg.append(act(gs[:, t, sl], ps[PG[t][c]][:, :], ACT.Tanh, tg, now, half, scale=rh2[:, t:t + 1]))
                free[PG[t][c]] = [sg[t]]
            return sg

        def ple_half(c, sg, t0):
            xt, yt = [], []
            sl = slice(512 * c, 512 * c + 512)
            for t in range(2):
                y = vstt(gs[:, t, sl], gs[:, t, sl], 1.0, ps[ACC[t][c]][:, :], ALU.add, ALU.mult, sg[t], t0)
                free[ACC[t][c]] = [y]
                xt.append(vstt(X[:, t, sl], gs[:, t, sl], 0.5, X[:, t, sl], ALU.mult, ALU.add, y, J["x"], n1))
                yt.append(vtt(Y[:, t, sl], X[:, t, sl], gf[:, sl], ALU.mult, xt[t], gfd, now))
            return xt, yt

        def ple_squares(c, xt, yt):
            out = square_half(q, c, xt)
            for t in range(2):
                sl = slice(c * 512, (c + 1) * 512)
                junk[t, c] = act(xn[:, t, sl], Y[:, t, sl], ACT.Square, yt[t], junk[t, c],
                                 accum=st[:, q + 8 + 2 * c + t:q + 8 + 2 * c + t + 1])
                out.append(junk[t, c])
            return out

        te = emb(ie, 0, pt0)
        xt0, yt0 = ple_half(0, ple_gate(0, tg), te)
        release(2)
        sg1 = ple_gate(1, pg(1, 1, i=ig))
        n0 = turn_half(0, G("n00"), yt0, Y)
        te = emb(ie, 1)
        done(ie, te, hold=True)
        sq = ple_squares(0, xt0, yt0)
        xt1, yt1 = ple_half(1, sg1, te)
        r1, r12 = st[:, q + 6:q + 8], st[:, q + 14:q + 16]
        r1t = None

        def second():
            nonlocal r1t, sq
            n1 = turn_half(1, G("n00"), yt1, Y)
            sq += ple_squares(1, xt1, yt1)
            r1t = rms_inv(r1, q, sq)
            a = vtt(st[:, q + 4:q + 6], r1, r1, ALU.mult, r1t)
            m = vtt(st[:, q + 12:q + 14], st[:, q + 8:q + 10], st[:, q + 10:q + 12], ALU.add, sq)
            m = vtt(st[:, q + 12:q + 14], st[:, q + 12:q + 14], st[:, q + 4:q + 6], ALU.mult, a, m)
            m = vts(st[:, q + 12:q + 14], st[:, q + 12:q + 14], 1.0 / D, EPS, ALU.mult, ALU.add, m)
            m = ppow(r12, st[:, q + 12:q + 14], 2, m)
            m = vtt(r12, r12, r1, ALU.mult, m)
            dg = diagonal(r12, m)
            release()
            return n1, dg

        xs = []

        def late():
            for t in range(2):
                xs.append(vts(X[:, t, :], Y[:, t, :], r1[:, t:t + 1], None, ALU.mult, None, r1t, yt0, yt1, sq))

        J = dict(n0=n0, second=second, late=late)

        def swiglu(layer, half, J):
            now = all_now()
            rbt = None
            a, b = f"fa{layer}{half}.", f"fb{layer}{half}."

            def end_a(g, ta):
                s = g % 2
                bk = 4 + 2 * s
                y = vtt(two(fr[:, s, :]), two(ps[bk][:, :]), rbc, ALU.mult, ta, rbt, now, ut.get(g - 2))
                free[bk] = [y]
                return act(fr[:, s, :], fr[:, s, :], ACT.Silu, y)

            def end_b(g, ya, tb):
                s = g % 2
                bk = 5 + 2 * s
                y = vtt(two(fu[:, s, :]), two(ps[bk][:, :]), rbc, ALU.mult, tb, rbt, now, ut.get(g - 2))
                free[bk] = [y]
                u_split(g, vtt(fu[:, s, :], fu[:, s, :], fr[:, s, :], ALU.mult, y, ya))

            def open_():
                nonlocal rbt
                ta, tb, rbt = opening((a + "0", b + "0"), (4, 5), J)
                ya = end_a(0, ta)
                release(2)
                end_b(0, ya, tb)
                release()
                return 1

            def up(g):
                bk = 4 + 2 * (g % 2)
                o = [[ps[bk + j][:, 0:256], ps[bk + j][:, 256:512]] for j in range(2)]
                ya = end_a(g, gemm_b(f"{a}{g}", hh, hl, 8, 256, o[0], free[bk], hold=True))
                release()
                end_b(g, ya, gemm_b(f"{b}{g}", hh, hl, 8, 256, o[1], free[bk + 1], hold=True))
                release()

            return layer_body(11, 1, open_, up, f"fd{layer}{half}.")

        c0, c1 = swiglu(0, 0, J)

        J = join(c0, c1, 0.5, G("n01"), xs)

        now = all_now()
        sm_ = far(0, 48).rearrange("p (t c) -> p t c", t=2)
        lf = far(48, 16).rearrange("p (t c) -> p t c", t=2)
        la, lb = far(64, 16), far(80, 16)
        Ft = far(96, 16).rearrange("p (t c) -> p t c", t=2)
        glT = fa[0:17, 128:384]
        nFT = fa[0:8, 384:640]
        gk = far(640, 512).rearrange("p (t c) -> p t c", t=2)
        gtmp = far(640, 512)
        vg = far(1152, 1024).rearrange("p (t c) -> p t c", t=2)
        go = far(2176, 1024)
        GT = far(3200, 512).rearrange("p (r c) -> p r c", r=2)
        enG = far(3712, 512).rearrange("p (r c) -> p r c", r=2)
        AT = far(3200, 1024).rearrange("p (s r t c) -> p s r t c", s=2, r=2, t=2)
        eE = far(4224, 512).rearrange("p (r c) -> p r c", r=2)
        ke = far(4736, 512).rearrange("p (r c) -> p r c", r=2)
        og = far(4224, 1024).rearrange("p (s c) -> p s c", s=2)
        kdc = far(5248, 512).rearrange("p (r c) -> p r c", r=2)
        ktk = far(5760, 512).rearrange("p (r t c) -> p r t c", r=2, t=2)
        ov = far(5248, 1024).rearrange("p (s c) -> p s c", s=2)
        eG = far(6272, 512).rearrange("p (r c) -> p r c", r=2)
        qd = far(6784, 512).rearrange("p (r c) -> p r c", r=2)
        sts = far(7296, 1536).rearrange("p (n r c) -> p n r c", n=3, r=2)
        ga, ge = far(7296, 512), far(7808, 512)
        nring = far(8832, 768).rearrange("p (s c) -> p s c", s=3)
        fsum = far(9600, 1152).rearrange("p (s c) -> p s c", s=3)
        qf = fx[:, 0:1024].rearrange("p (k c) -> p k c", k=4)
        kf = fx[:, 1024:2048].rearrange("p (k c) -> p k c", k=4)
        vf = xnf[:, 1024:2048].rearrange("p (t c) -> p t c", t=2)
        mh = rar(0, 2048).rearrange("p (k c) -> p k c", k=8)
        ml = rar(2048, 2048).rearrange("p (k c) -> p k c", k=8)
        r1c = J["r"]

        def flat(a):
            return a.rearrange("p r c -> p (r c)")

        def ptt(o, x, y, op, *w):
            return PO.add(lambda e: e.tensor_tensor(o, x, y, op), w)

        vb = [[ps[4][:, :]], [ps[5][:, :]]]
        gemm_a("vg.0", hh, hl, range(4), 512, vb, True, False, J["n0"], free[4], free[5])
        n1, dg = J["second"]()
        i = take("qf0")
        ob = [ps[6][:, 0:256], ps[6][:, 256:512]]
        b_part(i, range(4), ob, True, False, free[6])
        t0 = b_part(i, range(4, 8), ob, False, True, n1)
        done(i, t0, hold=True)
        rbt = spread(dg, 0)
        ft = [now]

        def qk_end(dst, g, b, t0, sc):
            y = vstt(dst[:, 2 * g:2 * g + 2, :], two(ps[b][:, :]), sc, rbc, ALU.mult, ALU.mult, t0, rbt, now)
            free[b] = [y]
            ft.append(y)

        qk_end(qf, 0, 6, t0, 0.125)
        release()
        t0 = gemm_a("vg.1", hh, hl, range(4, 8), 512, vb, False, True)
        vt = []
        for t in range(2):
            y = act(vg[:, t, :], ps[4 + t][:, :], ACT.Copy, t0, now, J["rtok"], scale=r1c[:, t:t + 1])
            free[4 + t] = [y]
            vt.append(y)
        i = take("small")
        sl = i % NHL
        for k in range(8):
            t0 = mm3(ps[1][:, 0:256], whi[:, sl, 40 * k:40 * k + 128], wlo[:, sl, 40 * k:40 * k + 128], hh[:, k, :],
                     hl[:, k, :], k == 0, k == 7, ready[i], free[1], mark=(k == 7))
        done(i, t0, hold=True)
        g1 = vset(fa[0:40, 128:384], 1.0, now)
        g1 = [vtt(fa[r:r + n, 128:384], ps[1][r:r + n, 0:256], rbb[r:r + n, 0, :], ALU.mult, t0, rbt, g1)
              for r, n in ((0, 16), (32, 8))]
        free[1] = [g1]
        release()

        def project(nm, dst, g, b, sc):
            t0 = gemm_b(f"{nm}{g}", hh, hl, 8, 256, [ps[b][:, 0:256], ps[b][:, 256:512]], free[b], hold=True)
            qk_end(dst, g, b, t0, sc)
            release()

        project("qf", qf, 1, 7, 0.125)
        for t in range(2):
            t0 = tp(ps[2][:, 64 * t:64 * t + 40], fa[0:40, 128 + 128 * t:256 + 128 * t], g1, free[2], mark=(t == 1))
        fl = [vtt(sm_[:, t, 0:8], ps[2][:, 64 * t + 32:64 * t + 40], fb8[:, :], ALU.add, t0, IN, now) for t in range(2)]
        free[2] = [fl]
        for t in range(2):
            t0 = mm(ps[3][:, 256 * t:256 * t + 256], glT[:, 128 * t:128 * t + 128], gw[:, :], True, True, g1, IN, free[3],
                    mark=(t == 1))
        project("kf", kf, 0, 4, 1.0)
        ls = [(gk, ps[3][:, :].rearrange("p (t c) -> p t c", t=2), ga.rearrange("p (t c) -> p t c", t=2),
               ge.rearrange("p (t c) -> p t c", t=2), t0),
              (lf, sm_[:, :, 0:8], la.rearrange("p (t c) -> p t c", t=2), lb.rearrange("p (t c) -> p t c", t=2), fl)]
        e0 = []
        for o, x, a, b, t0 in ls:
            y = act(a, x, ACT.Abs, t0, now)
            e0.append(act(b, a, ACT.Exp, y, scale=-1.0))
        e1 = [act(a, b, ACT.Ln, y, bias=C("ones")[:, 0:1]) for (_, _, a, b, _), y in zip(ls, e0)]
        project("kf", kf, 1, 5, 1.0)
        lg, lff = [vstt(o, x, 0.0, a, ALU.min, ALU.subtract, y, now) for (o, x, a, _, _), y in zip(ls, e1)]
        free[3] = [lg]

        vb = [[ps[6][:, :]], [ps[7][:, :]]]
        gemm_a("vf.0", hh, hl, range(4), 512, vb, True, False, free[6], free[7], hold=True)
        for p in range(2):
            for t in range(2):
                tc = mm(ps[2][:, 256 * p + 128 * t:256 * p + 128 * t + 128], gk[:, t, 128 * p:128 * p + 128], C("tri64"),
                        True, True, lg, free[2], mark=(p == 1 and t == 1))
        mm(ps[3][0:8, 0:256], lf[:, 0, :], cst[:, CONST["tri"][0]:CONST["tri"][0] + 256], True, False, lff, free[3])
        t0 = mm(ps[3][0:8, 128:256], lf[:, 1, :], C("tri"), False, True, mark=True)
        yf = vts(nFT, ps[3][0:8, 0:256], -1.0, None, ALU.mult, None, t0, now)
        fw = PO.dma(fscratch.ap(), nFT, s_fw, 16, [yf])
        mm(ps[1][:, 0:8], C("tri"), lf[:, 0, :], True, True, free[1])
        mm(ps[1][:, 8:16], C("ones"), lf[:, 0, :], True, False)
        t0 = mm(ps[1][:, 8:16], C("tri"), lf[:, 1, :], False, True, mark=True)
        yF = vcopy(Ft, ps[1][:, 0:16].rearrange("p (t c) -> p t c", t=2), t0, now)
        free[3], free[1] = [yf], [yF]
        ft.append(yF)
        yg = vcopy(flat(GT), ps[2][:, :], tc, now)
        free[2] = [yg]
        e1 = act(eG, GT, ACT.Exp, yg, now)
        e2 = act(enG, GT, ACT.Exp, yg, scale=-1.0)
        for p in range(2):
            for c in range(4):
                e3 = act(eE[:, p, 64 * c:64 * c + 64], GT[:, p, 64 * c:64 * c + 64], ACT.Exp, yg, scale=-1.0,
                         bias=GT[:, p, 64 * c + 63:64 * c + 64])
        cm = C("cm")
        fsapp = fscratch.ap()
        na, nu = {}, {}

        def forget_load(h):
            if h < 8:
                src = bass.AP(fsapp.tensor, 256 * h, [[0, 128], [1, 256]])
                nt[h] = PO.dma(nring[:, h % 3, :], src, s_fr[h % 3], 16 * (h // 3 + 1), [fw, na.get(h - 3), now])

        def forget_mask(h):
            if h < 8:
                k = h % 3
                ptt(fsum[:, k, 0:128], nring[:, k, 0:128], cm[:, 128:256], ALU.add, nt[h], nu.get(h - 3), now)
                na[h] = ptt(fsum[:, k, 128:384], nring[:, k, :], cm, ALU.add)

        nt = {}
        for h in range(3):
            forget_load(h)
        for h in range(3):
            forget_mask(h)
        forget_load(3)
        vft = []
        t0 = gemm_a("vf.1", hh, hl, range(4, 8), 512, vb, False, True, hold=True)
        for t in range(2):
            y = act(vf[:, t, :], ps[6 + t][:, :], ACT.Copy, t0, now, scale=r1c[:, t:t + 1])
            free[6 + t] = [y]
            vft.append(y)

        pq = vtt(qd, eG, rbc, ALU.mult, e1, rbt, now)
        pk = vtt(enG, enG, rbc, ALU.mult, e2)
        pe = vtt(eE, eE, rbc, ALU.mult, e3)

        def head_f(h):
            lo = 64 * (h % 2)

            def used(e):
                nu[h] = e
                forget_load(h + 4)
                forget_mask(h + 3)

            return dict(after=lambda: vft if h else [], q=lambda t: qf[lo:lo + 64, h // 2, 128 * t:128 * t + 128],
                        k=lambda n: kf[lo:lo + 64, h // 2, 0:n],
                        v=lambda k: vf[:, k, 64 * h:64 * h + 64],
                        row=Ft[:, :, h], add=fsum[:, h % 3, :], added=lambda: na[h], used=used)

        gm = []

        def by_steps(tag, b):
            i = take(tag)
            s = i % NHL
            for f in range(2):
                for k in range(8):
                    c = k * 256 + f * 128
                    t0 = mm3(ps[b][:, 256 * f:256 * f + 256], whi[:, s, c:c + 128], wlo[:, s, c:c + 128], hh[:, k, :],
                             hl[:, k, :], k == 0, k == 7, ready[i], free[b], mark=(f == 1 and k == 7))
                    if (f, k) != (1, 7):
                        yield
            done(i, t0, hold=True)
            return t0

        def out_gate(g, b):
            t0 = yield from by_steps(f"go{g}", b)
            gx = go[:, 512 * g:512 * g + 512]
            y = vtt(two(gx), two(ps[b][:, :]), rbc, ALU.mult, t0, now)
            free[b] = [y]
            a = act(gtmp, gx, ACT.Tanh, y, tc, gt2.get(g - 1), scale=0.5)
            gt2[g] = vstt(gx, gtmp, 1.0, gx, ALU.add, ALU.mult, a)
            yield

        gt2, lin = {}, {}

        def linear():
            t0 = yield from by_steps("qg", 0)
            yq = vstt(flat(qd), ps[0][:, :], 0.125, flat(qd), ALU.mult, ALU.mult, t0, pq)
            free[0] = [yq]
            yield
            t0 = yield from by_steps("kg", 1)
            yk = vtt(flat(kdc), ps[1][:, :], flat(enG), ALU.mult, t0, pk, now)
            ye = vtt(flat(ke), ps[1][:, :], flat(eE), ALU.mult, pe, now)
            free[1] = [ye]
            yield
            yield from out_gate(0, 2)
            ta = []
            for p in range(2):
                for t in range(2):
                    for par in range(2):
                        r0 = 64 * par
                        tk = slice(128 * t, 128 * t + 128)
                        c = 256 * p + 128 * t
                        t0 = mm(ps[par][:, c:c + 128], kdc[r0:r0 + 64, p, tk], qd[r0:r0 + 64, p, tk], True, True, yq, yk,
                                free[par], mark=True)
                    yield
            m64 = C("m64").unsqueeze(1).to_broadcast([128, 4, 128])
            ya = []
            for par in range(2):
                y = vtt(AT[:, par].rearrange("p r t c -> p (r t) c"), ps[par][:, :].rearrange("p (g c) -> p g c", g=4), m64,
                        ALU.mult, t0, ye, e1, e2, e3)
                free[par] = [y]
                ya.append(y)
            for p in range(2):
                for t in range(2):
                    c = 256 * p + 128 * t
                    t0 = tp(ps[3][:, c:c + 128], ke[:, p, 128 * t:128 * t + 128], ye, free[3], mark=(p == 1 and t == 1))
            y = act(ktk, ps[3][:, :].rearrange("p (r t c) -> p r t c", r=2, t=2), ACT.Copy, t0, now)
            free[3] = [y]
            yield
            og1 = out_gate(1, 2)
            for _ in range(8):
                next(og1)
                yield
            KB = (0, 1, 3)
            kv = []
            for c in range(3):
                t, r0 = c // 2, 64 * (c % 2)
                for p in range(2):
                    t0 = mm(ps[KB[c]][:, 256 * p:256 * p + 256], ktk[r0:r0 + 64, p, t, :],
                            vg[r0:r0 + 64, t, 256 * p:256 * p + 256], True, True, y, vt, free[KB[c]], mark=(p == 1))
                kv.append(t0)
                yield
            ys = vcopy(sts[:, 0].rearrange("p r c -> p (r c)"), ps[0][:, :], kv[0], lg)
            free[0] = [ys]
            for c in range(1, 3):
                for p in range(2):
                    ys = vstt(sts[:, c, p, :], sts[:, c - 1, p, :], eG[:, p, 64 * c + 63:64 * c + 64],
                              ps[KB[c]][:, 256 * p:256 * p + 256], ALU.mult, ALU.add, kv[c], ys, e1)
                free[KB[c]] = [ys]
            yield from og1
            lin.update(ya=ya, ys=ys)

        other2 = linear()

        def fill2(n):
            for _ in range(n + n // 2 if n < 100 else n):
                next(other2, None)

        at2 = attention([head_f(h) for h in range(8)], True, lambda j: mh[:, 4 + j, :], lambda j: ml[:, 4 + j, :], ft,
                        fill=fill2, SB=(4, 5), TB=(6,), OB=(7,))
        fill2(200)
        release()
        ys = lin["ys"]
        gov = go.rearrange("p (r s c) -> p s r c", r=2, s=2)
        mhv, mlv = (a[:, 0:4, :].rearrange("p (r s) c -> p s r c", s=2) for a in (mh, ml))
        to = []
        for par in range(2):
            b = 4 + par
            r0 = 64 * par
            for p in range(2):
                h = 2 * p + par
                for t in range(2):
                    o = ps[b][:, 256 * p + 128 * t:256 * p + 128 * t + 128]
                    mm(o, vg[:, t, 128 * h:128 * h + 128], AT[:, par, p, t, :], True, False, lin["ya"], vt, free[b])
                    for c in range(2 * t, 2 * t + 2):
                        if c >= 1:
                            t0 = mm(o[:, 64 * (c % 2):64 * (c % 2) + 64],
                                    sts[r0:r0 + 64, c - 1, p, 128 * par:128 * par + 128],
                                    qd[r0:r0 + 64, p, 64 * c:64 * c + 64], False, True, ys, mark=(p == 1 and c == 3))
            to.append(act(og[:, par, :], ps[b][:, :], ACT.Square, t0))
        tq = [mm(ps[6 + par][:, :], C("ones"), og[:, par, :], True, True, to[par], free[6 + par], mark=True)
              for par in range(2)]
        for c in range(2):
            proj_start("eo", c, 1, mh, ml, at2, hold=True)
        y = []
        for par in range(2):
            y.append(vts(ov[:, par, :], ps[6 + par][:, :], 1.0 / 128, EPS, ALU.mult, ALU.add, tq[par]))
            free[6 + par] = [y[par]]
        y = [act(ov[:, par, :], ov[:, par, :], ACT.Ln, y[par]) for par in range(2)]
        y = [act(ov[:, par, :], ov[:, par, :], ACT.Exp, y[par], scale=-0.5) for par in range(2)]
        for par in range(2):
            b = 4 + par
            a = vstt(ov[:, par, :], ps[b][:, :], G("g_gla")[:, 0:1], ov[:, par, :], ALU.mult, ALU.mult, y[par])
            free[b] = [a]
            o2 = ov[:, par, :].rearrange("p (r c) -> p r c", r=2)
            a = vstt(o2, o2, 0.5, gov[:, par], ALU.mult, ALU.mult, a, gt2[1])
            c = act(mhv[:, par], o2, ACT.Copy, a, now)
            gm.append(vtt(mlv[:, par], o2, mhv[:, par].bitcast(F), ALU.subtract, c))
        release()
        c0, c1 = proj_end("eo", 0, mh, ml, gm)
        J = join(c0, c1, 1.0, G("n02"))
        c0, c1 = swiglu(0, 1, J)
        J = join(c0, c1, 0.5, G("n10"))
        c0, c1 = swiglu(1, 0, J)
        J = join(c0, c1, 0.5, G("n11"))

        now = all_now()
        qT = far(0, 2048).rearrange("p (k c) -> p k c", k=8)
        kT = far(2048, 2048).rearrange("p (k c) -> p k c", k=8)
        vv = far(4096, 2048).rearrange("p (t c) -> p t c", t=2)
        ck = far(6144, 512).rearrange("p (t c) -> p t c", t=2)
        kw = far(6656, 256)
        kiu = far(6912, 256)
        wi = far(7168, 16).rearrange("p (t c) -> p t c", t=2)
        acc = far(7184, 384)
        wk = far(7568, 384)
        msk = far(7952, 384)
        bring = far(8336, 768).rearrange("p (s c) -> p s c", s=3)
        bsum = far(9104, 1152).rearrange("p (s c) -> p s c", s=3)
        trow = fa[0:16, 10256:10768]
        qiT = fx[:, 0:1024].rearrange("p (k c) -> p k c", k=4)
        rl = fx[:, 1024:2048].rearrange("p (s c) -> p s c", s=2)
        top = [st[:, 200 + 8 * t:208 + 8 * t] for t in range(2)]
        r1c = J["r"]
        cm = C("cm")

        def kw_part(i, ks, *w):
            sl = i % NHL
            for k in ks:
                t0 = mm3(ps[4][:, 0:256], whi[:, sl, 72 * k:72 * k + 128], wlo[:, sl, 72 * k:72 * k + 128], hh[:, k, :],
                         hl[:, k, :], k == 0, k == 7, ready[i], *w, mark=(k == ks[-1]))
            return t0

        ik, iq = take("kwi"), take("qi0")
        oq = [ps[5][:, 0:256], ps[5][:, 256:512]]
        kw_part(ik, range(4), J["n0"], free[4])
        b_part(iq, range(2), oq, True, False, free[5])
        n1, dg = J["second"]()
        b_part(iq, range(2, 4), oq, False, False)
        tk = kw_part(ik, range(4, 8), n1)
        done(ik, tk, hold=True)
        rbt = spread(dg, 0)
        t0 = b_part(iq, range(4, 8), oq, False, True)
        done(iq, t0, hold=True)
        kwt = vtt(kw[0:72, :], ps[4][0:72, 0:256], rbb[0:72, 0, :], ALU.mult, tk, rbt, now)
        free[4] = [kwt]
        kit = PO.dma(kiu[64:128, :], kw[0:64, :], s_ki, 16, [kwt, now])
        qy = [kwt, kit]

        def turned(dst, g, b, t0, to):
            y = vstt(dst[:, 2 * g:2 * g + 2, :], two(ps[b][:, :]), 0.125, rbc, ALU.mult, ALU.mult, t0, rbt, now)
            free[b] = [y]
            to.append(y)

        turned(qiT, 0, 5, t0, qy)
        release()
        t0 = gemm_b("qi1", hh, hl, 8, 256, [ps[6][:, 0:256], ps[6][:, 256:512]], free[6], hold=True)
        turned(qiT, 1, 6, t0, qy)
        release()
        for t in range(2):
            t0 = tp(ps[7][:, 128 * t:128 * t + 72], kw[0:72, 128 * t:128 * t + 128], kwt, free[7], mark=(t == 1))
        wy = act(wi, ps[7][:, 0:256].rearrange("p (t c) -> p t c", t=2)[:, :, 64:72], ACT.Copy, t0, now,
                 scale=float(np.float32(8 ** -0.5)))
        free[7] = [wy]

        OFF, KL = (0, 128), (128, 256)
        av, rt = None, {}
        ic = take("ckv")
        for h in range(8):
            b = h % 4
            lo = 64 * (h % 2)
            kk = kw if h % 2 == 0 else kiu
            for t in range(2):
                t0 = mm(ps[b][:, OFF[t]:OFF[t] + KL[t]], qiT[lo:lo + 64, h // 2, 128 * t:128 * t + 128],
                        kk[lo:lo + 64, 0:KL[t]], True, True, qy, free[b], mark=(t == 1))
            for t in range(2):
                a = slice(256 * h, 256 * h + 256)
                tc = mm3(ps[4 + t][:, 0:256], hh[:, h, 128 * t:128 * t + 128], hl[:, h, 128 * t:128 * t + 128],
                         whi[:, ic % NHL, a], wlo[:, ic % NHL, a], h == 0, h == 7, ready[ic], free[4], free[5],
                         mark=(h == 7 and t == 1))
            s = h % 2
            y = act(rl[:, s, 0:384], ps[b][:, 0:384], ACT.Relu, t0, now, rt.get(h - 2))
            free[b] = [y]
            for t in range(2):
                a = acc[:, OFF[t]:OFF[t] + KL[t]]
                r = rl[:, s, OFF[t]:OFF[t] + KL[t]]
                if h == 0:
                    av = vts(a, r, wi[:, t, h:h + 1], None, ALU.mult, None, y, wy, now)
                else:
                    av = vstt(a, r, wi[:, t, h:h + 1], a, ALU.mult, ALU.add, y, av)
            rt[h] = av

        t0 = mm(ps[7][0:16, :], t5s[:, :], C("hot", 32), True, True, IN, free[7], mark=True)
        y = act(trow, ps[7][0:16, :], ACT.Copy, t0, now)
        free[7] = [y]
        t5w = PO.dma(scratch.ap(), trow, s_t5w, 16, [y])

        done(ic, tc, hold=True)
        cy = []
        for t in range(2):
            y = act(ck[:, t, :], ps[4 + t][:, 0:256], ACT.Copy, tc, now, scale=r1c[:, t:t + 1])
            free[4 + t] = [y]
            cy.append(y)
        release()

        def rounds():
            a = [vtt(wk[:, 0:128], acc[:, 0:128], cm[:, 128:256], ALU.add, av, now),
                 vtt(wk[:, 128:384], acc[:, 128:384], cm, ALU.add)]
            for r in range(8):
                for t in range(2):
                    w_ = wk[:, OFF[t]:OFF[t] + KL[t]]
                    a[t] = VE.add(lambda e, w_=w_, t=t: e.max(top[t], w_), [a[t]])
                for t in range(2):
                    w_ = wk[:, OFF[t]:OFF[t] + KL[t]]
                    a[t] = VE.add(lambda e, w_=w_, t=t: e.match_replace(w_, top[t], w_, GONE), [a[t]])
                yield
            y = vts(msk, wk, GONE, 1.0, ALU.is_equal, ALU.subtract, a)
            y = vts(msk, msk, -NEG, None, ALU.mult, None, y)
            mk.append(vtt(msk[:, 0:128], msk[:, 0:128], cm[:, 128:256], ALU.add, y))
            mk.append(vtt(msk[:, 128:384], msk[:, 128:384], cm, ALU.add, y))
            yield

        mk = []
        topk = rounds()
        ch = rar(0, 512).rearrange("p (k c) -> p k c", k=2)
        cl = rar(512, 512).rearrange("p (k c) -> p k c", k=2)
        dt = [now]
        r = norm_stat(lambda t: ck[:, t, :], 256, lambda t: xn[:, t, 0:256], st[:, 4:6], cy, now)
        next(topk)
        yc = [vts(xn[:, t, 0:256], ck[:, t, :], st[:, 4 + t:5 + t], None, ALU.mult, None, r) for t in range(2)]
        t0 = gemm_b("q0", hh, hl, 8, 256, [ps[7][:, 0:256], ps[7][:, 256:512]], free[7], hold=True)
        next(topk)
        turned(qT, 0, 7, t0, dt)
        release(1)
        next(topk)
        release(1)
        for k in range(2):
            for t in range(2):
                tr = tp(ps[6][:, 256 * k + 128 * t:256 * k + 128 * t + 128], xn[:, t, k * 128:(k + 1) * 128], yc, free[6],
                        mark=(k == 1 and t == 1))
        hs = [act(ch[:, k, :], ps[6][:, 256 * k:256 * k + 256], ACT.Copy, tr, now, scale=G("g_ckv")[:, k:k + 1])
              for k in range(2)]
        nc_ = [vstt(cl[:, k, :], ps[6][:, 256 * k:256 * k + 256], G("g_ckv")[:, k:k + 1], ch[:, k, :].bitcast(F), ALU.mult,
                    ALU.subtract, hs, now) for k in range(2)]
        free[6] = [nc_[1]]
        t0 = gemm_b("q1", hh, hl, 8, 256, [ps[4][:, 0:256], ps[4][:, 256:512]], free[4], hold=True)
        next(topk)
        turned(qT, 1, 4, t0, dt)
        release(1)
        next(topk)
        release(1)
        i = take("uk")
        s = i % NHL
        for f in range(8):
            b = f // 2
            for k in range(2):
                a = k * 1024 + f * 128
                t0 = mm3(ps[b][:, 256 * (f % 2):256 * (f % 2) + 256], whi[:, s, a:a + 128], wlo[:, s, a:a + 128],
                         ch[:, k, :], cl[:, k, :], k == 0, k == 1, ready[i], nc_, free[b], mark=(k == 1 and f % 2 == 1))
            if f % 2:
                y = act(kT[:, f - 1:f + 1, :], two(ps[b][:, :]), ACT.Copy, t0, now)
                free[b] = [y]
                dt.append(y)
        done(i, t0, hold=True)
        next(topk)
        next(topk)
        VB = [[4, 5], [6, 7]]
        t0 = gemm_a("uv", ch, cl, range(2), 1024, [[ps[b][:, :] for b in r] for r in VB], True, True,
                    [free[b] for b in range(4, 8)], hold=True)
        for _ in topk:
            pass
        vvt = []
        for t in range(2):
            for c in range(2):
                b = VB[t][c]
                y = act(vv[:, t, 512 * c:512 * c + 512], ps[b][:, :], ACT.Copy, t0, now)
                free[b] = [y]
                vvt.append(y)

        ba, bu = {}, {}
        sapp = scratch.ap()

        def bias_load(h):
            if h < 16:
                k = h % 3
                src = bass.AP(sapp.tensor, 512 * h + 128, [[1, 128], [1, 256]])
                bt[h] = PO.dma(bring[:, k, :], src, s_bias[k], 16 * (h // 3 + 1), [t5w, ba.get(h - 3), now])

        def bias_mask(h):
            if h < 16:
                k = h % 3
                for t in range(2):
                    at0 = bring[:, k, KL[t] - 1:KL[t]]
                    back = bass.AP(at0.tensor, at0.offset, [list(at0.ap[0]), [-1, KL[t]]])
                    o, m_ = bsum[:, k, OFF[t]:OFF[t] + KL[t]], msk[:, OFF[t]:OFF[t] + KL[t]]
                    ba[h] = PO.add(lambda e, o=o, back=back, m_=m_: e.tensor_tensor(o, back, m_, ALU.add),
                                   [bt[h], mk, bu.get(h - 3), now])

        bt = {}

        def head_d(h):
            lo = 64 * (h % 2)

            def used(e):
                bu[h] = e
                bias_load(h + 4)
                bias_mask(h + 3)

            return dict(q=lambda t: qT[lo:lo + 64, h // 2, 128 * t:128 * t + 128],
                        k=lambda n: kT[lo:lo + 64, h // 2, 0:n],
                        v=lambda k: vv[:, k, 64 * h:64 * h + 64],
                        add=bsum[:, h % 3, :], added=lambda: ba[h], used=used,
                        after=lambda: [late_q[h // 4 - 2]] if h >= 8 else vvt if h else [])

        for h in range(3):
            bias_load(h)
        for h in range(3):
            bias_mask(h)
        bias_load(3)
        at3, late_q = [], []

        def beside():
            for g in (2, 3):
                t0 = yield from by_steps(f"q{g}", g - 2)
                turned(qT, g, g - 2, t0, late_q)
                yield
            while len(at3) < 4:
                yield
            yield
            yield
            for c in range(2):
                i = take(f"oo{c}.0")
                s = i % NHL
                for k in range(4):
                    for t in range(2):
                        tk = slice(128 * t, 128 * t + 128)
                        t0 = mm3(accs[t][c], mh[:, k, tk], ml[:, k, tk], whi[:, s, 512 * k:512 * k + 512],
                                 wlo[:, s, 512 * k:512 * k + 512], k == 0, False, ready[i], at3[0:4],
                                 free[ACC[0][c]], free[ACC[1][c]], mark=(k == 3 and t == 1))
                        if (k, t) != (3, 1):
                            yield
                done(i, t0, hold=True)
                yield

        other3 = beside()

        def fill3(n):
            for _ in range(n if n > 2 else 1 if n == 2 else 0 if len(at3) >= 4 else 2):
                next(other3, None)

        attention([head_d(h) for h in range(16)], True, lambda j: mh[:, j, :], lambda j: ml[:, j, :], dt,
                  fill=fill3, outs=at3, SB=(4, 5), TB=(6,), OB=(7,), first=2)
        fill3(200)
        release()
        c0, c1 = proj_end("oo", 1, mh, ml, at3)
        J = join(c0, c1, 1.0, G("n12"))
        c0, c1 = swiglu(1, 1, J)
        gfd = PO.dma(gf, GFIN2.partition_broadcast(128), s_gf, 32, all_now())
        q = 128 + 16 * (joins[0] % 4)
        rt0 = add_half(0, 0.5, c0())
        sq = square_half(q, 0, rt0)
        for f in c1:
            tok = f()
        rt1 = add_half(1, 0.5, tok)
        sq += square_half(q, 1, rt1)
        r = st[:, q + 6:q + 8]
        rt = rms_inv(r, q, sq)
        ov = OUT.rearrange("(t p) d -> p t d", p=128)
        for t in range(2):
            y = vstt(X[:, t, :], X[:, t, :], r[:, t:t + 1], gf, ALU.mult, ALU.mult, rt, gfd)
            out = SP.dma(ov[:, t, :], X[:, t, :], s_out, 16 * t + 16, [y])
        assert at[0] == len(P)

        block = ctx.enter_context(nc.Block())

        @block.sync
        def _(e):
            SP.play(e)
            e.wait_ge(*out)
            e.wait_ge(*t5w)
            e.wait_ge(*fw)

        @block.tensor
        def _(e):
            PE.play(e)

        @block.scalar
        def _(e):
            AC.play(e)

        @block.vector
        def _(e):
            VE.play(e)

        @block.gpsimd
        def _(e):
            PO.play(e)


def layout(inputs):
    a = {k: np.asarray(v) for k, v in inputs.items()}
    w = {n: a[n][0] for n in ("w_in", "w_qb", "w_kvb", "w_oa", "w_ob", "w_o", "w_up", "w_down", "w_ple_gate", "w_ple")}
    for layer in range(2):
        for half in range(2):
            w[f"ffn_in{layer}{half}"] = a["ffn_w_in_2"][layer, half]
            w[f"ffn_out{layer}{half}"] = a["ffn_w_out_2"][layer, half]
    w["even_in"], w["even_out"] = a["even_w_in_2"][0], a["even_w_out_2"][0]
    w["odd_in"], w["odd_out"] = a["odd_w_in_2"][0], a["odd_w_out_2"][0]
    w["w_ukT"] = a["mla_w_uk_2"][0].transpose(2, 0, 1).reshape(256, 1024)
    w["w_uv"] = a["mla_w_uv_2"][0].transpose(1, 0, 2).reshape(256, 1024)
    P = plan()
    W = np.zeros((len(P), 128, CW), np.float32)
    for i, (_, pieces) in enumerate(P):
        c = 0
        for name, r0, c0, n in pieces:
            W[i, :, c:c + n] = w[name][r0:r0 + 128, c0:c0 + n]
            c += n

    gains = np.zeros((128, NGAIN), np.float32)
    ng = a["norm_g_2"]
    for name, g in dict(g_mix=a["g_mix"][0], g_qa=a["g_qa"][0], g_kva=a["g_kva"][0], g_mlp=a["g_mlp"][0],
                        g_ple=a["g_ple"][0], n00=ng[0, 0], n01=ng[0, 1], n02=ng[0, 2], n10=ng[1, 0], n11=ng[1, 1],
                        n12=ng[1, 2], g_gla=a["gla_norm_g_2"][0], g_ckv=a["mla_kv_norm_g_2"][0]).items():
        o, n = GAIN[name]
        gains[:, o:o + n] = g.reshape(n, 128).T
    return {
        "w_chunks": W,
        "x_in": np.ascontiguousarray(a["x"][0]),
        "p_t": np.ascontiguousarray(a["p"][0, 0].T),
        "consts": constants(),
        "gains": gains,
        "g_qk": np.concatenate([np.tile(a["g_qn"][0], 8), np.tile(a["g_kn"][0], 2)]),
        "g_fin": np.ascontiguousarray(a["g_final"]),
        "g_fin2": np.ascontiguousarray(a["final_norm_g_2"]),
        "gla_gate": np.concatenate([a["gla_w_gate_2"][0], a["gla_b_gate_2"]], 0),
        "fox_b": np.ascontiguousarray(a["fox_b_f_2"][0]),
        "t5": np.ascontiguousarray(a["t5_table_2"]),
    }


def kernel(**inputs):
    import concourse.bacc as _bacc
    from concourse.bass_utils import run_bass_kernel_spmd as _run

    nc = _bacc.Bacc("TRN2", target_bir_lowering=False, num_devices=1)
    arrays = layout(inputs)
    args = [nc.dram_tensor(n, a.shape, mybir.dt.from_np(a.dtype), kind="ExternalInput").ap() for n, a in arrays.items()]
    args.append(nc.dram_tensor("out_dram", (S, D), F, kind="ExternalOutput").ap())
    program(nc, *args)
    r = _run(nc, [arrays], core_ids=[0])
    return r.results[0]["out_dram"].reshape(1, S, D)
```
